# Optimizing a Trainium2 kernel written in Bass

```python
import math
import numpy as np
import jax
import jax.numpy as jnp
from jax import lax

D_MODEL = 1024
BATCH = 1
SEQ = 512
DEPTH = 2

MLA_HEADS = 8
QK_NOPE_DIM = 64
QK_ROPE_DIM = 32
QK_HEAD_DIM = QK_NOPE_DIM + QK_ROPE_DIM
V_HEAD_DIM = 64
KV_LORA_RANK = 4 * V_HEAD_DIM
Q_LORA_RANK = 3 * KV_LORA_RANK
ROPE_THETA = 10000.0
ATTN_Q_BLOCK = 128

MLSTM_HEADS = 4
MLSTM_HEAD_DIM = 128
MLSTM_INNER = MLSTM_HEADS * MLSTM_HEAD_DIM
CONV_WIDTH = 4
MLSTM_CHUNK = 64

PEER_HEADS = 8
PEER_NKEYS = 128
PEER_N_EXPERTS = PEER_NKEYS * PEER_NKEYS
PEER_KEY_DIM = 128
PEER_HALF_DIM = PEER_KEY_DIM // 2
PEER_TOPK = 16
PEER_TOKEN_BLOCK = 128

RMS_EPS = 1e-6
N_ADA = 6

IN_SPLITS = (Q_LORA_RANK, KV_LORA_RANK, QK_ROPE_DIM, MLSTM_INNER, MLSTM_INNER,
             MLSTM_HEADS, MLSTM_HEADS, D_MODEL, D_MODEL)
IN_COLS = sum(IN_SPLITS)

kernel_name = "hybrid_mla_mlstm_peer_adaln"

def rms_norm(x, g):
    xf = x.astype(jnp.float32)
    y = xf * lax.rsqrt(jnp.mean(xf * xf, axis=-1, keepdims=True) + RMS_EPS)
    return (y * g.astype(jnp.float32)).astype(x.dtype)

def modulate(h, shift, scale):
    return h * (1.0 + scale[:, None, :]) + shift[:, None, :]

def rope_tables(positions):
    inv_freq = ROPE_THETA ** (-jnp.arange(0, QK_ROPE_DIM, 2, dtype=jnp.float32) / QK_ROPE_DIM)
    ang = positions.astype(jnp.float32)[..., None] * inv_freq
    return jnp.cos(ang)[:, :, None, :], jnp.sin(ang)[:, :, None, :]

def apply_rope(x, cos, sin):
    x1, x2 = jnp.split(x.astype(jnp.float32), 2, axis=-1)
    return jnp.concatenate([x1 * cos - x2 * sin, x2 * cos + x1 * sin], axis=-1).astype(x.dtype)

def block_causal_attention(q, k, v):
    B, S, H, Dq = q.shape
    Dv = v.shape[-1]
    nb = S // ATTN_Q_BLOCK
    scale = Dq ** -0.5
    qb = jnp.moveaxis(q.reshape(B, nb, ATTN_Q_BLOCK, H, Dq), 1, 0)
    kpos = jnp.arange(S)

    def one_block(args):
        q_blk, start = args
        s = jnp.einsum('bqhd,bkhd->bhqk', q_blk, k, preferred_element_type=jnp.float32) * scale
        qpos = start + jnp.arange(ATTN_Q_BLOCK)
        s = jnp.where(kpos[None, :] <= qpos[:, None], s, -jnp.inf)
        p = jax.nn.softmax(s, axis=-1).astype(v.dtype)
        return jnp.einsum('bhqk,bkhd->bqhd', p, v)

    out = lax.map(one_block, (qb, jnp.arange(nb) * ATTN_Q_BLOCK))
    return jnp.moveaxis(out, 0, 1).reshape(B, S, H * Dv)

def mla_branch(q_lat, kv_lat, k_rope, cos, sin, q_norm_g, w_q_up, kv_norm_g, w_kv_up):
    B, S, _ = q_lat.shape
    q = (rms_norm(q_lat, q_norm_g) @ w_q_up).reshape(B, S, MLA_HEADS, QK_HEAD_DIM)
    q = jnp.concatenate([q[..., :QK_NOPE_DIM], apply_rope(q[..., QK_NOPE_DIM:], cos, sin)], axis=-1)
    kv = (rms_norm(kv_lat, kv_norm_g) @ w_kv_up).reshape(B, S, MLA_HEADS, QK_NOPE_DIM + V_HEAD_DIM)
    k_nope, v = kv[..., :QK_NOPE_DIM], kv[..., QK_NOPE_DIM:]
    k_pe = apply_rope(k_rope[:, :, None, :], cos, sin)
    k = jnp.concatenate([k_nope, jnp.broadcast_to(k_pe, (B, S, MLA_HEADS, QK_ROPE_DIM))], axis=-1)
    return block_causal_attention(q, k, v)

def causal_depthwise_conv(u, w, b):
    y = lax.conv_general_dilated(u, w[:, None, :], window_strides=(1,),
                                 padding=((CONV_WIDTH - 1, 0),),
                                 dimension_numbers=('NWC', 'WIO', 'NWC'),
                                 feature_group_count=u.shape[-1])
    return y + b

def mlstm_chunkwise(q, k, v, log_i, log_f):
    B, H, S, d = q.shape
    L = MLSTM_CHUNK
    nc = S // L
    qc = q.reshape(B, H, nc, L, d)
    kc = k.reshape(B, H, nc, L, d)
    vc = v.reshape(B, H, nc, L, d)
    ic = log_i.reshape(B, H, nc, L)
    bcum = jnp.cumsum(log_f.reshape(B, H, nc, L), axis=-1)
    causal = jnp.tril(jnp.ones((L, L), dtype=bool))
    log_d = jnp.where(causal, bcum[..., :, None] - bcum[..., None, :] + ic[..., None, :], -jnp.inf)
    b_last = bcum[..., -1]
    log_a = b_last[..., None] - bcum + ic
    a_max = jnp.max(log_a, axis=-1)

    def step(carry, xs):
        C, n, m = carry
        k_j, v_j, la_j, amax_j, bl_j = xs
        m_new = jnp.maximum(bl_j + m, amax_j)
        decay = jnp.exp(bl_j + m - m_new)
        w = jnp.exp(la_j - m_new[..., None])
        vw = v_j * w[..., None]
        C_new = decay[..., None, None] * C + jnp.einsum('bhld,bhle->bhde', vw, k_j)
        n_new = decay[..., None] * n + jnp.einsum('bhl,bhle->bhe', w, k_j)
        return (C_new, n_new, m_new), (C, n, m)

    xs = (jnp.moveaxis(kc, 2, 0), jnp.moveaxis(vc, 2, 0), jnp.moveaxis(log_a, 2, 0),
          jnp.moveaxis(a_max, 2, 0), jnp.moveaxis(b_last, 2, 0))
    init = (jnp.zeros((B, H, d, d), jnp.float32), jnp.zeros((B, H, d), jnp.float32),
            jnp.zeros((B, H), jnp.float32))
    _, (C_prev, n_prev, m_prev) = lax.scan(step, init, xs)
    C_prev = jnp.moveaxis(C_prev, 0, 2)
    n_prev = jnp.moveaxis(n_prev, 0, 2)
    m_prev = jnp.moveaxis(m_prev, 0, 2)

    log_inter = bcum + m_prev[..., None]
    m_t = jnp.maximum(log_inter, jnp.max(log_d, axis=-1))
    inter_w = jnp.exp(log_inter - m_t)
    d_w = jnp.exp(log_d - m_t[..., None])
    s = jnp.einsum('bhcte,bhcse->bhcts', qc, kc) * d_w
    num = inter_w[..., None] * jnp.einsum('bhcde,bhcte->bhctd', C_prev, qc) \
        + jnp.einsum('bhcts,bhcsd->bhctd', s, vc)
    den = inter_w * jnp.einsum('bhce,bhcte->bhct', n_prev, qc) + jnp.sum(s, axis=-1)
    h = num / jnp.maximum(jnp.abs(den), jnp.exp(-m_t))[..., None]
    return h.reshape(B, H, S, d)

def mlstm_branch(u, o_pre, i_pre, f_pre, conv_w, conv_b, wq, wk, wv, b_i, b_f, norm_g, skip):
    B, S, _ = u.shape
    conv_act = jax.nn.silu(causal_depthwise_conv(u, conv_w, conv_b))
    ch = conv_act.reshape(B, S, MLSTM_HEADS, MLSTM_HEAD_DIM)
    uh = u.reshape(B, S, MLSTM_HEADS, MLSTM_HEAD_DIM)
    q = jnp.einsum('bshd,hde->bhse', ch, wq).astype(jnp.float32)
    k = jnp.einsum('bshd,hde->bhse', ch, wk).astype(jnp.float32) * (MLSTM_HEAD_DIM ** -0.5)
    v = jnp.einsum('bshd,hde->bhse', uh, wv).astype(jnp.float32)
    log_i = jnp.swapaxes((i_pre + b_i).astype(jnp.float32), 1, 2)
    log_f = jnp.swapaxes(jax.nn.log_sigmoid((f_pre + b_f).astype(jnp.float32)), 1, 2)
    h = jnp.swapaxes(mlstm_chunkwise(q, k, v, log_i, log_f), 1, 2)
    mu = jnp.mean(h, axis=-1, keepdims=True)
    var = jnp.mean(jnp.square(h - mu), axis=-1, keepdims=True)
    hn = ((h - mu) * lax.rsqrt(var + RMS_EPS)).reshape(B, S, MLSTM_INNER) * norm_g.astype(jnp.float32)
    out = jax.nn.sigmoid(o_pre.astype(jnp.float32)) * (hn + skip * conv_act)
    return out.astype(u.dtype)

def peer_ffn(h, w_q, sub_keys, u_tab, v_tab):
    B, S, D = h.shape
    T = B * S
    HK = PEER_HEADS * PEER_TOPK
    ht = h.reshape(T, D)
    q = (ht @ w_q).reshape(T, PEER_HEADS, 2, PEER_HALF_DIM)
    scores = jnp.einsum('thpd,hpnd->thpn', q, sub_keys, preferred_element_type=jnp.float32)
    s_top, i_top = lax.top_k(scores, PEER_TOPK)
    cand = (s_top[:, :, 0, :, None] + s_top[:, :, 1, None, :]).reshape(T, PEER_HEADS, PEER_TOPK * PEER_TOPK)
    cand_idx = (i_top[:, :, 0, :, None] * PEER_NKEYS + i_top[:, :, 1, None, :]).reshape(T, PEER_HEADS, PEER_TOPK * PEER_TOPK)
    best, pos = lax.top_k(cand, PEER_TOPK)
    expert_idx = jnp.take_along_axis(cand_idx, pos, axis=-1)
    gates = jax.nn.softmax(best, axis=-1)
    nb = T // PEER_TOKEN_BLOCK

    def one_block(args):
        x_b, idx_b, g_b = args
        u_sel = jnp.take(u_tab, idx_b, axis=0)
        act = jax.nn.gelu(jnp.einsum('td,ted->te', x_b, u_sel).astype(jnp.float32), approximate=False)
        w = (act * g_b).astype(x_b.dtype)
        v_sel = jnp.take(v_tab, idx_b, axis=0)
        return jnp.einsum('te,ted->td', w, v_sel)

    y = lax.map(one_block, (ht.reshape(nb, PEER_TOKEN_BLOCK, D),
                            expert_idx.reshape(nb, PEER_TOKEN_BLOCK, HK),
                            gates.reshape(nb, PEER_TOKEN_BLOCK, HK)))
    return y.reshape(B, S, D)

def setup_inputs(seed: int = 0) -> dict:
    key = jax.random.key(seed)
    ks = jax.random.split(key, 32)
    f32 = jnp.float32
    D = D_MODEL

    def nrm(k, shape, scale):
        return jax.random.normal(k, shape, f32) * scale

    x = nrm(ks[0], (BATCH, SEQ, D), 1.0)
    c = nrm(ks[1], (BATCH, D), 1.0)
    positions = jnp.broadcast_to(jnp.arange(SEQ, dtype=jnp.int32), (BATCH, SEQ))
    b_f = jnp.broadcast_to(jnp.linspace(3.0, 6.0, MLSTM_HEADS, dtype=f32), (DEPTH, MLSTM_HEADS)) \
        + nrm(ks[2], (DEPTH, MLSTM_HEADS), 0.1)
    return {
        "x": x,
        "c": c,
        "positions": positions,
        "w_ada": nrm(ks[3], (DEPTH, D, N_ADA * D), D ** -0.5),
        "b_ada": nrm(ks[4], (DEPTH, N_ADA * D), 0.02),
        "norm1_g": 1.0 + nrm(ks[5], (DEPTH, D), 0.02),
        "w_in": nrm(ks[6], (DEPTH, D, IN_COLS), D ** -0.5),
        "q_norm_g": 1.0 + nrm(ks[7], (DEPTH, Q_LORA_RANK), 0.02),
        "w_q_up": nrm(ks[8], (DEPTH, Q_LORA_RANK, MLA_HEADS * QK_HEAD_DIM), Q_LORA_RANK ** -0.5),
        "kv_norm_g": 1.0 + nrm(ks[9], (DEPTH, KV_LORA_RANK), 0.02),
        "w_kv_up": nrm(ks[10], (DEPTH, KV_LORA_RANK, MLA_HEADS * (QK_NOPE_DIM + V_HEAD_DIM)), KV_LORA_RANK ** -0.5),
        "w_branch_a": nrm(ks[11], (DEPTH, MLA_HEADS * V_HEAD_DIM, D), (MLA_HEADS * V_HEAD_DIM) ** -0.5),
        "conv_w": nrm(ks[12], (DEPTH, CONV_WIDTH, MLSTM_INNER), CONV_WIDTH ** -0.5),
        "conv_b": nrm(ks[13], (DEPTH, MLSTM_INNER), 0.02),
        "wq_m": nrm(ks[14], (DEPTH, MLSTM_HEADS, MLSTM_HEAD_DIM, MLSTM_HEAD_DIM), MLSTM_HEAD_DIM ** -0.5),
        "wk_m": nrm(ks[15], (DEPTH, MLSTM_HEADS, MLSTM_HEAD_DIM, MLSTM_HEAD_DIM), MLSTM_HEAD_DIM ** -0.5),
        "wv_m": nrm(ks[16], (DEPTH, MLSTM_HEADS, MLSTM_HEAD_DIM, MLSTM_HEAD_DIM), MLSTM_HEAD_DIM ** -0.5),
        "b_i": nrm(ks[17], (DEPTH, MLSTM_HEADS), 0.1),
        "b_f": b_f,
        "mh_norm_g": 1.0 + nrm(ks[18], (DEPTH, MLSTM_INNER), 0.02),
        "m_skip": 1.0 + nrm(ks[19], (DEPTH, MLSTM_INNER), 0.02),
        "w_branch_m": nrm(ks[20], (DEPTH, MLSTM_INNER, D), MLSTM_INNER ** -0.5),
        "w_out": nrm(ks[21], (DEPTH, D, D), D ** -0.5),
        "norm2_g": 1.0 + nrm(ks[22], (DEPTH, D), 0.02),
        "peer_wq": nrm(ks[23], (DEPTH, D, PEER_HEADS * PEER_KEY_DIM), D ** -0.5),
        "peer_keys": nrm(ks[24], (DEPTH, PEER_HEADS, 2, PEER_NKEYS, PEER_HALF_DIM), PEER_HALF_DIM ** -0.5),
        "peer_u": nrm(ks[25], (DEPTH, PEER_N_EXPERTS, D), D ** -0.5),
        "peer_v": nrm(ks[26], (DEPTH, PEER_N_EXPERTS, D), PEER_HEADS ** -0.5),
        "final_g": 1.0 + nrm(ks[27], (D,), 0.02),
    }

def reference(x, c, positions, w_ada, b_ada, norm1_g, w_in, q_norm_g, w_q_up, kv_norm_g, w_kv_up,
              w_branch_a, conv_w, conv_b, wq_m, wk_m, wv_m, b_i, b_f, mh_norm_g, m_skip,
              w_branch_m, w_out, norm2_g, peer_wq, peer_keys, peer_u, peer_v, final_g):
    cos, sin = rope_tables(positions)
    c_act = jax.nn.silu(c)
    split_points = np.cumsum(IN_SPLITS)[:-1].tolist()
    for l in range(DEPTH):
        ada = c_act @ w_ada[l] + b_ada[l]
        shift1, scale1, gate1, shift2, scale2, gate2 = jnp.split(ada, N_ADA, axis=-1)

        h = modulate(rms_norm(x, norm1_g[l]), shift1, scale1)
        proj = h @ w_in[l]
        q_lat, kv_lat, k_rope, u_m, o_pre, i_pre, f_pre, ga_pre, gm_pre = jnp.split(proj, split_points, axis=-1)
        y_a = mla_branch(q_lat, kv_lat, k_rope, cos, sin, q_norm_g[l], w_q_up[l],
                         kv_norm_g[l], w_kv_up[l]) @ w_branch_a[l]
        y_m = mlstm_branch(u_m, o_pre, i_pre, f_pre, conv_w[l], conv_b[l], wq_m[l], wk_m[l], wv_m[l],
                           b_i[l], b_f[l], mh_norm_g[l], m_skip[l]) @ w_branch_m[l]
        merged = jax.nn.sigmoid(ga_pre) * y_a + jax.nn.sigmoid(gm_pre) * y_m
        x = x + gate1[:, None, :] * (merged @ w_out[l])

        h2 = modulate(rms_norm(x, norm2_g[l]), shift2, scale2)
        x = x + gate2[:, None, :] * peer_ffn(h2, peer_wq[l], peer_keys[l], peer_u[l], peer_v[l])
    return rms_norm(x, final_g)


_drawn_inputs = setup_inputs


def setup_inputs(seed=0):
    import zlib

    import numpy as np

    out = dict(_drawn_inputs(seed))
    spreads = {}
    factors = {'q_norm_g': 6.422,
     'kv_norm_g': 3.638,
     'b_i': 8.0,
     'mh_norm_g': 3.68,
     'm_skip': 4.046,
     'final_g': 3.123}
    for name, (base, spread) in spreads.items():
        noise = np.random.default_rng([zlib.crc32(name.encode()), seed]).standard_normal(out[name].shape)
        drawn = base * np.exp(spread * noise) if base else spread * noise
        out[name] = jnp.asarray(drawn.astype(out[name].dtype))
    for name, factor in factors.items():
        out[name] = (out[name] * factor).astype(out[name].dtype)
    return out
```

```python
from contextlib import ExitStack

import numpy as np

import concourse.bass as bass
from concourse import mybir

F32 = mybir.dt.float32
U32 = mybir.dt.uint32
I32 = mybir.dt.int32
ALU = mybir.AluOpType
ACT = mybir.ActivationFunctionType
AX = mybir.AxisListType

P = 128
D = 1024
SEQ = 512
DEPTH = 2
TILES = SEQ // P
KT = D // P
HEADS = 8
NOPE, ROPE, VDIM = 64, 32, 64
QK = NOPE + ROPE
Q_LORA, KV_LORA = 768, 256
QT, KVT = Q_LORA // P, KV_LORA // P
THETA = 10000.0
MH, MD = 4, 128
MI = MH * MD
CONV = 4
PH, NKEYS, HALF, TOPK = 8, 128, 64, 16
EXPERTS = NKEYS * NKEYS
EPS = 1e-6
NEG = -1e30
FLOOR = -3.0e38
SM_SCALE = QK ** -0.5
K_SCALE = MD ** -0.5

IT_KV, IT_Q, IT_KPE = 0, KVT, KVT + QT
IT_KUP, IT_VUP, IT_QUP = IT_KPE + 1, IT_KPE + 2, IT_KPE + 3
IT_IF = IT_QUP + HEADS
IT_U, IT_O = IT_IF + 1, IT_IF + 1 + MH
IT_MQK = IT_O + MH
IT_MV = IT_MQK + 1
IT_MERGE = IT_MV + 1
IT_OUT = IT_MERGE + 3 * KT
IT_PQ = IT_OUT + KT
IT_KEYS = IT_PQ + PH
N_ITEMS = IT_KEYS + 2
W_SLOTS = 6
assert N_ITEMS % W_SLOTS == 0

ADA = 6 * D
ADA_W = 256
ADA_STEPS = ADA // ADA_W
ADA_SLOTS = 3
ADA_FIRST = 2 * D // ADA_W
SEC = D // ADA_W

C_QG, C_KVG = 0, QT
C_CW = C_KVG + KVT
C_CB = C_CW + MH * CONV
C_MG, C_SK = C_CB + MH, C_CB + 2 * MH
C_BI, C_BF = C_CB + 3 * MH, C_CB + 3 * MH + 1
N_COLS = C_BF + 1

K_ID, K_MQ, K_MT, K_SEL = 0, P, 2 * P, 3 * P
K_IOTA = K_SEL + MH * P
K_FREQ, K_SIGN, K_HPI = K_IOTA + TOPK, K_IOTA + TOPK + 1, K_IOTA + TOPK + 2
N_CONST = K_HPI + 1

B_KPE = KVT + QT
B_K, B_V = B_KPE + 1, B_KPE + 1 + HEADS
B_Q = B_V + TILES
B_N = B_Q + HEADS
D_V = 1 + 2 * MH
D_QK = D_V + TILES

UNITS = TILES * PH
RING = 8
GROUP = 2
ROUTE_PARTS = TOPK // GROUP
assert ROUTE_PARTS == 8
ROW = 2 * D
TWO_PI = 6.283185307179586
PI_LO = 3.1415925
ROUND = 12582912.0
TP_HI = 6.28125
TP_LO = TWO_PI - TP_HI


def build_trunk(nc, x_in, ct_in, pos_in, wada_in, bada_in, ng_in, w_in, cols_in, const_in, fg_in,
                experts_in, out):
    with ExitStack() as ctx:
        def sb(name, shape, dt=F32):
            return ctx.enter_context(nc.sbuf_tensor(name, shape, dt))

        def sem(name):
            return ctx.enter_context(nc.semaphore(name))

        x = sb("x", [P, TILES, D])
        ada = sb("ada", [P, ADA])
        const = sb("const", [P, N_CONST])
        ones = sb("ones", [P, P])
        zeros = sb("zeros", [P, SEQ])
        cols = sb("cols", [P, N_COLS])
        rope = sb("rope", [P, SEQ])
        cact = sb("cact", [P, KT])
        layer_row = sb("layer_row", [P, 1])
        small = sb("small", [P, 32])
        h_tok = sb("h_tok", [P, TILES, D])
        hT = sb("hT", [P, KT, SEQ])
        w_ring = sb("w_ring", [P, W_SLOTS, D])
        ARENA = 100 * 256
        arena = sb("arena", [P, ARENA])
        hT_flat = hT[:, :, :].rearrange("p k t -> p (k t)")
        h_flat = h_tok[:, :, :].rearrange("p t d -> p (t d)")

        def at(kib, n, area=None):
            a = arena if area is None else area
            o = int(kib * 256)
            return a[:, o:o + n]

        ident = const[:, K_ID:K_ID + P]
        mask_q = const[:, K_MQ:K_MQ + P]
        mask_t = const[:, K_MT:K_MT + P]
        sel = const[:, K_SEL:K_SEL + MH * P].rearrange("p (h m) -> p h m", h=MH)
        iota = const[:, K_IOTA:K_IOTA + TOPK]

        lat = at(0, 8 * SEQ).rearrange("p (j t) -> p j t", j=8)
        sq = at(16, 2 * SEQ).rearrange("p (b t) -> p b t", b=2)
        qh = at(20, HEADS * SEQ).rearrange("p (h t) -> p h t", h=HEADS)
        kh = at(36, HEADS * SEQ).rearrange("p (h t) -> p h t", h=HEADS)
        v = at(52, TILES * SEQ).rearrange("p (t e) -> p t e", t=TILES)
        kpe = at(60, SEQ)
        rtmp = at(62, SEQ)
        rms = at(64, SEQ)
        ng1 = at(66, D)
        wada = at(70, ADA_SLOTS * KT * ADA_W).rearrange("p (s k n) -> p s k n", s=ADA_SLOTS, k=KT)
        acc = at(94, 2 * ADA_W).rearrange("p (b n) -> p b n", b=2)
        ng2 = at(96, D)
        junk = at(0, D)
        prob = at(0, 3 * SEQ).rearrange("p (b t) -> p b t", b=3)
        probT = at(6, 2 * SEQ).rearrange("p (b t) -> p b t", b=2)
        scol = at(10, 5 * 32).rearrange("p (r i) -> p r i", r=5)
        att = at(62, TILES * SEQ).rearrange("p (t e) -> p t e", t=TILES)
        attT = at(92, 4 * SEQ).rearrange("p (k t) -> p k t", k=4)
        PAD = CONV - 1
        UP = SEQ + PAD
        up = at(0, MH * UP).rearrange("p (h t) -> p h t", h=MH)
        ca = at(9, MH * SEQ).rearrange("p (h t) -> p h t", h=MH)
        so = at(17, MH * SEQ).rearrange("p (h t) -> p h t", h=MH)
        VW = MD + 1
        v1 = at(25, TILES * MH * VW).rearrange("p (t h e) -> p t h e", t=TILES, h=MH)
        mq = at(34, 2 * SEQ).rearrange("p (b t) -> p b t", b=2)
        mk = at(38, 2 * SEQ).rearrange("p (b t) -> p b t", b=2)
        rows = at(42, 10 * SEQ).rearrange("p (r t) -> p r t", r=10)
        R_I, R_F, R_T, R_LN, R_CUM, R_A, R_M, R_NM, R_S, R_E = range(10)
        nmb = at(62, 2 * SEQ).rearrange("p (b t) -> p b t", b=2)
        nmd = at(66, 2 * SEQ).rearrange("p (b t) -> p b t", b=2)
        dw = at(70, 2 * SEQ).rearrange("p (b t) -> p b t", b=2)
        P_OFF = [0, 512, 896, 1152]
        pm = at(74, 2 * 1280).rearrange("p (b t) -> p b t", b=2)
        hn = at(84, 2 * MI).rearrange("p (b e) -> p b e", b=2)
        ae = at(88, 32).rearrange("p (r t h) -> p r t h", r=2, t=TILES)
        mcol = at(88.25, 64)
        ctmp = at(89, SEQ)
        ymT = at(0, MH * SEQ, h_flat).rearrange("p (h t) -> p h t", h=MH)
        mgT = at(0, KT * SEQ).rearrange("p (k t) -> p k t", k=KT)
        sg = at(16, 4 * SEQ).rearrange("p (b g t) -> p b g t", b=2, g=2)
        mt = at(24, 4 * SEQ).rearrange("p (b g t) -> p b g t", b=2, g=2)
        qp = at(0, PH * SEQ).rearrange("p (h t) -> p h t", h=PH)
        scores = at(68, UNITS * 2 * NKEYS)
        ring = at(0, RING * ROW).rearrange("p (r d) -> p r d", r=RING)
        ytmp = at(64, D)
        h_now = at(0, D, hT_flat)
        diag = at(4, 8 * P, hT_flat).rearrange("p (r m) -> p r m", r=8)
        stage = at(8, 2 * 2 * NKEYS, hT_flat).rearrange("p (b q n) -> p b q n", b=2, q=2)
        rest = at(10, NKEYS, hT_flat)
        cand = at(10.5, 2 * TOPK * TOPK, hT_flat).rearrange("p (b n) -> p b n", b=2)
        hot = at(12.5, 2 * TOPK * TOPK, hT_flat)
        rcol = at(14.5, 20 * TOPK, hT_flat)
        top = rcol[:, 0:2 * TOPK].rearrange("p (q n) -> p q n", q=2)
        top_i = rcol[:, 2 * TOPK:4 * TOPK].bitcast(U32).rearrange("p (q n) -> p q n", q=2)
        top_f = rcol[:, 4 * TOPK:6 * TOPK].rearrange("p (q n) -> p q n", q=2)
        best = rcol[:, 6 * TOPK:7 * TOPK]
        pos = rcol[:, 7 * TOPK:8 * TOPK].bitcast(U32)
        posab = rcol[:, 8 * TOPK:10 * TOPK].bitcast(U32).rearrange("p (q n) -> p q n", q=2)
        posab_f = rcol[:, 10 * TOPK:12 * TOPK].rearrange("p (q n) -> p q n", q=2)
        pick = rcol[:, 12 * TOPK:14 * TOPK]
        flat_i = rcol[:, 14 * TOPK:15 * TOPK]
        gexp = rcol[:, 15 * TOPK:16 * TOPK]
        gate = rcol[:, 16 * TOPK:18 * TOPK].rearrange("p (b n) -> p b n", b=2)
        dots = sb("dots", [P, 2, TOPK])
        gel = sb("gel", [P, 2, TOPK])
        idx = sb("idx", [P, 2, TOPK], U32)
        gs = sb("gs", [P, 4])
        ang = at(0, SEQ)
        turns = at(2, SEQ)
        pos_i = at(4, SEQ).bitcast(I32)

        bank = [ctx.enter_context(nc.psum_tensor(f"bank{i}", [P, 512], F32)) for i in range(8)]

        gathered = [sem(f"gathered{r}") for r in range(RING)]
        once_dma, once_act, once_dve, stored = sem("once_dma"), sem("once_act"), sem("once_dve"), sem("stored")
        names = ("out_used ada_acc ada_sum ada_ev par_dma ss_ready ms_ready sd_ready h_ready tp_ready tp_ev "
                 "mm_ready act_ev dve_ev sq_ready ss_mm rt_ready sqrt_ready latn "
                 "sc_ready nm_ready p_ready pt_ready pt_ev o_ready o_ev at_ready at_ev "
                 "d_ready d_ev pads lnf rows_a rows_s rows_e ae_ready ae_ev conv_ready ca_ready "
                 "nmb_ready nmb_ev nmd_ready dw_ready s_ready pm_ready n_ready n_ev var_ready dev_ready "
                 "hn_ready hnT_ready y_ev e_ready e_act e_dve wo_ready x_ready "
                 "q_ready q_ev s2_ready s2_act s2_dve "
                 "passed stage_ready best_ready exp_ready idx_ready dots_ready gelu_ready diag_ready "
                 "slot_free h_now_ready y_done y_free").split()
        w_loaded = [sem(f"w_loaded{i}") for i in range(W_SLOTS)]
        ada_loaded = [sem(f"ada_loaded{i}") for i in range(ADA_SLOTS)]
        S = {n: sem(n) for n in names}
        layer_sems = w_loaded + ada_loaded + list(S.values())

        def w_here(pe, item):
            pe.wait_ge(w_loaded[item % W_SLOTS], 16 * (item // W_SLOTS + 1))
            return w_ring[:, item % W_SLOTS, :]

        def item_used(sp, i):
            if i < IT_KUP:
                sp.wait_ge(S["mm_ready"], i + 1)
            elif i == IT_KUP:
                sp.wait_ge(S["mm_ready"], B_V)
            elif i < IT_IF:
                sp.wait_ge(S["mm_ready"], B_Q + i - IT_VUP)
            elif i < IT_MQK:
                sp.wait_ge(S["d_ready"], i - IT_IF + 1)
            elif i < IT_MERGE:
                sp.wait_ge(S["d_ready"], D_QK + 2 * MH)
            elif i < IT_OUT:
                sp.wait_ge(S["e_ready"], i - IT_MERGE + 1)
            elif i < IT_PQ - 1:
                sp.wait_ge(S["out_used"], i - IT_OUT + 1)
            elif i == IT_PQ - 1:
                sp.wait_ge(S["wo_ready"], 2 * TILES)
            else:
                sp.wait_ge(S["q_ready"], i - IT_PQ + 1)

        def load_weights(sp, l, first, last):
            for i in range(first, min(last, N_ITEMS)):
                if i >= W_SLOTS:
                    item_used(sp, i - W_SLOTS)
                sp.dma_start(w_ring[:, i % W_SLOTS, :],
                             w_in[bass.ds(l, 1), i].rearrange("a p n -> (a p) n")
                             ).then_inc(w_loaded[i % W_SLOTS], 16)

        def load_ada(sp, l, k):
            if k >= ADA_SLOTS:
                sp.wait_ge(S["ada_acc"], k - ADA_SLOTS + 1)
            sp.dma_start(wada[:, k % ADA_SLOTS, :, :].rearrange("p k n -> p (k n)"),
                         wada_in[bass.ds(l, 1), k].rearrange("a p n -> (a p) n")
                         ).then_inc(ada_loaded[k % ADA_SLOTS], 16)

        def ada_sum_dve(ve, k):
            ve.wait_ge(ada_loaded[k % ADA_SLOTS], 16 * (k // ADA_SLOTS + 1))
            if k >= 2:
                ve.wait_ge(S["ada_sum"], k - 1)
            a, w = acc[:, k % 2, :], wada[:, k % ADA_SLOTS]
            ins = nc.vector.tensor_scalar(a, w[:, 0, :], cact[:, 0:1], None, ALU.mult)
            for j in range(1, KT):
                ve.drain()
                ins = nc.vector.scalar_tensor_tensor(out=a, in0=w[:, j, :], scalar=cact[:, j:j + 1], in1=a,
                                                     op0=ALU.mult, op1=ALU.add)
            ins.then_inc(S["ada_acc"], 1)

        def ada_bias_dve(ve, k):
            ve.wait_ge(S["ada_sum"], k + 1)
            if k == 0:
                ve.wait_ge(S["par_dma"], 16 * 4)
            a = ada[:, k * ADA_W:(k + 1) * ADA_W]
            nc.vector.tensor_tensor(a, a, bank[5 + k % 2][:, 0:ADA_W], ALU.add).then_inc(S["ada_ev"], 1)
            if k // SEC in (1, 4):
                g = (ng1 if k // SEC == 1 else ng2)[:, (k % SEC) * ADA_W:(k % SEC + 1) * ADA_W]
                ve.drain()
                nc.vector.scalar_tensor_tensor(out=a, in0=a, scalar=1.0, in1=g, op0=ALU.add, op1=ALU.mult)

        def ada_pe(pe, k):
            pe.wait_ge(S["ada_acc"], k + 1)
            if k >= 2:
                pe.wait_ge(S["ada_ev"], k - 1)
            nc.tensor.matmul(bank[5 + k % 2][:, 0:ADA_W], ones[:, :], acc[:, k % 2, :], start=True,
                             stop=True).then_inc(S["ada_sum"], 1)

        def norm_act_sums(ac, n, scratch):
            for t in range(TILES):
                ac.drain()
                ins = nc.scalar.activation(scratch, x[:, t, :], ACT.Square, accum_out=small[:, t:t + 1])
            ac.drain().then_inc(S["ss_ready"], 1)
            ac.wait_ge(S["ms_ready"], n + 1)
            nc.scalar.activation(small[:, 8:12], small[:, 4:8], ACT.Sqrt).then_inc(S["sd_ready"], 1)

        def norm_dve(ve, n, shift, gain):
            ve.wait_ge(S["ss_ready"], n + 1)
            nc.vector.tensor_scalar(small[:, 4:8], small[:, 0:4], 1.0 / D, EPS, ALU.mult,
                                    ALU.add).then_inc(S["ms_ready"], 1)
            ve.wait_ge(S["sd_ready"], n + 1)
            nc.vector.reciprocal(small[:, 12:16], small[:, 8:12])
            ve.drain()
            for t in range(TILES):
                nc.vector.scalar_tensor_tensor(out=h_tok[:, t, :], in0=x[:, t, :], scalar=small[:, 12 + t:13 + t],
                                               in1=gain, op0=ALU.mult, op1=ALU.mult)
                ve.drain()
                nc.vector.tensor_tensor(h_tok[:, t, :], h_tok[:, t, :], shift, ALU.add).then_inc(S["h_ready"], 1)

        def norm_pe(pe, n):
            for t in range(TILES):
                pe.wait_ge(S["h_ready"], n * TILES + t + 1)
                for g in range(2):
                    i = 2 * t + g
                    if i >= 4:
                        pe.wait_ge(S["tp_ev"], n * 2 * TILES + i - 3)
                    for j in range(4):
                        ins = nc.tensor.transpose(bank[i % 4][:, j * P:(j + 1) * P],
                                                  h_tok[:, t, (4 * g + j) * P:(4 * g + j + 1) * P], ident)
                    ins.then_inc(S["tp_ready"], 1)

        def norm_act_copies(ac, n):
            for t in range(TILES):
                for g in range(2):
                    i = 2 * t + g
                    ac.wait_ge(S["tp_ready"], n * 2 * TILES + i + 1)
                    nc.scalar.copy(hT[:, 4 * g:4 * g + 4, t * P:(t + 1) * P],
                                   bank[i % 4][:, :].rearrange("p (j t) -> p j t", j=4)).then_inc(S["tp_ev"], 1)

        with nc.Block() as block:
            @block.sync
            def _(sp):
                sp.dma_start(x[:, :, :], x_in.rearrange("(t p) d -> p t d", p=P)).then_inc(once_dma, 16)
                sp.dma_start(const[:, :], const_in).then_inc(once_dma, 16)
                sp.dma_start(cact[:, :], ct_in).then_inc(once_dma, 16)
                sp.dma_start(pos_i, pos_in.to_broadcast([P, SEQ])).then_inc(once_dma, 16)

            @block.vector
            def _(ve):
                nc.vector.memset(ones[:, :], 1.0)
                nc.vector.memset(zeros[:, :], 0.0)
                nc.vector.memset(layer_row[:, :], 0.0)
                ve.wait_ge(once_dma, 64)
                nc.vector.tensor_copy(ang, pos_i)
                ve.drain()
                nc.vector.tensor_scalar(ang, ang, const[:, K_FREQ:K_FREQ + 1], None, ALU.mult)
                ve.drain()
                nc.vector.tensor_scalar(turns, ang, 1.0 / TWO_PI, ROUND, ALU.mult, ALU.add)
                ve.drain()
                nc.vector.tensor_scalar(turns, turns, ROUND, None, ALU.subtract)
                ve.drain()
                for part in (TP_HI, TP_LO):
                    nc.vector.scalar_tensor_tensor(out=ang, in0=turns, scalar=-part, in1=ang, op0=ALU.mult,
                                                   op1=ALU.add)
                    ve.drain()
                nc.vector.tensor_scalar(ang, ang, PI_LO, -PI_LO, ALU.min, ALU.max).then_inc(once_dve, 1)

            @block.scalar
            def _(ac):
                ac.wait_ge(once_dma, 64)
                nc.scalar.activation(cact[:, :], cact[:, :], ACT.Silu)
                ac.wait_ge(once_dve, 1)
                nc.scalar.activation(turns[64:96, :], ang[64:96, :], ACT.Abs)
                ac.drain()
                nc.scalar.activation(rope[64:96, :], turns[64:96, :], ACT.Sin, scale=-1.0,
                                     bias=const[64:96, K_HPI:K_HPI + 1])
                nc.scalar.activation(rope[96:128, :], ang[96:128, :], ACT.Sin,
                                     scale=const[96:128, K_SIGN:K_SIGN + 1]).then_inc(once_act, 1)

        with nc.Fori(0, DEPTH) as l:
            with nc.Block() as block:
                @block.sync
                def _(sp):
                    sp.dma_start(ada[:, :], bada_in[bass.ds(l, 1), :].to_broadcast([P, ADA])
                                 ).then_inc(S["par_dma"], 16)
                    for k in range(2):
                        load_ada(sp, l, k)
                    sp.dma_start(cols[:, :], cols_in[bass.ds(l, 1)].rearrange("a p n -> (a p) n")
                                 ).then_inc(S["par_dma"], 16)
                    for n, g in enumerate((ng1, ng2)):
                        sp.dma_start(g, ng_in[bass.ds(l, 1), n:n + 1, :].rearrange("a b n -> (a b) n")
                                     .to_broadcast([P, D])).then_inc(S["par_dma"], 16)
                    for k in range(2, ADA_FIRST):
                        load_ada(sp, l, k)
                    load_weights(sp, l, 0, W_SLOTS)

                @block.vector
                def _(ve):
                    for k in range(ADA_FIRST):
                        ada_sum_dve(ve, k)
                        if k:
                            ada_bias_dve(ve, k - 1)
                    ada_bias_dve(ve, ADA_FIRST - 1)
                    ve.drain()
                    norm_dve(ve, 0, ada[:, 0:D], ada[:, D:2 * D])

                @block.tensor
                def _(pe):
                    for k in range(ADA_FIRST):
                        ada_pe(pe, k)
                    norm_pe(pe, 0)

                @block.scalar
                def _(ac):
                    norm_act_sums(ac, 0, junk)
                    norm_act_copies(ac, 0)

            act_tiles = [b for b in range(B_N) if b != B_KPE]
            dve_tiles = [b for b in range(B_N) if b == B_KPE or b >= B_Q]

            def bank_free(pe, b):
                if b in act_tiles:
                    pe.wait_ge(S["act_ev"], act_tiles.index(b) + 1)
                if b in dve_tiles:
                    pe.wait_ge(S["dve_ev"], dve_tiles.index(b) + 1)

            with nc.Block() as block:
                @block.sync
                def _(sp):
                    for k in range(ADA_FIRST, ADA_FIRST + 3):
                        load_ada(sp, l, k)
                    for b in range(IT_KUP):
                        load_weights(sp, l, W_SLOTS + b, W_SLOTS + b + 1)
                        load_ada(sp, l, ADA_FIRST + 3 + b)
                    for k in range(ADA_FIRST + 3 + IT_KUP, ADA_STEPS):
                        load_ada(sp, l, k)
                    load_weights(sp, l, W_SLOTS + IT_KUP, IT_IF + W_SLOTS)

                @block.tensor
                def _(pe):
                    def square_sum(b):
                        pe.wait_ge(S["sq_ready"], b + 1)
                        nc.tensor.matmul(bank[3 if b < KVT else 4][:, :], ones[:, :], sq[:, b % 2, :],
                                         start=b in (0, KVT), stop=b in (KVT - 1, B_KPE - 1)
                                         ).then_inc(S["ss_mm"], 1)

                    for b in range(B_N):
                        if b >= 3:
                            bank_free(pe, b - 3)
                        o = bank[b % 3]
                        if b <= B_KPE:
                            w = w_here(pe, b)
                            for k in range(KT):
                                ins = nc.tensor.matmul(o[:, :], w[:, k * P:(k + 1) * P], hT[:, k, :],
                                                       start=k == 0, stop=k == KT - 1)
                            ins.then_inc(S["mm_ready"], 1)
                        elif b < B_V:
                            if b == B_K:
                                w = w_here(pe, IT_KUP)
                                pe.wait_ge(S["latn"], 1)
                            h = b - B_K
                            for j in range(KVT):
                                ins = nc.tensor.matmul(o[0:NOPE, :], w[:, j * 512 + h * NOPE:j * 512 + (h + 1) * NOPE],
                                                       lat[:, j, :], start=j == 0, stop=j == KVT - 1)
                            ins.then_inc(S["mm_ready"], 1)
                        elif b < B_Q:
                            if b == B_V:
                                w = w_here(pe, IT_VUP)
                            t = b - B_V
                            for j in range(KVT):
                                ins = nc.tensor.matmul(o[:, :], lat[:, j, t * P:(t + 1) * P],
                                                       w[:, j * 512:(j + 1) * 512], start=j == 0, stop=j == KVT - 1)
                            ins.then_inc(S["mm_ready"], 1)
                        else:
                            w = w_here(pe, IT_QUP + b - B_Q)
                            if b == B_Q:
                                pe.wait_ge(S["latn"], 2)
                            for j in range(QT):
                                ins = nc.tensor.matmul(o[:, :], w[:, j * P:(j + 1) * P], lat[:, KVT + j, :],
                                                       start=j == 0, stop=j == QT - 1)
                            ins.then_inc(S["mm_ready"], 1)
                        if 1 <= b <= B_KPE:
                            square_sum(b - 1)
                        if ADA_FIRST + b < ADA_STEPS:
                            ada_pe(pe, ADA_FIRST + b)

                @block.scalar
                def _(ac):
                    def sqrt(n):
                        ac.wait_ge(S["rt_ready"], n)
                        nc.scalar.activation(rms, rms, ACT.Sqrt).then_inc(S["sqrt_ready"], 1)

                    for b in act_tiles:
                        ac.wait_ge(S["mm_ready"], b + 1)
                        o = bank[b % 3]
                        if b < B_KPE:
                            nc.scalar.copy(lat[:, b, :], o[:, :]).then_inc(S["act_ev"], 1)
                            ac.drain()
                            if b >= 2:
                                ac.wait_ge(S["ss_mm"], b - 1)
                            nc.scalar.activation(sq[:, b % 2, :], lat[:, b, :], ACT.Square).then_inc(S["sq_ready"], 1)
                            if b == KVT:
                                sqrt(1)
                            if b == B_KPE - 1:
                                sqrt(2)
                        elif b < B_V:
                            nc.scalar.copy(kh[0:NOPE, b - B_K, :], o[0:NOPE, :]).then_inc(S["act_ev"], 1)
                        elif b < B_Q:
                            nc.scalar.copy(v[:, b - B_V, :], o[:, :]).then_inc(S["act_ev"], 1)
                        else:
                            nc.scalar.copy(qh[0:NOPE, b - B_Q, :], o[0:NOPE, :]).then_inc(S["act_ev"], 1)

                @block.vector
                def _(ve):
                    def ada_step(k):
                        if k < ADA_STEPS:
                            ada_sum_dve(ve, k)
                        if k > ADA_FIRST:
                            ada_bias_dve(ve, k - 1)

                    def mean_square(n, width):
                        ve.wait_ge(S["ss_mm"], KVT if n == 0 else B_KPE)
                        nc.vector.tensor_scalar(rms, bank[3 + n][:, :], 1.0 / width, EPS, ALU.mult,
                                                ALU.add).then_inc(S["rt_ready"], 1)

                    def scale_latents(n, first, count, gain):
                        ve.wait_ge(S["sqrt_ready"], n + 1)
                        nc.vector.reciprocal(rms, rms)
                        ve.drain()
                        for j in range(count):
                            nc.vector.scalar_tensor_tensor(out=lat[:, first + j, :], in0=lat[:, first + j, :],
                                                           scalar=cols[:, gain + j:gain + j + 1], in1=rms,
                                                           op0=ALU.mult, op1=ALU.mult)
                        ve.drain().then_inc(S["latn"], 1)

                    def rotate(o, dst):
                        nc.vector.tensor_tensor(rtmp[64:96, :], o[96:128, :], rope[96:128, :], ALU.mult)
                        nc.vector.tensor_tensor(dst, o[64:96, :], rope[64:96, :], ALU.mult)
                        ve.drain().then_inc(S["dve_ev"], 1)
                        nc.vector.tensor_tensor(dst, dst, rtmp[64:96, :], ALU.add)
                        ve.drain()

                    for b in range(ADA_STEPS - ADA_FIRST + 1):
                        ada_step(ADA_FIRST + b)
                        if b == 2:
                            mean_square(0, KV_LORA)
                        if b == 3:
                            scale_latents(0, 0, KVT, C_KVG)
                        if b == B_KPE:
                            ve.wait_ge(S["mm_ready"], B_KPE + 1)
                            rotate(bank[B_KPE % 3], kpe[64:96, :])
                            ve.sem_inc(S["pads"], 1)
                            mean_square(1, Q_LORA)
                        if b == B_KPE + 1:
                            scale_latents(1, KVT, QT, C_QG)
                    for h in range(HEADS):
                        ve.wait_ge(S["mm_ready"], B_Q + h + 1)
                        rotate(bank[(B_Q + h) % 3], qh[64:96, h, :])

                @block.gpsimd
                def _(po):
                    po.wait_ge(S["pads"], 1)
                    for h in range(HEADS):
                        nc.gpsimd.tensor_copy(kh[64:96, h, :], kpe[64:96, :])

            ITEMS = HEADS * TILES
            with nc.Block() as block:
                @block.tensor
                def _(pe):
                    def score(i):
                        h, t = divmod(i, TILES)
                        n = (t + 1) * P
                        if i >= 2:
                            pe.wait_ge(S["p_ready"], i - 1)
                        nc.tensor.matmul(bank[i % 2][:, 0:n], qh[0:QK, h, t * P:(t + 1) * P], kh[0:QK, h, 0:n],
                                         start=True, stop=True).then_inc(S["sc_ready"], 1)

                    def turn(i):
                        t = i % TILES
                        pe.wait_ge(S["p_ready"], i + 1)
                        if i >= 2:
                            pe.wait_ge(S["pt_ev"], i - 1)
                        for j in range(t + 1):
                            ins = nc.tensor.transpose(bank[2 + i % 2][:, j * P:(j + 1) * P],
                                                      prob[:, i % 3, j * P:(j + 1) * P], ident)
                        ins.then_inc(S["pt_ready"], 1)

                    def values(i):
                        h, t = divmod(i, TILES)
                        pe.wait_ge(S["pt_ev"], i + 1)
                        if i >= 2:
                            pe.wait_ge(S["o_ev"], i - 1)
                        for j in range(t + 1):
                            ins = nc.tensor.matmul(bank[4 + i % 2][:, 0:VDIM], probT[:, i % 2, j * P:(j + 1) * P],
                                                   v[:, j, h * VDIM:(h + 1) * VDIM], start=j == 0, stop=j == t)
                        ins.then_inc(S["o_ready"], 1)

                    for i in range(ITEMS + 2):
                        if i < ITEMS:
                            score(i)
                        if 1 <= i <= ITEMS:
                            turn(i - 1)
                        if i >= 2:
                            values(i - 2)
                    pe.wait_ge(S["o_ev"], ITEMS)
                    for f in range(4):
                        if f >= 2:
                            pe.wait_ge(S["at_ev"], f - 1)
                        for t in range(TILES):
                            ins = nc.tensor.transpose(bank[6 + f % 2][:, t * P:(t + 1) * P],
                                                      att[:, t, f * P:(f + 1) * P], ident)
                        ins.then_inc(S["at_ready"], 1)

                @block.vector
                def _(ve):
                    def maximum(i):
                        t = i % TILES
                        n = (t + 1) * P
                        s = bank[i % 2]
                        ve.wait_ge(S["sc_ready"], i + 1)
                        nc.vector.tensor_tensor(s[:, t * P:n], s[:, t * P:n], mask_q, ALU.add)
                        ve.drain()
                        nc.vector.tensor_reduce(scol[:, 0, i:i + 1], s[:, 0:n], AX.X, ALU.max)
                        ve.drain()
                        nc.vector.tensor_scalar(scol[:, 1, i:i + 1], scol[:, 0, i:i + 1], -SM_SCALE, None,
                                                ALU.mult).then_inc(S["nm_ready"], 1)

                    def normalise(i):
                        h, t = divmod(i, TILES)
                        ve.wait_ge(S["o_ready"], i + 1)
                        nc.vector.reciprocal(scol[:, 3, i:i + 1], scol[:, 2, i:i + 1])
                        ve.drain()
                        nc.vector.tensor_scalar(att[:, t, h * VDIM:(h + 1) * VDIM], bank[4 + i % 2][:, 0:VDIM],
                                                scol[:, 3, i:i + 1], None, ALU.mult).then_inc(S["o_ev"], 1)

                    for i in range(ITEMS + 3):
                        if i < ITEMS:
                            maximum(i)
                        if i >= 3:
                            normalise(i - 3)

                @block.scalar
                def _(ac):
                    for i in range(ITEMS + 1):
                        if i < ITEMS:
                            n = (i % TILES + 1) * P
                            ac.wait_ge(S["nm_ready"], i + 1)
                            if i >= 3:
                                ac.wait_ge(S["pt_ready"], i - 2)
                            nc.scalar.activation(prob[:, i % 3, 0:n], bank[i % 2][:, 0:n], ACT.Exp,
                                                 bias=scol[:, 1, i:i + 1], scale=SM_SCALE,
                                                 accum_out=scol[:, 2, i:i + 1])
                            ac.drain().then_inc(S["p_ready"], 1)
                        if i >= 1:
                            n = ((i - 1) % TILES + 1) * P
                            ac.wait_ge(S["pt_ready"], i)
                            if i >= 3:
                                ac.wait_ge(S["o_ready"], i - 2)
                            nc.scalar.copy(probT[:, (i - 1) % 2, 0:n], bank[2 + (i - 1) % 2][:, 0:n]
                                           ).then_inc(S["pt_ev"], 1)
                    for f in range(4):
                        ac.wait_ge(S["at_ready"], f + 1)
                        nc.scalar.copy(attT[:, f, :], bank[6 + f % 2][:, :]).then_inc(S["at_ev"], 1)

            with nc.Block() as block:
                @block.sync
                def _(sp):
                    load_weights(sp, l, IT_IF + W_SLOTS, IT_MERGE + W_SLOTS)

                @block.gpsimd
                def _(po):
                    nc.gpsimd.memset(up[:, :, 0:PAD], 0.0)
                    nc.gpsimd.memset(v1[:, :, :, MD:VW], 1.0).then_inc(S["pads"], 1)

                def turn_back(pe, h):
                    pe.wait_ge(S["hn_ready"], h + 1)
                    if h == 0:
                        pe.wait_ge(S["ae_ev"], 1)
                    else:
                        pe.wait_ge(S["y_ev"], h)
                    for t in range(TILES):
                        ins = nc.tensor.transpose(bank[2][:, t * P:(t + 1) * P], hn[:, h % 2, t * P:(t + 1) * P],
                                                  ident)
                    ins.then_inc(S["hnT_ready"], 1)

                @block.tensor
                def _(pe):
                    def free(e):
                        if e >= 2:
                            pe.wait_ge(S["d_ev"], e - 1)
                        return bank[e % 2]

                    def queries_keys(h):
                        if h == 0:
                            w_here(pe, IT_MQK)
                        w = w_ring[:, IT_MQK % W_SLOTS, :]
                        pe.wait_ge(S["ca_ready"], h + 1)
                        for q in range(2):
                            o = free(D_QK + 2 * h + q)
                            ins = nc.tensor.matmul(o[:, :], w[:, (q * MH + h) * MD:(q * MH + h + 1) * MD], ca[:, h, :],
                                                   start=True, stop=True)
                            ins.then_inc(S["d_ready"], 1)

                    for e in range(D_V):
                        w = w_here(pe, IT_IF + e)
                        o = free(e)
                        m = 64 if e == 0 else P
                        for k in range(KT):
                            ins = nc.tensor.matmul(o[0:m, :], w[:, k * P:k * P + m], hT[:, k, :], start=k == 0,
                                                   stop=k == KT - 1)
                        ins.then_inc(S["d_ready"], 1)
                    w = w_here(pe, IT_MV)
                    for t in range(TILES):
                        o = free(D_V + t)
                        for h in range(MH):
                            ins = nc.tensor.matmul(o[:, h * MD:(h + 1) * MD], up[:, h, PAD + t * P:PAD + (t + 1) * P],
                                                   w[:, h * MD:(h + 1) * MD], start=True, stop=True)
                        ins.then_inc(S["d_ready"], 1)
                    for r, row in enumerate((R_A, R_E)):
                        pe.wait_ge(S["rows_a" if r == 0 else "rows_e"], 1)
                        for t in range(TILES):
                            c = (r * TILES + t) * MH
                            ins = nc.tensor.transpose(bank[2][:, c:c + MH], rows[0:MH, row, t * P:(t + 1) * P],
                                                      ident[0:MH, 0:MH])
                    ins.then_inc(S["ae_ready"], 1)
                    queries_keys(0)
                    for h in range(MH):
                        if h >= 1:
                            pe.wait_ge(S["nmb_ev"], h)
                        nc.tensor.matmul(bank[3][:, :], sel[0:MH, h, :], rows[0:MH, R_NM, :], start=True,
                                         stop=True).then_inc(S["nmb_ready"], 1)
                        pe.wait_ge(S["d_ev"], D_QK + 2 * h + 2)
                        for s in range(TILES):
                            g = h * TILES + s
                            if g >= 2:
                                pe.wait_ge(S["pm_ready"], g - 1)
                            nc.tensor.matmul(bank[4 + g % 2][:, 0:SEQ - s * P], mk[:, h % 2, s * P:(s + 1) * P],
                                             mq[:, h % 2, s * P:SEQ], start=True, stop=True
                                             ).then_inc(S["s_ready"], 1)
                        if h + 1 < MH:
                            queries_keys(h + 1)
                        for half in range(2):
                            pe.wait_ge(S["pm_ready"], h * TILES + 2 * half + 2)
                            if h >= 1:
                                pe.wait_ge(S["n_ev"], 2 * (h - 1) + half + 1)
                            for t in (2 * half, 2 * half + 1):
                                for s in range(t + 1):
                                    o = P_OFF[s] + (t - s) * P
                                    ins = nc.tensor.matmul(bank[6 + half][:, (t % 2) * 256:(t % 2) * 256 + VW],
                                                           pm[:, h % 2, o:o + P], v1[:, s, h, :], start=s == 0,
                                                           stop=s == t)
                            ins.then_inc(S["n_ready"], 1)
                        if h >= 1:
                            turn_back(pe, h - 1)
                    turn_back(pe, MH - 1)

                @block.scalar
                def _(ac):
                    def taken(e):
                        ac.wait_ge(S["d_ready"], e + 1)
                        return bank[e % 2]

                    def queries_keys(h):
                        for q, (dst, scale) in enumerate(((mq, 1.0), (mk, K_SCALE))):
                            o = taken(D_QK + 2 * h + q)
                            nc.scalar.mul(dst[:, h % 2, :], o[:, :], scale).then_inc(S["d_ev"], 1)

                    o = taken(0)
                    nc.scalar.activation(rows[0:MH, R_I, :], o[0:MH, :], ACT.Identity,
                                         bias=cols[0:MH, C_BI:C_BI + 1])
                    nc.scalar.activation(rows[0:MH, R_F, :], o[32:32 + MH, :], ACT.Identity,
                                         bias=cols[0:MH, C_BF:C_BF + 1])
                    ac.drain().then_inc(S["d_ev"], 1)
                    nc.scalar.activation(rows[0:MH, R_T, :], rows[0:MH, R_F, :], ACT.Abs)
                    ac.drain()
                    nc.scalar.activation(rows[0:MH, R_T, :], rows[0:MH, R_T, :], ACT.Exp, scale=-1.0)
                    ac.drain()
                    nc.scalar.activation(rows[0:MH, R_LN, :], rows[0:MH, R_T, :], ACT.Ln,
                                         bias=1.0).then_inc(S["lnf"], 1)
                    for h in range(MH):
                        o = taken(1 + h)
                        nc.scalar.copy(up[:, h, PAD:UP], o[:, :]).then_inc(S["d_ev"], 1)
                    for h in range(MH):
                        o = taken(1 + MH + h)
                        nc.scalar.activation(so[:, h, :], o[:, :], ACT.Sigmoid).then_inc(S["d_ev"], 1)
                    for t in range(TILES):
                        o = taken(D_V + t)
                        nc.scalar.copy(v1[:, t, :, 0:MD], o[:, :].rearrange("p (h e) -> p h e", h=MH)
                                       ).then_inc(S["d_ev"], 1)
                    for h in range(MH):
                        ac.wait_ge(S["conv_ready"], h + 1)
                        nc.scalar.activation(ca[:, h, :], ca[:, h, :], ACT.Silu).then_inc(S["ca_ready"], 1)
                    ac.wait_ge(S["rows_s"], 1)
                    nc.scalar.activation(rows[0:MH, R_E, :], rows[0:MH, R_S, :], ACT.Exp,
                                         scale=-1.0).then_inc(S["rows_e"], 1)
                    queries_keys(0)
                    ac.wait_ge(S["ae_ev"], 1)
                    for h in range(MH):
                        ac.wait_ge(S["nmb_ready"], h + 1)
                        nc.scalar.copy(nmb[:, h % 2, :], bank[3][:, :])
                        ac.drain().then_inc(S["nmb_ev"], 1)
                        ac.wait_ge(S["nmd_ready"], h + 1)
                        for s in range(TILES):
                            g = h * TILES + s
                            if g >= 2:
                                ac.wait_ge(S["pm_ready"], g - 1)
                            a_s = ae[:, 0, s, h:h + 1]
                            ins = nc.scalar.activation(dw[:, g % 2, 0:P], nmd[:, h % 2, s * P:(s + 1) * P], ACT.Exp,
                                                       bias=a_s)
                            if s + 1 < TILES:
                                ins = nc.scalar.activation(dw[:, g % 2, P:SEQ - s * P], nmb[:, h % 2, (s + 1) * P:SEQ],
                                                           ACT.Exp, bias=a_s)
                            ac.drain().then_inc(S["dw_ready"], 1)
                        if h + 1 < MH:
                            queries_keys(h + 1)
                        ac.wait_ge(S["var_ready"], h + 1)
                        nc.scalar.activation(mcol[:, 52:56], mcol[:, 48:52], ACT.Sqrt).then_inc(S["dev_ready"], 1)

                @block.vector
                def _(ve):
                    def conv(h):
                        ve.wait_ge(S["d_ev"], h + 2)
                        if h == 0:
                            ve.wait_ge(S["pads"], 2)
                        c = C_CW + h * CONV
                        nc.vector.tensor_scalar(ca[:, h, :], up[:, h, PAD:UP], cols[:, c + PAD:c + PAD + 1],
                                                cols[:, C_CB + h:C_CB + h + 1], ALU.mult, ALU.add)
                        for j in range(PAD):
                            ve.drain()
                            nc.vector.scalar_tensor_tensor(out=ca[:, h, :], in0=up[:, h, j:j + SEQ],
                                                           scalar=cols[:, c + j:c + j + 1], in1=ca[:, h, :],
                                                           op0=ALU.mult, op1=ALU.add)
                        ve.drain().then_inc(S["conv_ready"], 1)

                    def row(r):
                        return rows[0:MH, r, :]

                    def gate_rows():
                        ve.wait_ge(S["lnf"], 1)
                        nc.vector.scalar_tensor_tensor(out=row(R_F), in0=row(R_F), scalar=0.0, in1=row(R_LN),
                                                       op0=ALU.min, op1=ALU.subtract)
                        nc.vector.memset(row(R_T), 1.0)
                        ve.drain()
                        nc.vector.tensor_tensor_scan(row(R_CUM), row(R_T), row(R_F), 0.0, ALU.mult, ALU.add)
                        ve.drain()
                        nc.vector.tensor_tensor(row(R_A), row(R_I), row(R_CUM), ALU.subtract).then_inc(S["rows_a"], 1)
                        ve.drain()
                        nc.vector.tensor_tensor_scan(row(R_M), row(R_A), row(R_A), 0.0, ALU.max, ALU.max)
                        ve.drain()
                        nc.vector.tensor_scalar(row(R_NM), row(R_M), -1.0, None, ALU.mult)
                        nc.vector.tensor_tensor(row(R_S), row(R_CUM), row(R_M), ALU.add)
                        ve.drain().then_inc(S["rows_s"], 1)

                    def weigh(h):
                        ve.wait_ge(S["nmb_ev"], h + 1)
                        nc.vector.tensor_tensor(nmd[:, h % 2, :].rearrange("p (s t) -> p s t", s=TILES),
                                                nmb[:, h % 2, :].rearrange("p (s t) -> p s t", s=TILES),
                                                mask_t.unsqueeze(1).to_broadcast([P, TILES, P]),
                                                ALU.add).then_inc(S["nmd_ready"], 1)
                        for s in range(TILES):
                            g, n = h * TILES + s, SEQ - s * P
                            ve.wait_ge(S["s_ready"], g + 1)
                            ve.wait_ge(S["dw_ready"], g + 1)
                            nc.vector.tensor_tensor(pm[:, h % 2, P_OFF[s]:P_OFF[s] + n], bank[4 + g % 2][:, 0:n],
                                                    dw[:, g % 2, 0:n], ALU.mult).then_inc(S["pm_ready"], 1)

                    def head_norm(h):
                        den, peak, inv = mcol[:, 0:4], mcol[:, 4:8], mcol[:, 8:12]
                        st6 = mcol[:, 12:36].rearrange("p (t c) -> p t c", t=TILES)
                        mv = mcol[:, 36:44].rearrange("p (t c) -> p t c", t=TILES)
                        for half in range(2):
                            ve.wait_ge(S["n_ready"], 2 * h + half + 1)
                            num = bank[6 + half][:, :].rearrange("p (t e) -> p t e", t=2)
                            nc.vector.tensor_copy(den[:, 2 * half:2 * half + 2], num[:, :, MD])
                        ve.drain()
                        nc.vector.scalar_tensor_tensor(out=peak, in0=den, scalar=-1.0, in1=den, op0=ALU.mult,
                                                       op1=ALU.max)
                        ve.drain()
                        nc.vector.tensor_tensor(peak, peak, ae[:, 1, :, h], ALU.max)
                        ve.drain()
                        nc.vector.reciprocal(inv, peak)
                        ve.drain()
                        hd = hn[:, h % 2, :].rearrange("p (t e) -> p t e", t=TILES)
                        for t in range(TILES):
                            ins = nc.vector.tensor_scalar(hd[:, t, :], bank[6 + t // 2][:, (t % 2) * 256:(t % 2) * 256 + MD],
                                                          inv[:, t:t + 1], None, ALU.mult)
                            if t % 2:
                                ins.then_inc(S["n_ev"], 1)
                        ve.drain()
                        for t in range(TILES):
                            nc.vector.bn_stats(st6[:, t, :], hd[:, t, :])
                        ve.drain()
                        for t in range(TILES):
                            nc.vector.bn_aggr(mv[:, t, :], st6[:, t, :])
                        ve.drain()
                        nc.vector.tensor_scalar(mcol[:, 48:52], mv[:, :, 1], EPS, None,
                                                ALU.add).then_inc(S["var_ready"], 1)
                        ve.wait_ge(S["dev_ready"], h + 1)
                        nc.vector.reciprocal(mcol[:, 56:60], mcol[:, 52:56])
                        ve.drain()
                        for t in range(TILES):
                            nc.vector.tensor_scalar(hd[:, t, :], hd[:, t, :], mv[:, t, 0:1], mcol[:, 56 + t:57 + t],
                                                    ALU.subtract, ALU.mult)
                        ve.drain().then_inc(S["hn_ready"], 1)

                    def gated(h):
                        nc.vector.tensor_scalar(ctmp, ca[:, h, :], cols[:, C_SK + h:C_SK + h + 1], None, ALU.mult)
                        ve.drain()
                        ve.wait_ge(S["hnT_ready"], h + 1)
                        nc.vector.scalar_tensor_tensor(out=ctmp, in0=bank[2][:, :], scalar=cols[:, C_MG + h:C_MG + h + 1],
                                                       in1=ctmp, op0=ALU.mult, op1=ALU.add).then_inc(S["y_ev"], 1)
                        ve.drain()
                        nc.vector.tensor_tensor(ymT[:, h, :], ctmp, so[:, h, :], ALU.mult)
                        ve.drain()

                    conv(0)
                    gate_rows()
                    for h in range(1, MH):
                        conv(h)
                    ve.wait_ge(S["ae_ready"], 1)
                    nc.vector.tensor_copy(ae[:, :, :, :].rearrange("p r t h -> p (r t h)"), bank[2][:, 0:32])
                    ve.drain().then_inc(S["ae_ev"], 1)
                    for h in range(MH):
                        weigh(h)
                        head_norm(h)
                        if h >= 1:
                            gated(h - 1)
                    gated(MH - 1)

            with nc.Block() as block:
                @block.sync
                def _(sp):
                    load_weights(sp, l, IT_MERGE + W_SLOTS, IT_PQ + W_SLOTS)

                @block.tensor
                def _(pe):
                    for j in range(KT):
                        o = bank[4 * (j % 2):4 * (j % 2) + 4]
                        if j >= 2:
                            pe.wait_ge(S["e_act"], 2 * (j - 1))
                            pe.wait_ge(S["e_dve"], j - 1)
                        for g in range(2):
                            w = w_here(pe, IT_MERGE + 3 * j + g)
                            for k in range(KT):
                                ins = nc.tensor.matmul(o[g][:, :], w[:, k * P:(k + 1) * P], hT[:, k, :], start=k == 0,
                                                       stop=k == KT - 1)
                            ins.then_inc(S["e_ready"], 1)
                        w = w_here(pe, IT_MERGE + 3 * j + 2)
                        for g, branch in enumerate((attT, ymT)):
                            for k in range(4):
                                ins = nc.tensor.matmul(o[2 + g][:, :], w[:, (4 * g + k) * P:(4 * g + k + 1) * P],
                                                       branch[:, k, :], start=k == 0, stop=k == 3)
                        ins.then_inc(S["e_ready"], 1)
                    pe.wait_ge(S["e_act"], 2 * KT)
                    pe.wait_ge(S["e_dve"], KT)
                    for k in range(KT):
                        w = w_here(pe, IT_OUT + k)
                        for t in range(TILES):
                            for c in range(2):
                                ins = nc.tensor.matmul(bank[2 * t + c][:, :], mgT[:, k, t * P:(t + 1) * P],
                                                       w[:, c * 512:(c + 1) * 512], start=k == 0, stop=k == KT - 1)
                                if k == KT - 1:
                                    ins.then_inc(S["wo_ready"], 1)
                        if k < KT - 1:
                            ins.then_inc(S["out_used"], 1)

                @block.scalar
                def _(ac):
                    for j in range(KT):
                        if j >= 2:
                            ac.wait_ge(S["e_dve"], j - 1)
                        for g in range(2):
                            ac.wait_ge(S["e_ready"], 3 * j + g + 1)
                            nc.scalar.activation(sg[:, j % 2, g, :], bank[4 * (j % 2) + g][:, :],
                                                 ACT.Sigmoid).then_inc(S["e_act"], 1)

                @block.vector
                def _(ve):
                    for j in range(KT):
                        ve.wait_ge(S["e_ready"], 3 * j + 3)
                        ve.wait_ge(S["e_act"], 2 * j + 2)
                        for g in range(2):
                            nc.vector.tensor_tensor(mt[:, j % 2, g, :], bank[4 * (j % 2) + 2 + g][:, :], sg[:, j % 2, g, :],
                                                    ALU.mult)
                        ve.drain()
                        nc.vector.tensor_tensor(mgT[:, j, :], mt[:, j % 2, 0, :], mt[:, j % 2, 1, :],
                                                ALU.add).then_inc(S["e_dve"], 1)
                    for t in range(TILES):
                        for c in range(2):
                            b = 2 * t + c
                            ve.wait_ge(S["wo_ready"], b + 1)
                            m = mt[:, b % 2, 0, :]
                            nc.vector.tensor_tensor(m, bank[b][:, :], ada[:, 2 * D + c * 512:2 * D + (c + 1) * 512],
                                                    ALU.mult)
                            ve.drain()
                            xs = x[:, t, c * 512:(c + 1) * 512]
                            nc.vector.tensor_tensor(xs, xs, m, ALU.add)

            SB = TILES * PH // 2
            with nc.Block() as block:
                @block.sync
                def _(sp):
                    load_weights(sp, l, IT_PQ + W_SLOTS, N_ITEMS)

                @block.tensor
                def _(pe):
                    norm_pe(pe, 1)
                    pe.wait_ge(S["tp_ev"], 4 * TILES)
                    for h in range(PH):
                        w = w_here(pe, IT_PQ + h)
                        if h >= 2:
                            pe.wait_ge(S["q_ev"], h - 1)
                        for k in range(KT):
                            ins = nc.tensor.matmul(bank[4 + h % 2][:, :], w[:, k * P:(k + 1) * P], hT[:, k, :],
                                                   start=k == 0, stop=k == KT - 1)
                        ins.then_inc(S["q_ready"], 1)
                    pe.wait_ge(S["q_ev"], PH)
                    w = [w_here(pe, IT_KEYS + i) for i in range(2)]
                    for i in range(SB):
                        t, hp = divmod(i, PH // 2)
                        if i >= 4:
                            pe.wait_ge(S["s2_act" if i % 2 == 0 else "s2_dve"], (i - 4) // 2 + 1)
                        for q in range(2):
                            h = 2 * hp + q
                            ins = nc.tensor.matmul(bank[i % 4][:, q * 256:(q + 1) * 256], qp[:, h, t * P:(t + 1) * P],
                                                   w[h // 4][:, (h % 4) * 256:(h % 4 + 1) * 256], start=True, stop=True)
                        ins.then_inc(S["s2_ready"], 1)

                @block.scalar
                def _(ac):
                    norm_act_sums(ac, 1, junk)
                    norm_act_copies(ac, 1)
                    for h in range(PH):
                        ac.wait_ge(S["q_ready"], h + 1)
                        nc.scalar.copy(qp[:, h, :], bank[4 + h % 2][:, :]).then_inc(S["q_ev"], 1)
                    for i in range(0, SB, 2):
                        ac.wait_ge(S["s2_ready"], i + 1)
                        nc.scalar.copy(scores[:, i * 512:(i + 1) * 512], bank[i % 4][:, :]).then_inc(S["s2_act"], 1)

                @block.vector
                def _(ve):
                    norm_dve(ve, 1, ada[:, 3 * D:4 * D], ada[:, 4 * D:5 * D])
                    for i in range(1, SB, 2):
                        ve.wait_ge(S["s2_ready"], i + 1)
                        nc.vector.tensor_copy(scores[:, i * 512:(i + 1) * 512], bank[i % 4][:, :]
                                              ).then_inc(S["s2_dve"], 1)

            def wait_alone(eng, s, value):
                eng.wait_ge(s, value)
                eng.sem_inc(S["passed"], 1)

            HEAD_PAIRS = PH // 2
            with nc.Block() as block:
                @block.gpsimd
                def _(po):
                    with po.Fori(0, TILES) as t:
                        with po.Fori(0, HEAD_PAIRS) as i:
                            for par in range(2):
                                n = t * PH + i * 2 + par
                                for s in range(TOPK):
                                    if s == 0:
                                        wait_alone(po, S["idx_ready"], n + 1)
                                    wait_alone(po, S["slot_free"], n * TOPK + (s + 1))
                                    po.indirect_dma_start(ring[:, s % RING, :], None, experts_in,
                                                          bass.IndirectOffsetOnAxis(ap=idx[:, par, s:s + 1], axis=0)
                                                          ).then_inc(gathered[s % RING], 16)

                @block.scalar
                def _(ac):
                    def stage_scores(n, par):
                        nc.scalar.copy(stage[:, par, :, :].rearrange("p q n -> p (q n)"),
                                       scores[:, bass.ds(n * (2 * NKEYS), 2 * NKEYS)]).then_inc(S["stage_ready"], 1)

                    def exponentials(n):
                        ac.wait_ge(S["best_ready"], n + 1)
                        nc.scalar.activation(gexp, best, ACT.Exp, bias=gs[:, 0:1], accum_out=gs[:, 1:2])
                        ac.drain().then_inc(S["exp_ready"], 1)

                    stage_scores(0, 0)
                    stage_scores(1, 1)
                    exponentials(0)
                    with ac.Fori(0, TILES) as t:
                        nc.scalar.copy(h_now, h_tok[:, bass.ds(t, 1), :].rearrange("p a d -> p (a d)")
                                       ).then_inc(S["h_now_ready"], 1)
                        with ac.Fori(0, HEAD_PAIRS) as i:
                            for par in range(2):
                                n = t * PH + i * 2 + par
                                stage_scores((n + 2) % UNITS, par)
                                for g in range(TOPK // GROUP):
                                    if g == 2:
                                        exponentials(n + 1)
                                    ac.wait_ge(S["dots_ready"], n * (TOPK // GROUP) + (g + 1))
                                    c = slice(g * GROUP, (g + 1) * GROUP)
                                    nc.scalar.activation(gel[:, par, c], dots[:, par, c],
                                                         ACT.Gelu).then_inc(S["gelu_ready"], 1)

                @block.vector
                def _(ve):
                    def top8(vals, poss, src, scratch):
                        nc.vector.max(vals, src)
                        ve.drain()
                        nc.vector.max_index(poss, vals, src)
                        if scratch is not None:
                            nc.vector.match_replace(scratch, vals, src, FLOOR)
                        ve.drain()

                    def route(part, n, par):
                        if part < 4:
                            q, half = divmod(part, 2)
                            if part == 0:
                                wait_alone(ve, S["stage_ready"], n + 1)
                            c = slice(8 * half, 8 * half + 8)
                            top8(top[:, q, c], top_i[:, q, c], rest if half else stage[:, par, q, :],
                                 None if half else rest)
                        elif part == 4:
                            a = top[:, 0, :].unsqueeze(2).to_broadcast([P, TOPK, TOPK])
                            b = top[:, 1, :].unsqueeze(1).to_broadcast([P, TOPK, TOPK])
                            nc.vector.tensor_tensor(cand[:, 0, :].rearrange("p (a b) -> p a b", a=TOPK), a, b, ALU.add)
                            nc.vector.tensor_copy(top_f[:, :, :], top_i[:, :, :])
                            ve.drain()
                            top8(best[:, 0:8], pos[:, 0:8], cand[:, 0, :], cand[:, 1, :])
                        elif part == 5:
                            top8(best[:, 8:16], pos[:, 8:16], cand[:, 1, :], None)
                            nc.vector.tensor_scalar(gs[:, 0:1], best[:, 0:1], -1.0, None, ALU.mult)
                            ve.drain().then_inc(S["best_ready"], 1)
                        elif part == 6:
                            nc.vector.tensor_scalar(posab[:, 0, :], pos, 4, None, ALU.logical_shift_right)
                            nc.vector.tensor_scalar(posab[:, 1, :], pos, 15, None, ALU.bitwise_and)
                            ve.drain()
                            nc.vector.tensor_copy(posab_f[:, :, :], posab[:, :, :])
                            ve.drain()
                            hot3 = hot.rearrange("p (k j) -> p k j", j=TOPK)
                            nc.vector.tensor_tensor(hot3, posab_f[:, :, :].rearrange("p q k -> p (q k)").unsqueeze(2)
                                                    .to_broadcast([P, 2 * TOPK, TOPK]),
                                                    iota.unsqueeze(1).to_broadcast([P, 2 * TOPK, TOPK]), ALU.is_equal)
                            ve.drain()
                            hot4 = hot.rearrange("p (q k j) -> p q k j", q=2, k=TOPK)
                            nc.vector.tensor_tensor(hot4, hot4, top_f[:, :, :].unsqueeze(2)
                                                    .to_broadcast([P, 2, TOPK, TOPK]), ALU.mult)
                            ve.drain()
                        else:
                            nc.vector.tensor_reduce(pick, hot.rearrange("p (k j) -> p k j", j=TOPK), AX.X, ALU.add)
                            ve.drain()
                            nc.vector.scalar_tensor_tensor(out=flat_i, in0=pick[:, 0:TOPK], scalar=float(NKEYS),
                                                           in1=pick[:, TOPK:2 * TOPK], op0=ALU.mult, op1=ALU.add)
                            ve.drain()
                            nc.vector.tensor_scalar(idx[:, par, :], flat_i, layer_row[:, 0:1], None, ALU.add)
                            ve.drain().then_inc(S["idx_ready"], 1)
                            ve.wait_ge(S["exp_ready"], n + 1)
                            nc.vector.reciprocal(gs[:, 2:3], gs[:, 1:2])
                            ve.drain()
                            nc.vector.tensor_scalar(gate[:, par, :], gexp, gs[:, 2:3], None, ALU.mult)
                            ve.drain()

                    for part in range(ROUTE_PARTS):
                        route(part, 0, 0)
                    for part in range(ROUTE_PARTS // 2):
                        route(part, 1, 1)
                    ve.sem_inc(S["y_free"], 1)
                    with ve.Fori(0, TILES) as t:
                        wait_alone(ve, S["h_now_ready"], t + 1)
                        with ve.Fori(0, HEAD_PAIRS) as i:
                            for par in range(2):
                                n = t * PH + i * 2 + par
                                for g in range(TOPK // GROUP):
                                    for s in range(g * GROUP, (g + 1) * GROUP):
                                        ve.wait_ge(gathered[s % RING],
                                                l * (UNITS * 32) + n * 32 + 16 * (s // RING + 1))
                                        u = ring[:, s % RING, 0:D]
                                        nc.vector.tensor_tensor_reduce(u, u, h_now, 1.0, 0.0, ALU.mult, ALU.add,
                                                                       dots[:, par, s:s + 1])
                                    ve.drain().then_inc(S["dots_ready"], 1)
                                    if g < ROUTE_PARTS // 2:
                                        route(g + ROUTE_PARTS // 2, n + 1, 1 - par)
                                    else:
                                        route(g - ROUTE_PARTS // 2, n + 2, par)
                                    ve.wait_ge(S["gelu_ready"], n * (TOPK // GROUP) + (g + 1))
                                    for s in range(g * GROUP, (g + 1) * GROUP):
                                        ve.wait_ge(S["slot_free"], n * TOPK + (s + 1))
                                        nc.vector.tensor_scalar(diag[:, s % 8, :], ident, gel[:, par, s:s + 1],
                                                                gate[:, par, s:s + 1], ALU.mult,
                                                                ALU.mult).then_inc(S["diag_ready"], 1)
                        ve.wait_ge(S["y_done"], t + 1)
                        for c in range(2):
                            nc.vector.tensor_tensor(ytmp[:, c * 512:(c + 1) * 512], bank[c][:, :],
                                                    ada[:, 5 * D + c * 512:5 * D + (c + 1) * 512], ALU.mult)
                        ve.drain().then_inc(S["y_free"], 1)
                        xt = x[:, bass.ds(t, 1), :].rearrange("p a d -> p (a d)")
                        nc.vector.tensor_tensor(xt, xt, ytmp, ALU.add)
                        ve.drain()
                    nc.vector.tensor_scalar(layer_row[:, :], layer_row[:, :], float(EXPERTS), None, ALU.add)

                @block.tensor
                def _(pe):
                    pe.sem_inc(S["slot_free"], RING)
                    with pe.Fori(0, TILES) as t:
                        pe.wait_ge(S["y_free"], t + 1)
                        for c in range(2):
                            nc.tensor.matmul(bank[c][:, :], zeros[:, 0:P], zeros[:, :], start=True, stop=False)
                        with pe.Fori(0, HEAD_PAIRS) as i:
                            for par in range(2):
                                n = t * PH + i * 2 + par
                                for s in range(TOPK):
                                    pe.wait_ge(S["diag_ready"], n * TOPK + (s + 1))
                                    for c in range(2):
                                        ins = nc.tensor.matmul(bank[c][:, :], diag[:, s % 8, :],
                                                               ring[:, s % RING, D + c * 512:D + (c + 1) * 512],
                                                               start=False, stop=False)
                                    ins.then_inc(S["slot_free"], 1)
                        for c in range(2):
                            ins = nc.tensor.matmul(bank[c][:, :], zeros[:, 0:P], zeros[:, :], start=False, stop=True)
                        ins.then_inc(S["y_done"], 1)

            nc.all_engine_barrier()
            for s in layer_sems:
                nc.gpsimd.sem_clear(s)
            nc.all_engine_barrier()

        fg = at(0, D)
        with nc.Block() as block:
            @block.sync
            def _(sp):
                sp.dma_start(fg, fg_in.to_broadcast([P, D])).then_inc(once_dma, 16)
                sp.wait_ge(S["h_ready"], 1)
                sp.dma_start(out.rearrange("(t p) d -> p t d", p=P), h_tok[:, :, :]).then_inc(stored, 16)
                sp.wait_ge(stored, 16)

            @block.scalar
            def _(ac):
                norm_act_sums(ac, 0, at(8, D))

            @block.vector
            def _(ve):
                ve.wait_ge(S["ss_ready"], 1)
                nc.vector.tensor_scalar(small[:, 4:8], small[:, 0:4], 1.0 / D, EPS, ALU.mult,
                                        ALU.add).then_inc(S["ms_ready"], 1)
                ve.wait_ge(S["sd_ready"], 1)
                nc.vector.reciprocal(small[:, 12:16], small[:, 8:12])
                ve.wait_ge(once_dma, 80)
                ve.drain()
                for t in range(TILES):
                    nc.vector.scalar_tensor_tensor(out=h_tok[:, t, :], in0=x[:, t, :], scalar=small[:, 12 + t:13 + t],
                                                   in1=fg, op0=ALU.mult, op1=ALU.mult)
                ve.drain().then_inc(S["h_ready"], 1)


def _feature_tiles(w):
    return w.reshape(w.shape[0] // P, P, w.shape[1]).transpose(1, 0, 2)


def _item(parts):
    flat = parts.reshape(P, -1)
    out = np.zeros((P, D), np.float32)
    out[:, :flat.shape[1]] = flat
    return out


def _weights(a, l):
    w = a["w_in"][l]
    edge = np.cumsum([0, Q_LORA, KV_LORA, ROPE, MI, MI, MH, MH, D, D])
    q, kv, kr, u, o, i, f, ga, gm = (w[:, edge[n]:edge[n + 1]] for n in range(9))
    swap = np.r_[ROPE // 2:ROPE, 0:ROPE // 2]
    items = [_item(_feature_tiles(kv[:, j * P:(j + 1) * P])) for j in range(KVT)]
    items += [_item(_feature_tiles(q[:, j * P:(j + 1) * P])) for j in range(QT)]
    none = np.zeros((D, NOPE), np.float32)
    items.append(_item(_feature_tiles(np.concatenate([none, kr, kr[:, swap]], 1))))
    up = a["w_kv_up"][l].reshape(KV_LORA, HEADS, NOPE + VDIM)
    items.append(_item(_feature_tiles(up[:, :, :NOPE].reshape(KV_LORA, -1))))
    items.append(_item(_feature_tiles(up[:, :, NOPE:].reshape(KV_LORA, -1))))
    qu = a["w_q_up"][l].reshape(Q_LORA, HEADS, QK)
    for h in range(HEADS):
        r = qu[:, h, NOPE:]
        items.append(_item(_feature_tiles(np.concatenate([qu[:, h, :NOPE], r, r[:, swap]], 1))))
    gates = np.zeros((D, P), np.float32)
    gates[:, 0:MH] = i
    gates[:, 32:32 + MH] = f
    items.append(_item(_feature_tiles(gates)))
    for m in (u, o):
        items += [_item(_feature_tiles(m[:, j * P:(j + 1) * P])) for j in range(MH)]
    items.append(_item(np.concatenate([a["wq_m"][l].transpose(1, 0, 2).reshape(P, -1),
                                       a["wk_m"][l].transpose(1, 0, 2).reshape(P, -1)], 1)))
    items.append(_item(a["wv_m"][l].transpose(1, 0, 2)))
    for j in range(KT):
        c = slice(j * P, (j + 1) * P)
        items += [_item(_feature_tiles(ga[:, c])), _item(_feature_tiles(gm[:, c]))]
        items.append(_item(np.concatenate([_feature_tiles(a["w_branch_a"][l][:, c]),
                                           _feature_tiles(a["w_branch_m"][l][:, c])], 1)))
    items += [_item(a["w_out"][l][k * P:(k + 1) * P]) for k in range(KT)]
    items += [_item(_feature_tiles(a["peer_wq"][l][:, h * P:(h + 1) * P])) for h in range(PH)]
    keys = np.zeros((P, PH, 2, NKEYS), np.float32)
    for q2 in range(2):
        keys[q2 * HALF:(q2 + 1) * HALF, :, q2, :] = a["peer_keys"][l][:, q2].transpose(2, 0, 1)
    keys = keys.reshape(P, PH, 2 * NKEYS)
    items += [_item(keys[:, 0:4]), _item(keys[:, 4:8])]
    return np.stack(items)


def _columns(a, l):
    c = np.zeros((P, N_COLS), np.float32)
    c[:, C_QG:C_QG + QT] = a["q_norm_g"][l].reshape(QT, P).T
    c[:, C_KVG:C_KVG + KVT] = a["kv_norm_g"][l].reshape(KVT, P).T
    c[:, C_CW:C_CW + MH * CONV] = a["conv_w"][l].reshape(CONV, MH, P).transpose(2, 1, 0).reshape(P, -1)
    c[:, C_CB:C_CB + MH] = a["conv_b"][l].reshape(MH, P).T
    c[:, C_MG:C_MG + MH] = a["mh_norm_g"][l].reshape(MH, P).T
    c[:, C_SK:C_SK + MH] = a["m_skip"][l].reshape(MH, P).T
    c[0:MH, C_BI] = a["b_i"][l]
    c[0:MH, C_BF] = a["b_f"][l]
    return c


def _constants():
    c = np.zeros((P, N_CONST), np.float32)
    c[:, K_ID:K_ID + P] = np.eye(P)
    above = np.triu(np.full((P, P), NEG, np.float32), 1)
    c[:, K_MQ:K_MQ + P] = above
    c[:, K_MT:K_MT + P] = above.T
    for h in range(MH):
        c[h, K_SEL + h * P:K_SEL + (h + 1) * P] = 1.0
    c[:, K_IOTA:K_IOTA + TOPK] = np.arange(TOPK)
    freq = np.float32(THETA) ** (-np.arange(0, ROPE, 2, dtype=np.float32) / np.float32(ROPE))
    c[64:128, K_FREQ] = np.tile(freq, 4)
    c[96:112, K_SIGN] = -1.0
    c[112:128, K_SIGN] = 1.0
    c[:, K_HPI] = np.pi / 2
    return c


def kernel(**inputs):
    import concourse.bacc as bacc
    from concourse.bass_utils import run_bass_kernel_spmd

    a = {k: np.asarray(v) for k, v in inputs.items()}
    wada = a["w_ada"].reshape(DEPTH, KT, P, ADA_STEPS, ADA_W).transpose(0, 3, 2, 1, 4)
    arrays = {
        "x": a["x"][0],
        "c_cols": a["c"][0].reshape(KT, P).T,
        "positions": a["positions"],
        "w_ada": wada.reshape(DEPTH, ADA_STEPS, P, KT * ADA_W),
        "b_ada": a["b_ada"],
        "norm_g": np.stack([a["norm1_g"], a["norm2_g"]], 1),
        "weights": np.stack([_weights(a, l) for l in range(DEPTH)]),
        "columns": np.stack([_columns(a, l) for l in range(DEPTH)]),
        "constants": _constants(),
        "final_g": a["final_g"][None, :],
        "experts": np.concatenate([a["peer_u"], a["peer_v"]], -1).reshape(DEPTH * EXPERTS, ROW),
    }
    arrays = {k: np.ascontiguousarray(v) for k, v in arrays.items()}
    nc = bacc.Bacc("TRN2", target_bir_lowering=False, num_devices=1)
    args = [nc.dram_tensor("in_" + k, v.shape, mybir.dt.from_np(v.dtype), kind="ExternalInput").ap()
            for k, v in arrays.items()]
    out = nc.dram_tensor("out_0", (SEQ, D), F32, kind="ExternalOutput").ap()
    build_trunk(nc, *args, out)
    r = run_bass_kernel_spmd(nc, [{"in_" + k: v for k, v in arrays.items()}], core_ids=[0])
    return r.results[0]["out_0"].reshape(1, SEQ, D)
```

```python
from contextlib import ExitStack

import numpy as np

import concourse.bass as bass
from concourse import mybir

F32 = mybir.dt.float32
U32 = mybir.dt.uint32
I32 = mybir.dt.int32
ALU = mybir.AluOpType
ACT = mybir.ActivationFunctionType
AX = mybir.AxisListType

P = 128
D = 1024
SEQ = 512
DEPTH = 2
TILES = SEQ // P
KT = D // P
HEADS = 8
NOPE, ROPE, VDIM = 64, 32, 64
QK = NOPE + ROPE
Q_LORA, KV_LORA = 768, 256
QT, KVT = Q_LORA // P, KV_LORA // P
THETA = 10000.0
MH, MD = 4, 128
MI = MH * MD
CONV = 4
PH, NKEYS, HALF, TOPK = 8, 128, 64, 16
EXPERTS = NKEYS * NKEYS
EPS = 1e-6
NEG = -1e30
FLOOR = -3.0e38
SM_SCALE = QK ** -0.5
K_SCALE = MD ** -0.5

IT_KV, IT_Q, IT_KPE = 0, KVT, KVT + QT
IT_KUP, IT_VUP, IT_QUP = IT_KPE + 1, IT_KPE + 2, IT_KPE + 3
IT_IF = IT_QUP + HEADS
IT_U, IT_O = IT_IF + 1, IT_IF + 1 + MH
IT_MV = IT_O + MH
IT_GA = IT_MV + 1
IT_MERGE = IT_GA + KT
IT_OUT = IT_MERGE + 2 * KT
IT_PQ = IT_OUT + KT
N_ITEMS = IT_PQ + PH + 2
IT_MQK = N_ITEMS
W_SLOTS = 6

ADA = 6 * D
ADA_W = 256
ADA_STEPS = ADA // ADA_W
ADA_SLOTS = 2
ADA_FIRST = 2 * D // ADA_W
SEC = D // ADA_W
ADA_LATE = ADA_STEPS - ADA_FIRST
ADA_ORDER = [*range(ADA_FIRST, ADA_STEPS), *range(ADA_FIRST)]

GATE_AT = [max(j, 2 * j - 1) for j in range(KT)]
BRANCH_AT = [min(2 * j + 2, KT + j) for j in range(KT)]
assert sorted(GATE_AT + BRANCH_AT) == list(range(2 * KT))

C_QG, C_KVG = 0, QT
C_CW = C_KVG + KVT
C_CB = C_CW + MH * CONV
C_MG, C_SK = C_CB + MH, C_CB + 2 * MH
C_BI, C_BF = C_CB + 3 * MH, C_CB + 3 * MH + 1
N_COLS = C_BF + 1

K_ID, K_MQ, K_MT, K_SEL = 0, P, 2 * P, 3 * P
K_IOTA = K_SEL + MH * P
K_FREQ, K_SIGN, K_HPI = K_IOTA + TOPK, K_IOTA + TOPK + 1, K_IOTA + TOPK + 2
N_CONST = K_HPI + 1

B_KPE = KVT + QT
B_K, B_V = B_KPE + 1, B_KPE + 1 + HEADS
B_Q = B_V + TILES
B_N = B_Q + HEADS
D_V = 1 + 2 * MH
D_HEAD = D_V + TILES
D_GA = KT // MH
D_PER = 2 + D_GA
D_N = D_HEAD + MH * D_PER

UNITS = TILES * PH
RING = 8
GROUP = 2
ROUTE_PARTS = TOPK // GROUP
assert ROUTE_PARTS == 8
ROW = 2 * D
TWO_PI = 6.283185307179586
PI_LO = 3.1415925
ROUND = 12582912.0
TP_HI = 6.28125
TP_LO = TWO_PI - TP_HI


def build_trunk(nc, x_in, ct_in, pos_in, wada_in, bada_in, ng_in, w_in, cols_in, const_in, fg_in,
                experts_in, out):
    with ExitStack() as ctx:
        def sb(name, shape, dt=F32):
            return ctx.enter_context(nc.sbuf_tensor(name, shape, dt))

        def sem(name):
            return ctx.enter_context(nc.semaphore(name))

        x = sb("x", [P, TILES, D])
        V_PAD = 64
        ada_all = sb("ada", [P, V_PAD + ADA])
        ada = ada_all[:, V_PAD:V_PAD + ADA]
        const = sb("const", [P, N_CONST])
        ones = sb("ones", [P, P])
        zeros = sb("zeros", [P, P])
        cols = sb("cols", [P, N_COLS])
        rope = sb("rope", [P, SEQ])
        cact = sb("cact", [P, KT])
        layer_row = sb("layer_row", [P, 1])
        small = sb("small", [P, 32])
        h_tok = sb("h_tok", [P, TILES, D])
        hT = sb("hT", [P, KT, SEQ])
        w_ring = sb("w_ring", [P, W_SLOTS, D])
        w_mqk = sb("w_mqk", [P, D])
        ARENA = 100 * 256
        arena = sb("arena", [P, ARENA])
        hT_flat = hT[:, :, :].rearrange("p k t -> p (k t)")
        h_flat = h_tok[:, :, :].rearrange("p t d -> p (t d)")

        def at(kib, n, area=None):
            a = arena if area is None else area
            o = int(kib * 256)
            return a[:, o:o + n]

        ident = const[:, K_ID:K_ID + P]
        mask_q = const[:, K_MQ:K_MQ + P]
        mask_t = const[:, K_MT:K_MT + P]
        sel = const[:, K_SEL:K_SEL + MH * P].rearrange("p (h m) -> p h m", h=MH)
        iota = const[:, K_IOTA:K_IOTA + TOPK]

        lat = at(0, 8 * SEQ).rearrange("p (j t) -> p j t", j=8)
        sq = at(16, 2 * SEQ).rearrange("p (b t) -> p b t", b=2)
        qh = at(20, HEADS * SEQ).rearrange("p (h t) -> p h t", h=HEADS)
        kh = at(36, HEADS * SEQ).rearrange("p (h t) -> p h t", h=HEADS)
        v = at(52, TILES * SEQ).rearrange("p (t e) -> p t e", t=TILES)
        kpe = at(60, SEQ)
        rtmp = at(62, SEQ)
        rms = at(64, SEQ)
        ada_early, ada_late = ((at(k, ADA_SLOTS * KT * ADA_W).rearrange("p (s k n) -> p s k n", s=ADA_SLOTS, k=KT),
                                at(k + 16, 2 * ADA_W).rearrange("p (b n) -> p b n", b=2), at(g, D))
                               for k, g in ((66, 84), (36, 60)))
        junk = at(0, D)
        ada_once = (*ada_early, list(range(ADA_FIRST)))
        ada_early, ada_late = (*ada_early, ADA_ORDER), (*ada_late, ADA_ORDER)
        prob = at(0, 3 * SEQ).rearrange("p (b t) -> p b t", b=3)
        probT = at(6, 2 * SEQ).rearrange("p (b t) -> p b t", b=2)
        scol = at(10, 5 * 32).rearrange("p (r i) -> p r i", r=5)
        so = at(11, MH * SEQ).rearrange("p (h t) -> p h t", h=MH)
        att = at(62, TILES * SEQ).rearrange("p (t e) -> p t e", t=TILES)
        PAD = CONV - 1
        UP = SEQ + PAD
        up = at(70, MH * UP).rearrange("p (h t) -> p h t", h=MH)
        ca = at(79, MH * SEQ).rearrange("p (h t) -> p h t", h=MH)
        attT = at(92, 4 * SEQ).rearrange("p (k t) -> p k t", k=4)
        row_i, row_f = (at(k, SEQ)[0:MH, :] for k in (87, 89))
        row_t, row_ln, row_cum, row_m, row_s = (at(2 * k, SEQ, h_flat)[0:MH, :] for k in range(5))
        row_nm = at(60, SEQ)[0:MH, :]
        row_a, row_e = row_i, row_s
        VW = MD + 1
        assert TILES * MH * VW <= V_PAD + 2 * D
        v1 = at(0, TILES * MH * VW, ada_all).rearrange("p (t h e) -> p t h e", t=TILES, h=MH)
        ae = at(10.75, 32).rearrange("p (r t h) -> p r t h", r=2, t=TILES)
        nmb = at(20, 2 * SEQ).rearrange("p (b t) -> p b t", b=2)
        nmd = at(24, 2 * SEQ).rearrange("p (b t) -> p b t", b=2)
        dw = at(28, 2 * SEQ).rearrange("p (b t) -> p b t", b=2)
        mk = at(32, 2 * SEQ).rearrange("p (b t) -> p b t", b=2)
        mq = at(53, 2 * SEQ).rearrange("p (b t) -> p b t", b=2)
        mcol = at(62, 64)
        P_OFF = [0, 512, 896, 1152]
        pm = at(0, 2 * 1280).rearrange("p (b t) -> p b t", b=2)
        hn = at(65, 2 * MI).rearrange("p (b e) -> p b e", b=2)
        ymT = at(0, MH * SEQ, h_flat).rearrange("p (h t) -> p h t", h=MH)
        ctmp = at(8, SEQ, h_flat)
        ga_raw = [at(k, SEQ) for k in (70, 72, 74, 76)] + [at(k, SEQ, h_flat) for k in (10, 12, 14)] + [at(57, SEQ)]
        mgT = at(0, KT * SEQ).rearrange("p (k t) -> p k t", k=KT)
        sg = at(16, 4 * SEQ).rearrange("p (b g t) -> p b g t", b=2, g=2)
        mt = at(24, 4 * SEQ).rearrange("p (b g t) -> p b g t", b=2, g=2)
        qp = at(48, PH * SEQ).rearrange("p (h t) -> p h t", h=PH)
        scores = at(68, UNITS * 2 * NKEYS)
        ring = at(0, RING * ROW).rearrange("p (r d) -> p r d", r=RING)
        h_now = at(0, D, hT_flat)
        diag = at(4, 8 * P, hT_flat).rearrange("p (r m) -> p r m", r=8)
        ytmp = at(8, D, hT_flat)
        stage = at(0, 2 * 2 * NKEYS, w_mqk).rearrange("p (b q n) -> p b q n", b=2, q=2)
        cand = at(2, 2 * TOPK * TOPK, w_mqk).rearrange("p (b n) -> p b n", b=2)
        hot = at(64, 2 * TOPK * TOPK)
        rest = at(66, NKEYS)
        rcol = at(66.5, 20 * TOPK)
        top = rcol[:, 0:2 * TOPK].rearrange("p (q n) -> p q n", q=2)
        top_i = rcol[:, 2 * TOPK:4 * TOPK].bitcast(U32).rearrange("p (q n) -> p q n", q=2)
        top_f = rcol[:, 4 * TOPK:6 * TOPK].rearrange("p (q n) -> p q n", q=2)
        best = rcol[:, 6 * TOPK:7 * TOPK]
        pos = rcol[:, 7 * TOPK:8 * TOPK].bitcast(U32)
        posab = rcol[:, 8 * TOPK:10 * TOPK].bitcast(U32).rearrange("p (q n) -> p q n", q=2)
        posab_f = rcol[:, 10 * TOPK:12 * TOPK].rearrange("p (q n) -> p q n", q=2)
        pick = rcol[:, 12 * TOPK:14 * TOPK]
        flat_i = rcol[:, 14 * TOPK:15 * TOPK]
        gexp = rcol[:, 15 * TOPK:16 * TOPK]
        gate = rcol[:, 16 * TOPK:18 * TOPK].rearrange("p (b n) -> p b n", b=2)
        dots = sb("dots", [P, 2, TOPK])
        gel = sb("gel", [P, 2, TOPK])
        idx = sb("idx", [P, 2, TOPK], U32)
        gs = sb("gs", [P, 4])
        ang = at(0, SEQ)
        turns = at(2, SEQ)
        pos_i = at(4, SEQ).bitcast(I32)

        bank = [ctx.enter_context(nc.psum_tensor(f"bank{i}", [P, 512], F32)) for i in range(8)]

        gathered = [sem(f"gathered{r}") for r in range(RING)]
        once_dma, once_act, once_dve, stored = sem("once_dma"), sem("once_act"), sem("once_dve"), sem("stored")
        names = ("out_used ada_acc ada_sum ada_ev bias_loaded cols_loaded mqk_loaded ss_ready ms_ready sd_ready h_ready tp_ready tp_ev "
                 "mm_ready act_ev dve_ev sq_ready ss_mm rt_ready sqrt_ready latn "
                 "sc_ready nm_ready p_ready pt_ready pt_ev o_ready o_ev at_ready at_ev "
                 "d_ready d_ev kpe_ready pads lnf rows_a rows_s rows_e ae_ready ae_ev conv_ready "
                 "nmb_ready nmb_ev nmd_ready dw_ready s_ready pm_ready n_ready n_ev var_ready dev_ready "
                 "hn_ready hnT_ready y_ev e_ready e_act e_dve wo_ready x_ready "
                 "q_ready q_ev s2_ready s2_act s2_dve "
                 "passed stage_ready best_ready exp_ready idx_ready dots_ready gelu_ready diag_ready "
                 "slot_free h_now_ready y_done y_free").split()
        w_loaded = [sem(f"w_loaded{i}") for i in range(W_SLOTS)]
        ada_loaded = [sem(f"ada_loaded{i}") for i in range(ADA_SLOTS)]
        S = {n: sem(n) for n in names}
        layer_sems = w_loaded + ada_loaded + list(S.values())

        def w_here(pe, item):
            pe.wait_ge(w_loaded[item % W_SLOTS], 16 * (item // W_SLOTS + 1))
            return w_ring[:, item % W_SLOTS, :]

        def item_used(sp, i):
            if i < IT_KUP:
                sp.wait_ge(S["mm_ready"], i + 1)
            elif i == IT_KUP:
                sp.wait_ge(S["mm_ready"], B_V)
            elif i < IT_IF:
                sp.wait_ge(S["mm_ready"], B_Q + i - IT_VUP)
            elif i < IT_MV:
                sp.wait_ge(S["d_ready"], i - IT_IF + 1)
            elif i < IT_GA:
                sp.wait_ge(S["d_ready"], D_HEAD)
            elif i < IT_MERGE:
                h, j = divmod(i - IT_GA, D_GA)
                sp.wait_ge(S["d_ready"], D_HEAD + h * D_PER + 2 + j + 1)
            elif i < IT_OUT:
                sp.wait_ge(S["e_ready"], i - IT_MERGE + 1)
            elif i < IT_PQ - 1:
                sp.wait_ge(S["out_used"], i - IT_OUT + 1)
            elif i == IT_PQ - 1:
                sp.wait_ge(S["wo_ready"], 2 * TILES)
            else:
                sp.wait_ge(S["q_ready"], i - IT_PQ + 1)

        def load_weights(sp, l, first, last):
            for i in range(first, min(last, N_ITEMS)):
                if i >= W_SLOTS:
                    item_used(sp, i - W_SLOTS)
                sp.dma_start(w_ring[:, i % W_SLOTS, :],
                             w_in[bass.ds(l, 1), i].rearrange("a p n -> (a p) n")
                             ).then_inc(w_loaded[i % W_SLOTS], 16)

        def load_ada(sp, area, l, i):
            k = area[3][i]
            if i >= ADA_SLOTS:
                sp.wait_ge(S["ada_acc"], i - ADA_SLOTS + 1)
            sp.dma_start(area[0][:, i % ADA_SLOTS, :, :].rearrange("p k n -> p (k n)"),
                         wada_in[bass.ds(l, 1), k].rearrange("a p n -> (a p) n")
                         ).then_inc(ada_loaded[i % ADA_SLOTS], 16)

        def load_ada_bias(sp, l, first, last):
            sp.dma_start(ada[:, first * D:last * D],
                         bada_in[bass.ds(l, 1), first * D:last * D].to_broadcast([P, (last - first) * D])
                         ).then_inc(S["bias_loaded"], 16)

        def load_gain(sp, area, l, n):
            sp.dma_start(area[2], ng_in[bass.ds(l, 1), n:n + 1, :].rearrange("a b n -> (a b) n")
                         .to_broadcast([P, D])).then_inc(S["bias_loaded"], 16)

        def ada_sum_dve(ve, area, i):
            ve.wait_ge(ada_loaded[i % ADA_SLOTS], 16 * (i // ADA_SLOTS + 1))
            if i >= 2:
                ve.wait_ge(S["ada_sum"], i - 1)
            a, w = area[1][:, i % 2, :], area[0][:, i % ADA_SLOTS]
            ins = nc.vector.tensor_scalar(a, w[:, 0, :], cact[:, 0:1], None, ALU.mult)
            for j in range(1, KT):
                ve.drain()
                ins = nc.vector.scalar_tensor_tensor(out=a, in0=w[:, j, :], scalar=cact[:, j:j + 1], in1=a,
                                                     op0=ALU.mult, op1=ALU.add)
            ins.then_inc(S["ada_acc"], 1)

        def ada_bias_dve(ve, area, i):
            k = area[3][i]
            ve.wait_ge(S["ada_sum"], i + 1)
            if i in (0, ADA_LATE):
                ve.wait_ge(S["bias_loaded"], 32 if i == 0 else 64)
            a = ada[:, k * ADA_W:(k + 1) * ADA_W]
            nc.vector.tensor_tensor(a, a, bank[6 + i % 2][:, 0:ADA_W], ALU.add).then_inc(S["ada_ev"], 1)
            if k // SEC in (1, 4):
                g = area[2][:, (k % SEC) * ADA_W:(k % SEC + 1) * ADA_W]
                ve.drain()
                nc.vector.scalar_tensor_tensor(out=a, in0=a, scalar=1.0, in1=g, op0=ALU.add, op1=ALU.mult)

        def ada_step_dve(ve, area, i, first, last):
            if i < last:
                ada_sum_dve(ve, area, i)
            if i > first:
                ada_bias_dve(ve, area, i - 1)

        def ada_pe(pe, area, i):
            pe.wait_ge(S["ada_acc"], i + 1)
            if i >= 2:
                pe.wait_ge(S["ada_ev"], i - 1)
            nc.tensor.matmul(bank[6 + i % 2][:, 0:ADA_W], ones[:, :], area[1][:, i % 2, :], start=True,
                             stop=True).then_inc(S["ada_sum"], 1)

        def clear_semaphores():
            nc.all_engine_barrier()
            for s in layer_sems:
                nc.gpsimd.sem_clear(s)
            nc.all_engine_barrier()

        def norm_act_sums(ac, n, scratch):
            for t in range(TILES):
                ac.drain()
                if n == 1:
                    ac.wait_ge(S["x_ready"], t + 1)
                ins = nc.scalar.activation(scratch, x[:, t, :], ACT.Square, accum_out=small[:, t:t + 1])
            ac.drain().then_inc(S["ss_ready"], 1)
            ac.wait_ge(S["ms_ready"], n + 1)
            nc.scalar.activation(small[:, 8:12], small[:, 4:8], ACT.Sqrt).then_inc(S["sd_ready"], 1)

        def norm_dve(ve, n, shift, gain):
            ve.wait_ge(S["ss_ready"], n + 1)
            nc.vector.tensor_scalar(small[:, 4:8], small[:, 0:4], 1.0 / D, EPS, ALU.mult,
                                    ALU.add).then_inc(S["ms_ready"], 1)
            ve.wait_ge(S["sd_ready"], n + 1)
            nc.vector.reciprocal(small[:, 12:16], small[:, 8:12])
            ve.drain()
            for t in range(TILES):
                nc.vector.scalar_tensor_tensor(out=h_tok[:, t, :], in0=x[:, t, :], scalar=small[:, 12 + t:13 + t],
                                               in1=gain, op0=ALU.mult, op1=ALU.mult)
                ve.drain()
                nc.vector.tensor_tensor(h_tok[:, t, :], h_tok[:, t, :], shift, ALU.add).then_inc(S["h_ready"], 1)

        def norm_pe(pe, n):
            for t in range(TILES):
                pe.wait_ge(S["h_ready"], n * TILES + t + 1)
                for g in range(2):
                    i = 2 * t + g
                    if i >= 4:
                        pe.wait_ge(S["tp_ev"], n * 2 * TILES + i - 3)
                    for j in range(4):
                        ins = nc.tensor.transpose(bank[i % 4][:, j * P:(j + 1) * P],
                                                  h_tok[:, t, (4 * g + j) * P:(4 * g + j + 1) * P], ident)
                    ins.then_inc(S["tp_ready"], 1)

        def norm_act_copies(ac, n):
            for t in range(TILES):
                for g in range(2):
                    i = 2 * t + g
                    ac.wait_ge(S["tp_ready"], n * 2 * TILES + i + 1)
                    nc.scalar.copy(hT[:, 4 * g:4 * g + 4, t * P:(t + 1) * P],
                                   bank[i % 4][:, :].rearrange("p (j t) -> p j t", j=4)).then_inc(S["tp_ev"], 1)

        with nc.Block() as block:
            @block.sync
            def _(sp):
                sp.dma_start(x[:, :, :], x_in.rearrange("(t p) d -> p t d", p=P)).then_inc(once_dma, 16)
                sp.dma_start(const[:, :], const_in).then_inc(once_dma, 16)
                sp.dma_start(cact[:, :], ct_in).then_inc(once_dma, 16)
                sp.dma_start(pos_i, pos_in.to_broadcast([P, SEQ])).then_inc(once_dma, 16)
                for i in range(ADA_SLOTS):
                    load_ada(sp, ada_once, 0, i)
                load_ada_bias(sp, 0, 0, 2)
                load_gain(sp, ada_once, 0, 0)
                for i in range(ADA_SLOTS, ADA_FIRST):
                    load_ada(sp, ada_once, 0, i)

            @block.tensor
            def _(pe):
                for i in range(ADA_FIRST):
                    ada_pe(pe, ada_once, i)

            @block.vector
            def _(ve):
                nc.vector.memset(ones[:, :], 1.0)
                nc.vector.memset(zeros[:, :], 0.0)
                nc.vector.memset(layer_row[:, :], 0.0)
                ve.wait_ge(once_dma, 64)
                nc.vector.tensor_copy(ang, pos_i)
                ve.drain()
                nc.vector.tensor_scalar(ang, ang, const[:, K_FREQ:K_FREQ + 1], None, ALU.mult)
                ve.drain()
                nc.vector.tensor_scalar(turns, ang, 1.0 / TWO_PI, ROUND, ALU.mult, ALU.add)
                ve.drain()
                nc.vector.tensor_scalar(turns, turns, ROUND, None, ALU.subtract)
                ve.drain()
                for part in (TP_HI, TP_LO):
                    nc.vector.scalar_tensor_tensor(out=ang, in0=turns, scalar=-part, in1=ang, op0=ALU.mult,
                                                   op1=ALU.add)
                    ve.drain()
                nc.vector.tensor_scalar(ang, ang, PI_LO, -PI_LO, ALU.min, ALU.max).then_inc(once_dve, 1)
                ve.drain()
                ve.wait_ge(once_act, 1)
                for i in range(ADA_FIRST + 1):
                    ada_step_dve(ve, ada_once, i, 0, ADA_FIRST)

            @block.scalar
            def _(ac):
                ac.wait_ge(once_dma, 64)
                nc.scalar.activation(cact[:, :], cact[:, :], ACT.Silu).then_inc(once_act, 1)
                ac.wait_ge(once_dve, 1)
                nc.scalar.activation(turns[64:96, :], ang[64:96, :], ACT.Abs)
                ac.drain()
                nc.scalar.activation(rope[64:96, :], turns[64:96, :], ACT.Sin, scale=-1.0,
                                     bias=const[64:96, K_HPI:K_HPI + 1])
                nc.scalar.activation(rope[96:128, :], ang[96:128, :], ACT.Sin,
                                     scale=const[96:128, K_SIGN:K_SIGN + 1]).then_inc(once_act, 1)

        clear_semaphores()
        with nc.Fori(0, DEPTH) as l:
            with nc.Block() as block:
                @block.sync
                def _(sp):
                    sp.dma_start(cols[:, :], cols_in[bass.ds(l, 1)].rearrange("a p n -> (a p) n")
                                 ).then_inc(S["cols_loaded"], 16)
                    load_weights(sp, l, 0, W_SLOTS)

                @block.vector
                def _(ve):
                    norm_dve(ve, 0, ada[:, 0:D], ada[:, D:2 * D])

                @block.tensor
                def _(pe):
                    norm_pe(pe, 0)

                @block.scalar
                def _(ac):
                    norm_act_sums(ac, 0, junk)
                    norm_act_copies(ac, 0)

            act_tiles = [b for b in range(B_N) if b != B_KPE]
            dve_tiles = [b for b in range(B_N) if b == B_KPE or b >= B_Q]

            ADA_AFTER = [*range(1, B_KPE + 1), B_K + 6, B_V + 1, B_V + 3, B_Q, B_Q + 3, B_Q + 5, B_Q + 7, B_Q + 7]

            def bank_free(pe, b):
                if b in act_tiles:
                    pe.wait_ge(S["act_ev"], act_tiles.index(b) + 1)
                if b in dve_tiles:
                    pe.wait_ge(S["dve_ev"], dve_tiles.index(b) + 1)

            with nc.Block() as block:
                @block.sync
                def _(sp):
                    for i in range(ADA_SLOTS):
                        load_ada(sp, ada_early, l, i)
                    load_ada_bias(sp, l, 2, 6)
                    load_gain(sp, ada_early, l, 1)
                    for i in range(W_SLOTS, IT_IF + W_SLOTS):
                        load_weights(sp, l, i, i + 1)
                        if ADA_SLOTS + i - W_SLOTS < ADA_LATE:
                            load_ada(sp, ada_early, l, ADA_SLOTS + i - W_SLOTS)
                    sp.dma_start(w_mqk[:, :], w_in[bass.ds(l, 1), IT_MQK].rearrange("a p n -> (a p) n")
                                 ).then_inc(S["mqk_loaded"], 16)

                @block.tensor
                def _(pe):
                    def square_sum(b):
                        pe.wait_ge(S["sq_ready"], b + 1)
                        nc.tensor.matmul(bank[3 if b < KVT else 4][:, :], ones[:, :], sq[:, b % 2, :],
                                         start=b in (0, KVT), stop=b in (KVT - 1, B_KPE - 1)
                                         ).then_inc(S["ss_mm"], 1)

                    for b in range(B_N):
                        if b >= 3:
                            bank_free(pe, b - 3)
                        o = bank[b % 3]
                        if b <= B_KPE:
                            w = w_here(pe, b)
                            for k in range(KT):
                                ins = nc.tensor.matmul(o[:, :], w[:, k * P:(k + 1) * P], hT[:, k, :],
                                                       start=k == 0, stop=k == KT - 1)
                            ins.then_inc(S["mm_ready"], 1)
                        elif b < B_V:
                            if b == B_K:
                                w = w_here(pe, IT_KUP)
                                pe.wait_ge(S["latn"], 1)
                            h = b - B_K
                            for j in range(KVT):
                                ins = nc.tensor.matmul(o[0:NOPE, :], w[:, j * 512 + h * NOPE:j * 512 + (h + 1) * NOPE],
                                                       lat[:, j, :], start=j == 0, stop=j == KVT - 1)
                            ins.then_inc(S["mm_ready"], 1)
                        elif b < B_Q:
                            if b == B_V:
                                w = w_here(pe, IT_VUP)
                            t = b - B_V
                            for j in range(KVT):
                                ins = nc.tensor.matmul(o[:, :], lat[:, j, t * P:(t + 1) * P],
                                                       w[:, j * 512:(j + 1) * 512], start=j == 0, stop=j == KVT - 1)
                            ins.then_inc(S["mm_ready"], 1)
                        else:
                            w = w_here(pe, IT_QUP + b - B_Q)
                            if b == B_Q:
                                pe.wait_ge(S["latn"], 2)
                            for j in range(QT):
                                ins = nc.tensor.matmul(o[:, :], w[:, j * P:(j + 1) * P], lat[:, KVT + j, :],
                                                       start=j == 0, stop=j == QT - 1)
                            ins.then_inc(S["mm_ready"], 1)
                        if 1 <= b <= B_KPE:
                            square_sum(b - 1)
                        for i in range(ADA_LATE):
                            if ADA_AFTER[i] == b:
                                ada_pe(pe, ada_early, i)

                @block.scalar
                def _(ac):
                    def sqrt(n):
                        ac.wait_ge(S["rt_ready"], n)
                        nc.scalar.activation(rms, rms, ACT.Sqrt).then_inc(S["sqrt_ready"], 1)

                    for b in act_tiles:
                        ac.wait_ge(S["mm_ready"], b + 1)
                        o = bank[b % 3]
                        if b < B_KPE:
                            nc.scalar.copy(lat[:, b, :], o[:, :]).then_inc(S["act_ev"], 1)
                            ac.drain()
                            if b >= 2:
                                ac.wait_ge(S["ss_mm"], b - 1)
                            nc.scalar.activation(sq[:, b % 2, :], lat[:, b, :], ACT.Square).then_inc(S["sq_ready"], 1)
                            if b == KVT:
                                sqrt(1)
                            if b == B_KPE - 1:
                                sqrt(2)
                        elif b < B_V:
                            nc.scalar.copy(kh[0:NOPE, b - B_K, :], o[0:NOPE, :]).then_inc(S["act_ev"], 1)
                        elif b < B_Q:
                            nc.scalar.copy(v[:, b - B_V, :], o[:, :]).then_inc(S["act_ev"], 1)
                        else:
                            nc.scalar.copy(qh[0:NOPE, b - B_Q, :], o[0:NOPE, :]).then_inc(S["act_ev"], 1)

                @block.vector
                def _(ve):
                    def mean_square(n, width):
                        ve.wait_ge(S["ss_mm"], KVT if n == 0 else B_KPE)
                        nc.vector.tensor_scalar(rms, bank[3 + n][:, :], 1.0 / width, EPS, ALU.mult,
                                                ALU.add).then_inc(S["rt_ready"], 1)

                    def scale_latents(n, first, count, gain):
                        ve.wait_ge(S["sqrt_ready"], n + 1)
                        nc.vector.reciprocal(rms, rms)
                        ve.drain()
                        for j in range(count):
                            nc.vector.scalar_tensor_tensor(out=lat[:, first + j, :], in0=lat[:, first + j, :],
                                                           scalar=cols[:, gain + j:gain + j + 1], in1=rms,
                                                           op0=ALU.mult, op1=ALU.mult)
                        ve.drain().then_inc(S["latn"], 1)

                    def rotate(o, dst):
                        nc.vector.tensor_tensor(rtmp[64:96, :], o[96:128, :], rope[96:128, :], ALU.mult)
                        nc.vector.tensor_tensor(dst, o[64:96, :], rope[64:96, :], ALU.mult)
                        ve.drain().then_inc(S["dve_ev"], 1)
                        nc.vector.tensor_tensor(dst, dst, rtmp[64:96, :], ALU.add)
                        ve.drain()

                    def ada_steps(first, last):
                        for i in range(first, last):
                            ada_step_dve(ve, ada_early, i, 0, ADA_LATE)

                    ada_steps(0, 2)
                    ve.wait_ge(S["cols_loaded"], 16)
                    mean_square(0, KV_LORA)
                    scale_latents(0, 0, KVT, C_KVG)
                    ada_steps(2, 8)
                    ve.wait_ge(S["mm_ready"], B_KPE + 1)
                    rotate(bank[B_KPE % 3], kpe[64:96, :])
                    ve.sem_inc(S["kpe_ready"], 1)
                    mean_square(1, Q_LORA)
                    scale_latents(1, KVT, QT, C_QG)
                    ada_steps(8, 12)
                    for h in range(HEADS):
                        ve.wait_ge(S["mm_ready"], B_Q + h + 1)
                        rotate(bank[(B_Q + h) % 3], qh[64:96, h, :])
                        if h % 2:
                            ada_steps(12 + h // 2, 13 + h // 2)
                    ada_steps(ADA_LATE, ADA_LATE + 1)

                @block.gpsimd
                def _(po):
                    po.wait_ge(S["kpe_ready"], 1)
                    for h in range(HEADS):
                        nc.gpsimd.tensor_copy(kh[64:96, h, :], kpe[64:96, :])

            ITEMS = HEADS * TILES
            V_ITEM = D_V * KT // 3
            AE_ITEM = V_ITEM + TILES + 1
            with nc.Block() as block:
                @block.sync
                def _(sp):
                    load_weights(sp, l, IT_IF + W_SLOTS, IT_MV + W_SLOTS)

                @block.gpsimd
                def _(po):
                    nc.gpsimd.memset(up[:, :, 0:PAD], 0.0)
                    nc.gpsimd.memset(v1[:, :, :, MD:VW], 1.0)
                    po.drain().then_inc(S["pads"], 1)

                @block.tensor
                def _(pe):
                    def score(i):
                        h, t = divmod(i, TILES)
                        n = (t + 1) * P
                        if i >= 2:
                            pe.wait_ge(S["p_ready"], i - 1)
                        nc.tensor.matmul(bank[i % 2][:, 0:n], qh[0:QK, h, t * P:(t + 1) * P], kh[0:QK, h, 0:n],
                                         start=True, stop=True).then_inc(S["sc_ready"], 1)

                    def turn(i):
                        t = i % TILES
                        pe.wait_ge(S["p_ready"], i + 1)
                        if i >= 2:
                            pe.wait_ge(S["pt_ev"], i - 1)
                        for j in range(t + 1):
                            ins = nc.tensor.transpose(bank[2 + i % 2][:, j * P:(j + 1) * P],
                                                      prob[:, i % 3, j * P:(j + 1) * P], ident)
                        ins.then_inc(S["pt_ready"], 1)

                    def values(i):
                        h, t = divmod(i, TILES)
                        pe.wait_ge(S["pt_ev"], i + 1)
                        if i >= 2:
                            pe.wait_ge(S["o_ev"], i - 1)
                        for j in range(t + 1):
                            ins = nc.tensor.matmul(bank[4 + i % 2][:, 0:VDIM], probT[:, i % 2, j * P:(j + 1) * P],
                                                   v[:, j, h * VDIM:(h + 1) * VDIM], start=j == 0, stop=j == t)
                        ins.then_inc(S["o_ready"], 1)

                    def project(n):
                        e, k = divmod(n, KT)
                        m = 64 if e == 0 else P
                        if k == 0:
                            w_here(pe, IT_IF + e)
                            if e >= 2:
                                pe.wait_ge(S["d_ev"], e - 1)
                        w = w_ring[:, (IT_IF + e) % W_SLOTS, :]
                        ins = nc.tensor.matmul(bank[6 + e % 2][0:m, :], w[:, k * P:k * P + m], hT[:, k, :],
                                               start=k == 0, stop=k == KT - 1)
                        if k == KT - 1:
                            ins.then_inc(S["d_ready"], 1)

                    def project_v(t):
                        e = D_V + t
                        if t == 0:
                            w_here(pe, IT_MV)
                        pe.wait_ge(S["d_ev"], e - 1)
                        w = w_ring[:, IT_MV % W_SLOTS, :]
                        for h in range(MH):
                            ins = nc.tensor.matmul(bank[6 + e % 2][:, h * MD:(h + 1) * MD],
                                                   up[:, h, PAD + t * P:PAD + (t + 1) * P],
                                                   w[:, h * MD:(h + 1) * MD], start=True, stop=True)
                        ins.then_inc(S["d_ready"], 1)

                    def gate_columns():
                        pe.wait_ge(S["d_ev"], D_HEAD - 1)
                        for r, (row, ready) in enumerate(((row_a, "rows_a"), (row_e, "rows_e"))):
                            pe.wait_ge(S[ready], 1)
                            for t in range(TILES):
                                c = (r * TILES + t) * MH
                                ins = nc.tensor.transpose(bank[7][:, c:c + MH], row[:, t * P:(t + 1) * P],
                                                          ident[0:MH, 0:MH])
                        ins.then_inc(S["ae_ready"], 1)

                    def turn_heads(f):
                        pe.wait_ge(S["o_ev"], 2 * TILES * (f + 1))
                        if f == 0:
                            pe.wait_ge(S["d_ev"], D_HEAD)
                        elif f == 1:
                            pe.wait_ge(S["ae_ev"], 1)
                        else:
                            pe.wait_ge(S["at_ev"], f - 1)
                        for t in range(TILES):
                            ins = nc.tensor.transpose(bank[6 + f % 2][:, t * P:(t + 1) * P],
                                                      att[:, t, f * P:(f + 1) * P], ident)
                        ins.then_inc(S["at_ready"], 1)

                    for i in range(ITEMS + 2):
                        if i < ITEMS:
                            score(i)
                        for n in range(3 * i, min(3 * i + 3, D_V * KT)):
                            project(n)
                        if V_ITEM <= i < V_ITEM + TILES:
                            project_v(i - V_ITEM)
                        if i == AE_ITEM:
                            gate_columns()
                        if 1 <= i <= ITEMS:
                            turn(i - 1)
                        if i >= 2:
                            values(i - 2)
                        if AE_ITEM < i <= AE_ITEM + 3:
                            turn_heads(i - AE_ITEM - 1)
                    turn_heads(3)

                @block.vector
                def _(ve):
                    def maximum(i):
                        t = i % TILES
                        n = (t + 1) * P
                        s = bank[i % 2]
                        ve.wait_ge(S["sc_ready"], i + 1)
                        nc.vector.tensor_tensor(s[:, t * P:n], s[:, t * P:n], mask_q, ALU.add)
                        ve.drain()
                        nc.vector.tensor_reduce(scol[:, 0, i:i + 1], s[:, 0:n], AX.X, ALU.max)
                        ve.drain()
                        nc.vector.tensor_scalar(scol[:, 1, i:i + 1], scol[:, 0, i:i + 1], -SM_SCALE, None,
                                                ALU.mult).then_inc(S["nm_ready"], 1)

                    def normalise(i):
                        h, t = divmod(i, TILES)
                        ve.wait_ge(S["o_ready"], i + 1)
                        nc.vector.reciprocal(scol[:, 3, i:i + 1], scol[:, 2, i:i + 1])
                        ve.drain()
                        nc.vector.tensor_scalar(att[:, t, h * VDIM:(h + 1) * VDIM], bank[4 + i % 2][:, 0:VDIM],
                                                scol[:, 3, i:i + 1], None, ALU.mult).then_inc(S["o_ev"], 1)

                    def gate_rows():
                        nc.vector.memset(row_m, 1.0)
                        ve.wait_ge(S["lnf"], 1)
                        nc.vector.scalar_tensor_tensor(out=row_f, in0=row_f, scalar=0.0, in1=row_ln,
                                                       op0=ALU.min, op1=ALU.subtract)
                        ve.drain()
                        nc.vector.tensor_tensor_scan(row_cum, row_m, row_f, 0.0, ALU.mult, ALU.add)
                        ve.drain()
                        nc.vector.tensor_tensor(row_a, row_i, row_cum, ALU.subtract).then_inc(S["rows_a"], 1)
                        ve.drain()
                        nc.vector.tensor_tensor_scan(row_m, row_a, row_a, 0.0, ALU.max, ALU.max)
                        ve.drain()
                        nc.vector.tensor_scalar(row_nm, row_m, -1.0, None, ALU.mult)
                        nc.vector.tensor_tensor(row_s, row_cum, row_m, ALU.add)
                        ve.drain().then_inc(S["rows_s"], 1)

                    def conv(h):
                        ve.wait_ge(S["d_ev"], h + 2)
                        ve.wait_ge(S["pads"], 1)
                        c = C_CW + h * CONV
                        nc.vector.tensor_scalar(ca[:, h, :], up[:, h, PAD:UP], cols[:, c + PAD:c + PAD + 1],
                                                cols[:, C_CB + h:C_CB + h + 1], ALU.mult, ALU.add)
                        for j in range(PAD):
                            ve.drain()
                            nc.vector.scalar_tensor_tensor(out=ca[:, h, :], in0=up[:, h, j:j + SEQ],
                                                           scalar=cols[:, c + j:c + j + 1], in1=ca[:, h, :],
                                                           op0=ALU.mult, op1=ALU.add)
                        ve.drain().then_inc(S["conv_ready"], 1)

                    for i in range(ITEMS + 3):
                        if i < ITEMS:
                            maximum(i)
                        if i >= 3:
                            normalise(i - 3)
                        if i == 6:
                            gate_rows()
                        if i in (9, 12, 15, 18):
                            conv(i // 3 - 3)
                        if i == AE_ITEM + 1:
                            ve.wait_ge(S["ae_ready"], 1)
                            nc.vector.tensor_copy(ae[:, :, :, :].rearrange("p r t h -> p (r t h)"),
                                                  bank[7][:, 0:32]).then_inc(S["ae_ev"], 1)

                @block.scalar
                def _(ac):
                    def keep_heads(f):
                        ac.wait_ge(S["at_ready"], f + 1)
                        nc.scalar.copy(attT[:, f, :], bank[6 + f % 2][:, :]).then_inc(S["at_ev"], 1)

                    for i in range(ITEMS + 1):
                        if i < ITEMS:
                            n = (i % TILES + 1) * P
                            ac.wait_ge(S["nm_ready"], i + 1)
                            if i >= 3:
                                ac.wait_ge(S["pt_ready"], i - 2)
                            nc.scalar.activation(prob[:, i % 3, 0:n], bank[i % 2][:, 0:n], ACT.Exp,
                                                 bias=scol[:, 1, i:i + 1], scale=SM_SCALE,
                                                 accum_out=scol[:, 2, i:i + 1])
                            ac.drain().then_inc(S["p_ready"], 1)
                        if i >= 1:
                            n = ((i - 1) % TILES + 1) * P
                            ac.wait_ge(S["pt_ready"], i)
                            if i >= 3:
                                ac.wait_ge(S["o_ready"], i - 2)
                            nc.scalar.copy(probT[:, (i - 1) % 2, 0:n], bank[2 + (i - 1) % 2][:, 0:n]
                                           ).then_inc(S["pt_ev"], 1)
                        for e in [e for e in range(D_V) if (KT * e + KT - 1) // 3 + 1 == i]:
                            ac.wait_ge(S["d_ready"], e + 1)
                            o = bank[6 + e % 2]
                            if e == 0:
                                nc.scalar.activation(row_i, o[0:MH, :], ACT.Identity, bias=cols[0:MH, C_BI:C_BI + 1])
                                nc.scalar.activation(row_f, o[32:32 + MH, :], ACT.Identity,
                                                     bias=cols[0:MH, C_BF:C_BF + 1])
                                ac.drain().then_inc(S["d_ev"], 1)
                            elif e <= MH:
                                nc.scalar.copy(up[:, e - 1, PAD:UP], o[:, :]).then_inc(S["d_ev"], 1)
                            else:
                                nc.scalar.copy(so[:, e - 1 - MH, :], o[:, :]).then_inc(S["d_ev"], 1)
                        if i == 4:
                            nc.scalar.activation(row_t, row_f, ACT.Abs)
                            ac.drain()
                            nc.scalar.activation(row_t, row_t, ACT.Exp, scale=-1.0)
                            ac.drain()
                            nc.scalar.activation(row_ln, row_t, ACT.Ln, bias=1.0).then_inc(S["lnf"], 1)
                        if i == 9:
                            ac.wait_ge(S["rows_s"], 1)
                            nc.scalar.activation(row_e, row_s, ACT.Exp, scale=-1.0).then_inc(S["rows_e"], 1)
                        if V_ITEM < i <= V_ITEM + TILES:
                            t = i - V_ITEM - 1
                            ac.wait_ge(S["d_ready"], D_V + t + 1)
                            nc.scalar.copy(v1[:, t, :, 0:MD], bank[6 + (D_V + t) % 2][:, :]
                                           .rearrange("p (h e) -> p h e", h=MH)).then_inc(S["d_ev"], 1)
                        if i > AE_ITEM + 1:
                            keep_heads(i - AE_ITEM - 2)
                    for h in range(MH):
                        ac.wait_ge(S["conv_ready"], h + 1)
                        nc.scalar.activation(ca[:, h, :], ca[:, h, :], ACT.Silu)
                    for f in range(ITEMS - AE_ITEM - 1, 4):
                        keep_heads(f)
                    for h in range(MH):
                        nc.scalar.activation(so[:, h, :], so[:, h, :], ACT.Sigmoid)

            with nc.Block() as block:
                @block.sync
                def _(sp):
                    load_weights(sp, l, IT_MV + W_SLOTS, IT_MERGE + W_SLOTS)
                    for i in range(ADA_SLOTS):
                        load_ada(sp, ada_late, (l + 1) % DEPTH, ADA_LATE + i)

                def turn_back(pe, h):
                    pe.wait_ge(S["hn_ready"], h + 1)
                    if h >= 1:
                        pe.wait_ge(S["y_ev"], h)
                    for t in range(TILES):
                        ins = nc.tensor.transpose(bank[2][:, t * P:(t + 1) * P], hn[:, h % 2, t * P:(t + 1) * P],
                                                  ident)
                    ins.then_inc(S["hnT_ready"], 1)

                def second_gate(pe, j):
                    w = w_here(pe, IT_MERGE + GATE_AT[j])
                    if j >= 2:
                        pe.wait_ge(S["e_act"], 2 * (j - 1))
                    else:
                        pe.wait_ge(S["d_ev"], D_N - 1 + j)
                    for k in range(KT):
                        ins = nc.tensor.matmul(bank[(D_N + j) % 2][:, :], w[:, k * P:(k + 1) * P], hT[:, k, :],
                                               start=k == 0, stop=k == KT - 1)
                    ins.then_inc(S["e_ready"], 1)

                @block.tensor
                def _(pe):
                    def free(e):
                        pe.wait_ge(S["d_ev"], e - 1)
                        return bank[e % 2]

                    def queries_keys(h):
                        w = w_mqk
                        for q in range(2):
                            o = free(D_HEAD + h * D_PER + q)
                            nc.tensor.matmul(o[:, :], w[:, (q * MH + h) * MD:(q * MH + h + 1) * MD], ca[:, h, :],
                                             start=True, stop=True).then_inc(S["d_ready"], 1)

                    def merge_gate(h, quarter):
                        for n in range(quarter * D_GA * KT // 4, (quarter + 1) * D_GA * KT // 4):
                            j, k = divmod(n, KT)
                            if k == 0:
                                w_here(pe, IT_GA + h * D_GA + j)
                                free(D_HEAD + h * D_PER + 2 + j)
                            o = bank[(D_HEAD + h * D_PER + 2 + j) % 2]
                            w = w_ring[:, (IT_GA + h * D_GA + j) % W_SLOTS, :]
                            ins = nc.tensor.matmul(o[:, :], w[:, k * P:(k + 1) * P], hT[:, k, :], start=k == 0,
                                                   stop=k == KT - 1)
                            if k == KT - 1:
                                ins.then_inc(S["d_ready"], 1)

                    pe.wait_ge(S["mqk_loaded"], 16)
                    queries_keys(0)
                    for h in range(MH):
                        if h >= 1:
                            pe.wait_ge(S["nmb_ev"], h)
                        nc.tensor.matmul(bank[3][:, :], sel[0:MH, h, :], row_nm, start=True,
                                         stop=True).then_inc(S["nmb_ready"], 1)
                        pe.wait_ge(S["d_ev"], D_HEAD + h * D_PER + 2)
                        for s in range(TILES):
                            g = h * TILES + s
                            if g >= 2:
                                pe.wait_ge(S["pm_ready"], g - 1)
                            nc.tensor.matmul(bank[4 + g % 2][:, 0:SEQ - s * P], mk[:, h % 2, s * P:(s + 1) * P],
                                             mq[:, h % 2, s * P:SEQ], start=True, stop=True
                                             ).then_inc(S["s_ready"], 1)
                            merge_gate(h, s)
                        if h + 1 < MH:
                            queries_keys(h + 1)
                        else:
                            second_gate(pe, 0)
                        for half in range(2):
                            pe.wait_ge(S["pm_ready"], h * TILES + 2 * half + 2)
                            if h >= 1:
                                pe.wait_ge(S["n_ev"], 2 * (h - 1) + half + 1)
                            for t in (2 * half, 2 * half + 1):
                                for s in range(t + 1):
                                    o = P_OFF[s] + (t - s) * P
                                    ins = nc.tensor.matmul(bank[6 + half][:, (t % 2) * 256:(t % 2) * 256 + VW],
                                                           pm[:, h % 2, o:o + P], v1[:, s, h, :], start=s == 0,
                                                           stop=s == t)
                            ins.then_inc(S["n_ready"], 1)
                        if h >= 1:
                            turn_back(pe, h - 1)
                        if h == MH - 1:
                            second_gate(pe, 1)
                    turn_back(pe, MH - 1)

                @block.scalar
                def _(ac):
                    def taken(e):
                        ac.wait_ge(S["d_ready"], e + 1)
                        return bank[e % 2]

                    def queries_keys(h):
                        for q, (dst, scale) in enumerate(((mq, 1.0), (mk, K_SCALE))):
                            o = taken(D_HEAD + h * D_PER + q)
                            nc.scalar.mul(dst[:, h % 2, :], o[:, :], scale).then_inc(S["d_ev"], 1)

                    queries_keys(0)
                    for h in range(MH):
                        ac.wait_ge(S["nmb_ready"], h + 1)
                        nc.scalar.copy(nmb[:, h % 2, :], bank[3][:, :])
                        ac.drain().then_inc(S["nmb_ev"], 1)
                        ac.wait_ge(S["nmd_ready"], h + 1)
                        for s in range(TILES):
                            g = h * TILES + s
                            if g >= 2:
                                ac.wait_ge(S["pm_ready"], g - 1)
                            a_s = ae[:, 0, s, h:h + 1]
                            ins = nc.scalar.activation(dw[:, g % 2, 0:P], nmd[:, h % 2, s * P:(s + 1) * P], ACT.Exp,
                                                       bias=a_s)
                            if s + 1 < TILES:
                                ins = nc.scalar.activation(dw[:, g % 2, P:SEQ - s * P], nmb[:, h % 2, (s + 1) * P:SEQ],
                                                           ACT.Exp, bias=a_s)
                            ac.drain().then_inc(S["dw_ready"], 1)
                        for j in range(D_GA):
                            o = taken(D_HEAD + h * D_PER + 2 + j)
                            nc.scalar.copy(ga_raw[h * D_GA + j], o[:, :]).then_inc(S["d_ev"], 1)
                        if h + 1 < MH:
                            queries_keys(h + 1)
                        ac.wait_ge(S["var_ready"], h + 1)
                        nc.scalar.activation(mcol[:, 52:56], mcol[:, 48:52], ACT.Sqrt).then_inc(S["dev_ready"], 1)

                @block.vector
                def _(ve):
                    def weigh(h):
                        ve.wait_ge(S["nmb_ev"], h + 1)
                        nc.vector.tensor_tensor(nmd[:, h % 2, :].rearrange("p (s t) -> p s t", s=TILES),
                                                nmb[:, h % 2, :].rearrange("p (s t) -> p s t", s=TILES),
                                                mask_t.unsqueeze(1).to_broadcast([P, TILES, P]),
                                                ALU.add).then_inc(S["nmd_ready"], 1)
                        for s in range(TILES):
                            g, n = h * TILES + s, SEQ - s * P
                            ve.wait_ge(S["s_ready"], g + 1)
                            ve.wait_ge(S["dw_ready"], g + 1)
                            nc.vector.tensor_tensor(pm[:, h % 2, P_OFF[s]:P_OFF[s] + n], bank[4 + g % 2][:, 0:n],
                                                    dw[:, g % 2, 0:n], ALU.mult).then_inc(S["pm_ready"], 1)

                    def head_norm(h):
                        den, peak, inv = mcol[:, 0:4], mcol[:, 4:8], mcol[:, 8:12]
                        st6 = mcol[:, 12:36].rearrange("p (t c) -> p t c", t=TILES)
                        mv = mcol[:, 36:44].rearrange("p (t c) -> p t c", t=TILES)
                        for half in range(2):
                            ve.wait_ge(S["n_ready"], 2 * h + half + 1)
                            num = bank[6 + half][:, :].rearrange("p (t e) -> p t e", t=2)
                            nc.vector.tensor_copy(den[:, 2 * half:2 * half + 2], num[:, :, MD])
                        ve.drain()
                        nc.vector.scalar_tensor_tensor(out=peak, in0=den, scalar=-1.0, in1=den, op0=ALU.mult,
                                                       op1=ALU.max)
                        ve.drain()
                        nc.vector.tensor_tensor(peak, peak, ae[:, 1, :, h], ALU.max)
                        ve.drain()
                        nc.vector.reciprocal(inv, peak)
                        ve.drain()
                        hd = hn[:, h % 2, :].rearrange("p (t e) -> p t e", t=TILES)
                        for t in range(TILES):
                            ins = nc.vector.tensor_scalar(hd[:, t, :], bank[6 + t // 2][:, (t % 2) * 256:(t % 2) * 256 + MD],
                                                          inv[:, t:t + 1], None, ALU.mult)
                            if t % 2:
                                ins.then_inc(S["n_ev"], 1)
                        ve.drain()
                        for t in range(TILES):
                            nc.vector.bn_stats(st6[:, t, :], hd[:, t, :])
                        ve.drain()
                        for t in range(TILES):
                            nc.vector.bn_aggr(mv[:, t, :], st6[:, t, :])
                        ve.drain()
                        nc.vector.tensor_scalar(mcol[:, 48:52], mv[:, :, 1], EPS, None,
                                                ALU.add).then_inc(S["var_ready"], 1)
                        ve.wait_ge(S["dev_ready"], h + 1)
                        nc.vector.reciprocal(mcol[:, 56:60], mcol[:, 52:56])
                        ve.drain()
                        for t in range(TILES):
                            nc.vector.tensor_scalar(hd[:, t, :], hd[:, t, :], mv[:, t, 0:1], mcol[:, 56 + t:57 + t],
                                                    ALU.subtract, ALU.mult)
                        ve.drain().then_inc(S["hn_ready"], 1)

                    def gated(h):
                        nc.vector.tensor_scalar(ctmp, ca[:, h, :], cols[:, C_SK + h:C_SK + h + 1], None, ALU.mult)
                        ve.drain()
                        ve.wait_ge(S["hnT_ready"], h + 1)
                        nc.vector.scalar_tensor_tensor(out=ctmp, in0=bank[2][:, :], scalar=cols[:, C_MG + h:C_MG + h + 1],
                                                       in1=ctmp, op0=ALU.mult, op1=ALU.add).then_inc(S["y_ev"], 1)
                        ve.drain()
                        nc.vector.tensor_tensor(ymT[:, h, :], ctmp, so[:, h, :], ALU.mult)
                        ve.drain()

                    for h in range(MH):
                        weigh(h)
                        head_norm(h)
                        if h >= 1:
                            gated(h - 1)
                    gated(MH - 1)

            def wait_alone(eng, s, value):
                eng.wait_ge(s, value)
                eng.sem_inc(S["passed"], 1)

            HEAD_PAIRS = PH // 2
            QP_SLOTS = 2
            SB = TILES * PH // 2
            SCORE_ORDER = [t * HEAD_PAIRS + hp for half in range(2) for t in range(TILES)
                           for hp in (2 * half, 2 * half + 1)]
            with nc.Block() as block:
                @block.sync
                def _(sp):
                    after = (l + 1) % DEPTH
                    load_ada_bias(sp, after, 0, 2)
                    load_gain(sp, ada_late, after, 0)
                    for n in range(2 * KT):
                        load_weights(sp, l, IT_MERGE + W_SLOTS + n, IT_MERGE + W_SLOTS + n + 1)
                        i = ADA_LATE + ADA_SLOTS + n // 2
                        if n % 2 and i < ADA_STEPS:
                            load_ada(sp, ada_late, after, i)
                    load_weights(sp, l, IT_MERGE + W_SLOTS + 2 * KT, IT_PQ + W_SLOTS)
                    load_weights(sp, l, IT_PQ + W_SLOTS, N_ITEMS)

                @block.gpsimd
                def _(po):
                    with po.Fori(0, TILES) as t:
                        with po.Fori(0, HEAD_PAIRS) as i:
                            for par in range(2):
                                n = t * PH + i * 2 + par
                                for s in range(TOPK):
                                    if s == 0:
                                        wait_alone(po, S["idx_ready"], n + 1)
                                    wait_alone(po, S["slot_free"], n * TOPK + (s + 1))
                                    po.indirect_dma_start(ring[:, s % RING, :], None, experts_in,
                                                          bass.IndirectOffsetOnAxis(ap=idx[:, par, s:s + 1], axis=0)
                                                          ).then_inc(gathered[s % RING], 16)

                @block.scalar
                def _(ac):
                    def keep_scores(half):
                        for m in range(half * SB // 2, (half + 1) * SB // 2, 2):
                            i = SCORE_ORDER[m]
                            ac.wait_ge(S["s2_ready"], m + 1)
                            nc.scalar.copy(scores[:, i * 512:(i + 1) * 512], bank[m % 4][:, :]).then_inc(S["s2_act"], 1)

                    def stage_scores(n, par):
                        nc.scalar.copy(stage[:, par, :, :].rearrange("p q n -> p (q n)"),
                                       scores[:, bass.ds(n * (2 * NKEYS), 2 * NKEYS)]).then_inc(S["stage_ready"], 1)

                    def exponentials(n):
                        ac.wait_ge(S["best_ready"], n + 1)
                        nc.scalar.activation(gexp, best, ACT.Exp, bias=gs[:, 0:1], accum_out=gs[:, 1:2])
                        ac.drain().then_inc(S["exp_ready"], 1)

                    for j in range(KT):
                        if j >= 2:
                            ac.wait_ge(S["e_dve"], j - 1)
                        nc.scalar.activation(sg[:, j % 2, 0, :], ga_raw[j], ACT.Sigmoid).then_inc(S["e_act"], 1)
                        ac.wait_ge(S["e_ready"], GATE_AT[j] + 1)
                        nc.scalar.activation(sg[:, j % 2, 1, :], bank[(D_N + j) % 2][:, :], ACT.Sigmoid
                                             ).then_inc(S["e_act"], 1)
                    norm_act_sums(ac, 1, at(16, D))
                    norm_act_copies(ac, 1)
                    for h in range(PH):
                        if h == PH // 2:
                            keep_scores(0)
                            ac.drain()
                            stage_scores(0, 0)
                            stage_scores(1, 1)
                        if h == PH - 2:
                            exponentials(0)
                        ac.wait_ge(S["q_ready"], h + 1)
                        nc.scalar.copy(qp[:, h, :], bank[4 + h % 2][:, :]).then_inc(S["q_ev"], 1)
                    keep_scores(1)
                    ac.drain()
                    ac.wait_ge(S["s2_dve"], SB // 2)
                    with ac.Fori(0, TILES) as t:
                        nc.scalar.copy(h_now, h_tok[:, bass.ds(t, 1), :].rearrange("p a d -> p (a d)")
                                       ).then_inc(S["h_now_ready"], 1)
                        with ac.Fori(0, HEAD_PAIRS) as i:
                            for par in range(2):
                                n = t * PH + i * 2 + par
                                stage_scores((n + 2) % UNITS, par)
                                for g in range(TOPK // GROUP):
                                    if g == 2:
                                        exponentials(n + 1)
                                    ac.wait_ge(S["dots_ready"], n * (TOPK // GROUP) + (g + 1))
                                    c = slice(g * GROUP, (g + 1) * GROUP)
                                    nc.scalar.activation(gel[:, par, c], dots[:, par, c],
                                                         ACT.Gelu).then_inc(S["gelu_ready"], 1)

                @block.vector
                def _(ve):
                    def top8(vals, poss, src, scratch):
                        nc.vector.max(vals, src)
                        ve.drain()
                        nc.vector.max_index(poss, vals, src)
                        if scratch is not None:
                            nc.vector.match_replace(scratch, vals, src, FLOOR)
                        ve.drain()

                    def route(part, n, par):
                        if part < 4:
                            q, half = divmod(part, 2)
                            if part == 0:
                                wait_alone(ve, S["stage_ready"], n + 1)
                            c = slice(8 * half, 8 * half + 8)
                            top8(top[:, q, c], top_i[:, q, c], rest if half else stage[:, par, q, :],
                                 None if half else rest)
                        elif part == 4:
                            a = top[:, 0, :].unsqueeze(2).to_broadcast([P, TOPK, TOPK])
                            b = top[:, 1, :].unsqueeze(1).to_broadcast([P, TOPK, TOPK])
                            nc.vector.tensor_tensor(cand[:, 0, :].rearrange("p (a b) -> p a b", a=TOPK), a, b, ALU.add)
                            nc.vector.tensor_copy(top_f[:, :, :], top_i[:, :, :])
                            ve.drain()
                            top8(best[:, 0:8], pos[:, 0:8], cand[:, 0, :], cand[:, 1, :])
                        elif part == 5:
                            top8(best[:, 8:16], pos[:, 8:16], cand[:, 1, :], None)
                            nc.vector.tensor_scalar(gs[:, 0:1], best[:, 0:1], -1.0, None, ALU.mult)
                            ve.drain().then_inc(S["best_ready"], 1)
                        elif part == 6:
                            nc.vector.tensor_scalar(posab[:, 0, :], pos, 4, None, ALU.logical_shift_right)
                            nc.vector.tensor_scalar(posab[:, 1, :], pos, 15, None, ALU.bitwise_and)
                            ve.drain()
                            nc.vector.tensor_copy(posab_f[:, :, :], posab[:, :, :])
                            ve.drain()
                            hot3 = hot.rearrange("p (k j) -> p k j", j=TOPK)
                            nc.vector.tensor_tensor(hot3, posab_f[:, :, :].rearrange("p q k -> p (q k)").unsqueeze(2)
                                                    .to_broadcast([P, 2 * TOPK, TOPK]),
                                                    iota.unsqueeze(1).to_broadcast([P, 2 * TOPK, TOPK]), ALU.is_equal)
                            ve.drain()
                            hot4 = hot.rearrange("p (q k j) -> p q k j", q=2, k=TOPK)
                            nc.vector.tensor_tensor(hot4, hot4, top_f[:, :, :].unsqueeze(2)
                                                    .to_broadcast([P, 2, TOPK, TOPK]), ALU.mult)
                            ve.drain()
                        else:
                            nc.vector.tensor_reduce(pick, hot.rearrange("p (k j) -> p k j", j=TOPK), AX.X, ALU.add)
                            ve.drain()
                            nc.vector.scalar_tensor_tensor(out=flat_i, in0=pick[:, 0:TOPK], scalar=float(NKEYS),
                                                           in1=pick[:, TOPK:2 * TOPK], op0=ALU.mult, op1=ALU.add)
                            ve.drain()
                            nc.vector.tensor_scalar(idx[:, par, :], flat_i, layer_row[:, 0:1], None, ALU.add)
                            ve.drain().then_inc(S["idx_ready"], 1)
                            ve.wait_ge(S["exp_ready"], n + 1)
                            nc.vector.reciprocal(gs[:, 2:3], gs[:, 1:2])
                            ve.drain()
                            nc.vector.tensor_scalar(gate[:, par, :], gexp, gs[:, 2:3], None, ALU.mult)
                            ve.drain()

                    def keep_scores(half):
                        for m in range(half * SB // 2 + 1, (half + 1) * SB // 2, 2):
                            i = SCORE_ORDER[m]
                            ve.wait_ge(S["s2_ready"], m + 1)
                            nc.vector.tensor_copy(scores[:, i * 512:(i + 1) * 512], bank[m % 4][:, :]
                                                  ).then_inc(S["s2_dve"], 1)

                    for j in range(KT):
                        ada_step_dve(ve, ada_late, ADA_LATE + j, ADA_LATE, ADA_STEPS)
                        ve.wait_ge(S["e_ready"], BRANCH_AT[j] + 1)
                        ve.wait_ge(S["e_act"], 2 * j + 2)
                        for g in range(2):
                            nc.vector.tensor_tensor(mt[:, j % 2, g, :], bank[2 + 2 * (j % 2) + g][:, :], sg[:, j % 2, g, :],
                                                    ALU.mult)
                        ve.drain()
                        nc.vector.tensor_tensor(mgT[:, j, :], mt[:, j % 2, 0, :], mt[:, j % 2, 1, :],
                                                ALU.add).then_inc(S["e_dve"], 1)
                    ada_step_dve(ve, ada_late, ADA_STEPS, ADA_LATE, ADA_STEPS)
                    for t in range(TILES):
                        for c in range(2):
                            b = 2 * t + c
                            ve.wait_ge(S["wo_ready"], b + 1)
                            m = mt[:, b % 2, 0, :]
                            nc.vector.tensor_tensor(m, bank[b][:, :], ada[:, 2 * D + c * 512:2 * D + (c + 1) * 512],
                                                    ALU.mult)
                            ve.drain()
                            xs = x[:, t, c * 512:(c + 1) * 512]
                            nc.vector.tensor_tensor(xs, xs, m, ALU.add)
                        ve.drain().then_inc(S["x_ready"], 1)
                    norm_dve(ve, 1, ada[:, 3 * D:4 * D], ada[:, 4 * D:5 * D])
                    keep_scores(0)
                    for part in range(ROUTE_PARTS):
                        route(part, 0, 0)
                    for part in range(ROUTE_PARTS // 2):
                        route(part, 1, 1)
                    keep_scores(1)
                    ve.sem_inc(S["y_free"], 1)
                    with ve.Fori(0, TILES) as t:
                        wait_alone(ve, S["h_now_ready"], t + 1)
                        with ve.Fori(0, HEAD_PAIRS) as i:
                            for par in range(2):
                                n = t * PH + i * 2 + par
                                for g in range(TOPK // GROUP):
                                    for s in range(g * GROUP, (g + 1) * GROUP):
                                        ve.wait_ge(gathered[s % RING],
                                                l * (UNITS * 32) + n * 32 + 16 * (s // RING + 1))
                                        u = ring[:, s % RING, 0:D]
                                        nc.vector.tensor_tensor_reduce(u, u, h_now, 1.0, 0.0, ALU.mult, ALU.add,
                                                                       dots[:, par, s:s + 1])
                                    ve.drain().then_inc(S["dots_ready"], 1)
                                    if g < ROUTE_PARTS // 2:
                                        route(g + ROUTE_PARTS // 2, n + 1, 1 - par)
                                    else:
                                        route(g - ROUTE_PARTS // 2, n + 2, par)
                                    ve.wait_ge(S["gelu_ready"], n * (TOPK // GROUP) + (g + 1))
                                    for s in range(g * GROUP, (g + 1) * GROUP):
                                        ve.wait_ge(S["slot_free"], n * TOPK + (s + 1))
                                        nc.vector.tensor_scalar(diag[:, s % 8, :], ident, gel[:, par, s:s + 1],
                                                                gate[:, par, s:s + 1], ALU.mult,
                                                                ALU.mult).then_inc(S["diag_ready"], 1)
                        ve.wait_ge(S["y_done"], t + 1)
                        for c in range(2):
                            nc.vector.tensor_tensor(ytmp[:, c * 512:(c + 1) * 512], bank[c][:, :],
                                                    ada[:, 5 * D + c * 512:5 * D + (c + 1) * 512], ALU.mult)
                        ve.drain().then_inc(S["y_free"], 1)
                        xt = x[:, bass.ds(t, 1), :].rearrange("p a d -> p (a d)")
                        nc.vector.tensor_tensor(xt, xt, ytmp, ALU.add)
                        ve.drain()
                    nc.vector.tensor_scalar(layer_row[:, :], layer_row[:, :], float(EXPERTS), None, ALU.add)

                @block.tensor
                def _(pe):
                    for j in range(KT):
                        w = w_here(pe, IT_MERGE + BRANCH_AT[j])
                        if j >= 2:
                            pe.wait_ge(S["e_dve"], j - 1)
                        for g, branch in enumerate((attT, ymT)):
                            for k in range(4):
                                ins = nc.tensor.matmul(bank[2 + 2 * (j % 2) + g][:, :],
                                                       w[:, (4 * g + k) * P:(4 * g + k + 1) * P],
                                                       branch[:, k, :], start=k == 0, stop=k == 3)
                        ins.then_inc(S["e_ready"], 1)
                        if j + 2 < KT:
                            second_gate(pe, j + 2)
                        ada_pe(pe, ada_late, ADA_LATE + j)
                    pe.wait_ge(S["e_act"], 2 * KT)
                    pe.wait_ge(S["e_dve"], KT)
                    pe.wait_ge(S["ada_ev"], ADA_STEPS)
                    for k in range(KT):
                        w = w_here(pe, IT_OUT + k)
                        for t in range(TILES):
                            for c in range(2):
                                ins = nc.tensor.matmul(bank[2 * t + c][:, :], mgT[:, k, t * P:(t + 1) * P],
                                                       w[:, c * 512:(c + 1) * 512], start=k == 0, stop=k == KT - 1)
                                if k == KT - 1:
                                    ins.then_inc(S["wo_ready"], 1)
                        if k < KT - 1:
                            ins.then_inc(S["out_used"], 1)
                    norm_pe(pe, 1)
                    pe.wait_ge(S["tp_ev"], 4 * TILES)
                    for half in range(2):
                        for h in range(half * PH // 2, (half + 1) * PH // 2):
                            w = w_here(pe, IT_PQ + h + half)
                            if h >= 2:
                                pe.wait_ge(S["q_ev"], h - 1)
                            for k in range(KT):
                                ins = nc.tensor.matmul(bank[4 + h % 2][:, :], w[:, k * P:(k + 1) * P], hT[:, k, :],
                                                       start=k == 0, stop=k == KT - 1)
                            ins.then_inc(S["q_ready"], 1)
                        pe.wait_ge(S["q_ev"], (half + 1) * PH // 2)
                        w = w_here(pe, IT_PQ + (half + 1) * PH // 2 + half)
                        for m in range(half * SB // 2, (half + 1) * SB // 2):
                            t, hp = divmod(SCORE_ORDER[m], HEAD_PAIRS)
                            if m >= 4:
                                pe.wait_ge(S["s2_act" if m % 2 == 0 else "s2_dve"], (m - 4) // 2 + 1)
                            for q in range(2):
                                h = 2 * hp + q
                                ins = nc.tensor.matmul(bank[m % 4][:, q * 256:(q + 1) * 256],
                                                       qp[:, h, t * P:(t + 1) * P],
                                                       w[:, (h % 4) * 256:(h % 4 + 1) * 256], start=True, stop=True)
                            ins.then_inc(S["s2_ready"], 1)
                        if half == 0:
                            pe.sem_inc(S["slot_free"], RING - QP_SLOTS)
                    pe.drain().then_inc(S["slot_free"], QP_SLOTS)
                    pe.wait_ge(S["s2_act"], SB // 2)
                    pe.wait_ge(S["s2_dve"], SB // 2)
                    with pe.Fori(0, TILES) as t:
                        pe.wait_ge(S["y_free"], t + 1)
                        for c in range(2):
                            nc.tensor.matmul(bank[c][:, :], zeros[:, :], const[:, 0:512], start=True, stop=False)
                        with pe.Fori(0, HEAD_PAIRS) as i:
                            for par in range(2):
                                n = t * PH + i * 2 + par
                                for s in range(TOPK):
                                    pe.wait_ge(S["diag_ready"], n * TOPK + (s + 1))
                                    for c in range(2):
                                        ins = nc.tensor.matmul(bank[c][:, :], diag[:, s % 8, :],
                                                               ring[:, s % RING, D + c * 512:D + (c + 1) * 512],
                                                               start=False, stop=False)
                                    ins.then_inc(S["slot_free"], 1)
                        for c in range(2):
                            ins = nc.tensor.matmul(bank[c][:, :], zeros[:, :], const[:, 0:512], start=False, stop=True)
                        ins.then_inc(S["y_done"], 1)

            clear_semaphores()

        fg = at(0, D)
        with nc.Block() as block:
            @block.sync
            def _(sp):
                sp.dma_start(fg, fg_in.to_broadcast([P, D])).then_inc(once_dma, 16)
                sp.wait_ge(S["h_ready"], 1)
                sp.dma_start(out.rearrange("(t p) d -> p t d", p=P), h_tok[:, :, :]).then_inc(stored, 16)
                sp.wait_ge(stored, 16)

            @block.scalar
            def _(ac):
                norm_act_sums(ac, 0, at(8, D))

            @block.vector
            def _(ve):
                ve.wait_ge(S["ss_ready"], 1)
                nc.vector.tensor_scalar(small[:, 4:8], small[:, 0:4], 1.0 / D, EPS, ALU.mult,
                                        ALU.add).then_inc(S["ms_ready"], 1)
                ve.wait_ge(S["sd_ready"], 1)
                nc.vector.reciprocal(small[:, 12:16], small[:, 8:12])
                ve.wait_ge(once_dma, 80)
                ve.drain()
                for t in range(TILES):
                    nc.vector.scalar_tensor_tensor(out=h_tok[:, t, :], in0=x[:, t, :], scalar=small[:, 12 + t:13 + t],
                                                   in1=fg, op0=ALU.mult, op1=ALU.mult)
                ve.drain().then_inc(S["h_ready"], 1)


def _feature_tiles(w):
    return w.reshape(w.shape[0] // P, P, w.shape[1]).transpose(1, 0, 2)


def _item(parts):
    flat = parts.reshape(P, -1)
    out = np.zeros((P, D), np.float32)
    out[:, :flat.shape[1]] = flat
    return out


def _weights(a, l):
    w = a["w_in"][l]
    edge = np.cumsum([0, Q_LORA, KV_LORA, ROPE, MI, MI, MH, MH, D, D])
    q, kv, kr, u, o, i, f, ga, gm = (w[:, edge[n]:edge[n + 1]] for n in range(9))
    swap = np.r_[ROPE // 2:ROPE, 0:ROPE // 2]
    items = [_item(_feature_tiles(kv[:, j * P:(j + 1) * P])) for j in range(KVT)]
    items += [_item(_feature_tiles(q[:, j * P:(j + 1) * P])) for j in range(QT)]
    none = np.zeros((D, NOPE), np.float32)
    items.append(_item(_feature_tiles(np.concatenate([none, kr, kr[:, swap]], 1))))
    up = a["w_kv_up"][l].reshape(KV_LORA, HEADS, NOPE + VDIM)
    items.append(_item(_feature_tiles(up[:, :, :NOPE].reshape(KV_LORA, -1))))
    items.append(_item(_feature_tiles(up[:, :, NOPE:].reshape(KV_LORA, -1))))
    qu = a["w_q_up"][l].reshape(Q_LORA, HEADS, QK)
    for h in range(HEADS):
        r = qu[:, h, NOPE:]
        items.append(_item(_feature_tiles(np.concatenate([qu[:, h, :NOPE], r, r[:, swap]], 1))))
    gates = np.zeros((D, P), np.float32)
    gates[:, 0:MH] = i
    gates[:, 32:32 + MH] = f
    items.append(_item(_feature_tiles(gates)))
    for m in (u, o):
        items += [_item(_feature_tiles(m[:, j * P:(j + 1) * P])) for j in range(MH)]
    items.append(_item(a["wv_m"][l].transpose(1, 0, 2)))
    items += [_item(_feature_tiles(ga[:, j * P:(j + 1) * P])) for j in range(KT)]
    merge = [None] * (2 * KT)
    for j in range(KT):
        c = slice(j * P, (j + 1) * P)
        merge[GATE_AT[j]] = _item(_feature_tiles(gm[:, c]))
        merge[BRANCH_AT[j]] = _item(np.concatenate([_feature_tiles(a["w_branch_a"][l][:, c]),
                                                    _feature_tiles(a["w_branch_m"][l][:, c])], 1))
    items += merge
    items += [_item(a["w_out"][l][k * P:(k + 1) * P]) for k in range(KT)]
    queries = [_item(_feature_tiles(a["peer_wq"][l][:, h * P:(h + 1) * P])) for h in range(PH)]
    keys = np.zeros((P, PH, 2, NKEYS), np.float32)
    for q2 in range(2):
        keys[q2 * HALF:(q2 + 1) * HALF, :, q2, :] = a["peer_keys"][l][:, q2].transpose(2, 0, 1)
    keys = keys.reshape(P, PH, 2 * NKEYS)
    for half in (slice(0, PH // 2), slice(PH // 2, PH)):
        items += [*queries[half], _item(keys[:, half])]
    items.append(_item(np.concatenate([a["wq_m"][l].transpose(1, 0, 2).reshape(P, -1),
                                       a["wk_m"][l].transpose(1, 0, 2).reshape(P, -1)], 1)))
    return np.stack(items)


def _columns(a, l):
    c = np.zeros((P, N_COLS), np.float32)
    c[:, C_QG:C_QG + QT] = a["q_norm_g"][l].reshape(QT, P).T
    c[:, C_KVG:C_KVG + KVT] = a["kv_norm_g"][l].reshape(KVT, P).T
    c[:, C_CW:C_CW + MH * CONV] = a["conv_w"][l].reshape(CONV, MH, P).transpose(2, 1, 0).reshape(P, -1)
    c[:, C_CB:C_CB + MH] = a["conv_b"][l].reshape(MH, P).T
    c[:, C_MG:C_MG + MH] = a["mh_norm_g"][l].reshape(MH, P).T
    c[:, C_SK:C_SK + MH] = a["m_skip"][l].reshape(MH, P).T
    c[0:MH, C_BI] = a["b_i"][l]
    c[0:MH, C_BF] = a["b_f"][l]
    return c


def _constants():
    c = np.zeros((P, N_CONST), np.float32)
    c[:, K_ID:K_ID + P] = np.eye(P)
    above = np.triu(np.full((P, P), NEG, np.float32), 1)
    c[:, K_MQ:K_MQ + P] = above
    c[:, K_MT:K_MT + P] = above.T
    for h in range(MH):
        c[h, K_SEL + h * P:K_SEL + (h + 1) * P] = 1.0
    c[:, K_IOTA:K_IOTA + TOPK] = np.arange(TOPK)
    freq = np.float32(THETA) ** (-np.arange(0, ROPE, 2, dtype=np.float32) / np.float32(ROPE))
    c[64:128, K_FREQ] = np.tile(freq, 4)
    c[96:112, K_SIGN] = -1.0
    c[112:128, K_SIGN] = 1.0
    c[:, K_HPI] = np.pi / 2
    return c


def kernel(**inputs):
    import concourse.bacc as bacc
    from concourse.bass_utils import run_bass_kernel_spmd

    a = {k: np.asarray(v) for k, v in inputs.items()}
    wada = a["w_ada"].reshape(DEPTH, KT, P, ADA_STEPS, ADA_W).transpose(0, 3, 2, 1, 4)
    arrays = {
        "x": a["x"][0],
        "c_cols": a["c"][0].reshape(KT, P).T,
        "positions": a["positions"],
        "w_ada": wada.reshape(DEPTH, ADA_STEPS, P, KT * ADA_W),
        "b_ada": a["b_ada"],
        "norm_g": np.stack([a["norm1_g"], a["norm2_g"]], 1),
        "weights": np.stack([_weights(a, l) for l in range(DEPTH)]),
        "columns": np.stack([_columns(a, l) for l in range(DEPTH)]),
        "constants": _constants(),
        "final_g": a["final_g"][None, :],
        "experts": np.concatenate([a["peer_u"], a["peer_v"]], -1).reshape(DEPTH * EXPERTS, ROW),
    }
    arrays = {k: np.ascontiguousarray(v) for k, v in arrays.items()}
    nc = bacc.Bacc("TRN2", target_bir_lowering=False, num_devices=1)
    args = [nc.dram_tensor("in_" + k, v.shape, mybir.dt.from_np(v.dtype), kind="ExternalInput").ap()
            for k, v in arrays.items()]
    out = nc.dram_tensor("out_0", (SEQ, D), F32, kind="ExternalOutput").ap()
    build_trunk(nc, *args, out)
    r = run_bass_kernel_spmd(nc, [{"in_" + k: v for k, v in arrays.items()}], core_ids=[0])
    return r.results[0]["out_0"].reshape(1, SEQ, D)
```

```python
from contextlib import ExitStack

import numpy as np

import concourse.bass as bass
from concourse import mybir

F32 = mybir.dt.float32
F32R = mybir.dt.float32r
U32 = mybir.dt.uint32
I32 = mybir.dt.int32
ALU = mybir.AluOpType
ACT = mybir.ActivationFunctionType
AX = mybir.AxisListType

P = 128
D = 1024
SEQ = 512
DEPTH = 2
TILES = SEQ // P
KT = D // P
HEADS = 8
NOPE, ROPE, VDIM = 64, 32, 64
QK = NOPE + ROPE
Q_LORA, KV_LORA = 768, 256
QT, KVT = Q_LORA // P, KV_LORA // P
THETA = 10000.0
MH, MD = 4, 128
MI = MH * MD
CONV = 4
PH, NKEYS, HALF, TOPK = 8, 128, 64, 16
EXPERTS = NKEYS * NKEYS
EPS = 1e-6
NEG = -1e30
FLOOR = -3.0e38
SM_SCALE = QK ** -0.5
K_SCALE = MD ** -0.5

IT_KV, IT_Q, IT_KPE = 0, KVT, KVT + QT
IT_KUP, IT_VUP, IT_QUP = IT_KPE + 1, IT_KPE + 2, IT_KPE + 3
IT_IF = IT_QUP + HEADS
IT_U, IT_O = IT_IF + 1, IT_IF + 1 + MH
IT_MV = IT_O + MH
IT_GA = IT_MV + 1
IT_MERGE = IT_GA + KT
IT_OUT = IT_MERGE + 2 * KT
IT_PQ = IT_OUT + KT
N_ITEMS = IT_PQ + PH + 2
IT_MQK = N_ITEMS
W_SLOTS = 4
HI_SLOTS = 2

ADA = 6 * D
ADA_W = 256
ADA_STEPS = ADA // ADA_W
ADA_SLOTS = 2
ADA_FIRST = 2 * D // ADA_W
SEC = D // ADA_W
ADA_LATE = ADA_STEPS - ADA_FIRST - 1
ADA_IN_MERGE = [[0], [1, 2], [3], [4, 5], [6], [7, 8], [], []]
LOAD_AFTER = [1, 3, 4, 5, 7, 8, 9]
assert len(LOAD_AFTER) == ADA_STEPS - ADA_LATE - ADA_SLOTS
ADA_ORDER = [*range(ADA_FIRST, ADA_STEPS), *range(ADA_FIRST)]

GATE_AT = [max(j, 2 * j - 1) for j in range(KT)]
BRANCH_AT = [min(2 * j + 2, KT + j) for j in range(KT)]
assert sorted(GATE_AT + BRANCH_AT) == list(range(2 * KT))

SPLIT = [*range(IT_KUP), *range(IT_IF, IT_MV), *range(IT_GA, IT_MERGE), *(IT_MERGE + g for g in GATE_AT),
         *range(IT_OUT, IT_PQ)]
SPLIT_IF, SPLIT_GA, SPLIT_GM, SPLIT_OUT = (SPLIT.index(i) for i in (IT_IF, IT_GA, IT_MERGE, IT_OUT))

C_QG, C_KVG = 0, QT
C_CW = C_KVG + KVT
C_CB = C_CW + MH * CONV
C_MG, C_SK = C_CB + MH, C_CB + 2 * MH
C_BI, C_BF = C_CB + 3 * MH, C_CB + 3 * MH + 1
N_COLS = C_BF + 1

K_ID, K_MQ, K_MT, K_SEL = 0, P, 2 * P, 3 * P
K_IOTA = K_SEL + MH * P
K_FREQ, K_SIGN, K_HPI = K_IOTA + TOPK, K_IOTA + TOPK + 1, K_IOTA + TOPK + 2
N_CONST = K_HPI + 1

B_KPE = KVT + QT
B_K, B_V = B_KPE + 1, B_KPE + 1 + HEADS
B_Q = B_V + TILES
B_N = B_Q + HEADS
D_V = 1 + 2 * MH
D_HEAD = D_V + TILES
D_GA = KT // MH
D_PER = 2 + D_GA
D_N = D_HEAD + MH * D_PER

UNITS = TILES * PH
RING = 8
GROUP = 2
ROUTE_PARTS = TOPK // GROUP
assert ROUTE_PARTS == 8
ROW = 2 * D
TWO_PI = 6.283185307179586
PI_LO = 3.1415925
ROUND = 12582912.0
TP_HI = 6.28125
TP_LO = TWO_PI - TP_HI


def build_trunk(nc, x_in, ct_in, pos_in, wada_in, bada_in, ng_in, w_in, cols_in, const_in, fg_in,
                experts_in, out):
    with ExitStack() as ctx:
        def sb(name, shape, dt=F32):
            return ctx.enter_context(nc.sbuf_tensor(name, shape, dt))

        def twins(name, shape):
            with nc.sbuf_tensor(name + "_r", shape, F32R) as rounded:
                pass
            plain = sb(name, shape)
            assert nc.lookup_mloc(plain).addr == nc.lookup_mloc(rounded).addr
            return plain, rounded

        def sem(name):
            return ctx.enter_context(nc.semaphore(name))

        x = sb("x", [P, TILES, D])
        V_PAD = 64
        ada_all = sb("ada", [P, V_PAD + ADA])
        ada = ada_all[:, V_PAD:V_PAD + ADA]
        const = sb("const", [P, N_CONST])
        ones = sb("ones", [P, P])
        zeros = sb("zeros", [P, P])
        cols = sb("cols", [P, N_COLS])
        rope = sb("rope", [P, SEQ])
        cact = sb("cact", [P, KT])
        layer_row = sb("layer_row", [P, 1])
        small = sb("small", [P, 32])
        h_tok, h_tok_r = twins("h_tok", [P, TILES, D])
        hT, h_high = twins("hT", [P, KT, SEQ])
        w_ring, w_low = twins("w_ring", [P, W_SLOTS, D])
        w_high = sb("w_high", [P, HI_SLOTS, D], F32R)
        w_mqk = sb("w_mqk", [P, D])
        ARENA = 100 * 256
        arena, arena_r = twins("arena", [P, ARENA])
        hT_flat = hT[:, :, :].rearrange("p k t -> p (k t)")
        h_flat = h_tok[:, :, :].rearrange("p t d -> p (t d)")
        h_flat_r = h_tok_r[:, :, :].rearrange("p t d -> p (t d)")

        h_low = h_tok_r[:, :, :].rearrange("p t (k m) -> p k t m", m=P)

        def at(kib, n, area=None):
            a = arena if area is None else area
            o = int(kib * 256)
            return a[:, o:o + n]

        ident = const[:, K_ID:K_ID + P]
        mask_q = const[:, K_MQ:K_MQ + P]
        mask_t = const[:, K_MT:K_MT + P]
        sel = const[:, K_SEL:K_SEL + MH * P].rearrange("p (h m) -> p h m", h=MH)
        iota = const[:, K_IOTA:K_IOTA + TOPK]

        lat = at(0, 8 * SEQ).rearrange("p (j t) -> p j t", j=8)
        sq = at(16, 2 * SEQ).rearrange("p (b t) -> p b t", b=2)
        qh = at(20, HEADS * SEQ).rearrange("p (h t) -> p h t", h=HEADS)
        kh = at(36, HEADS * SEQ).rearrange("p (h t) -> p h t", h=HEADS)
        v = at(52, TILES * SEQ).rearrange("p (t e) -> p t e", t=TILES)
        kpe = at(60, SEQ)
        rtmp = at(62, SEQ)
        rms = at(64, SEQ)
        ada_early, ada_late = (([at(k, KT * ADA_W).rearrange("p (k n) -> p k n", k=KT) for k in slots],
                                at(a, 2 * ADA_W).rearrange("p (b n) -> p b n", b=2), at(g, D))
                               for slots, a, g in (((66, 74), 82, 84), ((59, 80), 52, 88)))
        junk = at(0, D)
        prob = at(0, 3 * SEQ).rearrange("p (b t) -> p b t", b=3)
        probT = at(6, 2 * SEQ).rearrange("p (b t) -> p b t", b=2)
        scol = at(10, 5 * 32).rearrange("p (r i) -> p r i", r=5)
        so = at(11, MH * SEQ).rearrange("p (h t) -> p h t", h=MH)
        att = at(62, TILES * SEQ).rearrange("p (t e) -> p t e", t=TILES)
        PAD = CONV - 1
        UP = SEQ + PAD
        up = at(70, MH * UP).rearrange("p (h t) -> p h t", h=MH)
        ca = at(79, MH * SEQ).rearrange("p (h t) -> p h t", h=MH)
        attT = at(92, 4 * SEQ).rearrange("p (k t) -> p k t", k=4)
        row_i, row_f = (at(k, SEQ)[0:MH, :] for k in (87, 89))
        row_t = row_m = at(92, SEQ)[0:MH, :]
        row_ln = row_cum = row_s = at(94, SEQ)[0:MH, :]
        row_nm = at(60, SEQ)[0:MH, :]
        row_a, row_e = row_i, row_s
        VW = MD + 1
        assert TILES * MH * VW <= V_PAD + 2 * D
        v1 = at(0, TILES * MH * VW, ada_all).rearrange("p (t h e) -> p t h e", t=TILES, h=MH)
        ae = at(10.75, 32).rearrange("p (r t h) -> p r t h", r=2, t=TILES)
        nmb = at(20, 2 * SEQ).rearrange("p (b t) -> p b t", b=2)
        nmd = at(24, 2 * SEQ).rearrange("p (b t) -> p b t", b=2)
        dw = at(28, 2 * SEQ).rearrange("p (b t) -> p b t", b=2)
        mk = at(32, 2 * SEQ).rearrange("p (b t) -> p b t", b=2)
        mq = at(53, 2 * SEQ).rearrange("p (b t) -> p b t", b=2)
        mcol = at(62, 64)
        P_OFF = [0, 512, 896, 1152]
        pm = at(0, 2 * 1280).rearrange("p (b t) -> p b t", b=2)
        hn = at(65, 2 * MI).rearrange("p (b e) -> p b e", b=2)
        ymT = at(36, MH * SEQ).rearrange("p (h t) -> p h t", h=MH)
        ctmp = at(44, SEQ)
        ga_raw = [at(k, SEQ) for k in (70, 72, 74, 76, 46, 48, 50, 57)]
        mg_high = at(0, KT * SEQ, arena_r).rearrange("p (k t) -> p k t", k=KT)
        mg_low = [at(k, SEQ, arena_r) for k in (32, 34, 44, 54, 67, 78)] + [at(k, SEQ, h_flat_r) for k in (0, 2)]
        sg = at(16, 4 * SEQ).rearrange("p (b g t) -> p b g t", b=2, g=2)
        mt = at(24, 4 * SEQ).rearrange("p (b g t) -> p b g t", b=2, g=2)
        qp = at(48, PH * SEQ).rearrange("p (h t) -> p h t", h=PH)
        scores = at(68, UNITS * 2 * NKEYS)
        ring = at(0, RING * ROW).rearrange("p (r d) -> p r d", r=RING)
        h_now = at(0, D, hT_flat)
        diag = at(4, 8 * P, hT_flat).rearrange("p (r m) -> p r m", r=8)
        ytmp = at(8, D, hT_flat)
        stage = at(0, 2 * 2 * NKEYS, w_mqk).rearrange("p (b q n) -> p b q n", b=2, q=2)
        cand = at(2, 2 * TOPK * TOPK, w_mqk).rearrange("p (b n) -> p b n", b=2)
        hot = at(64, 2 * TOPK * TOPK)
        rest = at(66, NKEYS)
        rcol = at(66.5, 20 * TOPK)
        top = rcol[:, 0:2 * TOPK].rearrange("p (q n) -> p q n", q=2)
        top_i = rcol[:, 2 * TOPK:4 * TOPK].bitcast(U32).rearrange("p (q n) -> p q n", q=2)
        top_f = rcol[:, 4 * TOPK:6 * TOPK].rearrange("p (q n) -> p q n", q=2)
        best = rcol[:, 6 * TOPK:7 * TOPK]
        pos = rcol[:, 7 * TOPK:8 * TOPK].bitcast(U32)
        posab = rcol[:, 8 * TOPK:10 * TOPK].bitcast(U32).rearrange("p (q n) -> p q n", q=2)
        posab_f = rcol[:, 10 * TOPK:12 * TOPK].rearrange("p (q n) -> p q n", q=2)
        pick = rcol[:, 12 * TOPK:14 * TOPK]
        flat_i = rcol[:, 14 * TOPK:15 * TOPK]
        gexp = rcol[:, 15 * TOPK:16 * TOPK]
        gate = rcol[:, 16 * TOPK:18 * TOPK].rearrange("p (b n) -> p b n", b=2)
        dots = sb("dots", [P, 2, TOPK])
        gel = sb("gel", [P, 2, TOPK])
        idx = sb("idx", [P, 2, TOPK], U32)
        gs = sb("gs", [P, 4])
        ang = at(0, SEQ)
        turns = at(2, SEQ)
        pos_i = at(4, SEQ).bitcast(I32)
        c_rows = at(8, KT * P).rearrange("p (k m) -> p k m", k=KT)
        first_w = at(12, ADA_FIRST * KT * ADA_W).rearrange("p (s n) -> p s n", s=ADA_FIRST)
        first_acc = at(76, ADA_FIRST // 2 * ADA_W).rearrange("p (s n) -> p s n", s=ADA_FIRST // 2)
        first_gain = at(84, D)

        bank = [ctx.enter_context(nc.psum_tensor(f"bank{i}", [P, 512], F32)) for i in range(8)]

        gathered = [sem(f"gathered{r}") for r in range(RING)]
        first_loaded = [sem(f"first_loaded{i}") for i in range(ADA_FIRST)]
        c_loaded, c_spread, x_loaded, first_bias, first_sum, first_done = (
            sem(n) for n in ("c_loaded", "c_spread", "x_loaded", "first_bias", "first_sum", "first_done"))
        once_dma, once_act, once_dve, stored = sem("once_dma"), sem("once_act"), sem("once_dve"), sem("stored")
        names = ("mg_high_ready mg_low_ready so_ready scaled high_ready low_ready tp_low out_used "
                 "ada_acc ada_sum ada_ev bias_loaded cols_loaded mqk_loaded ss_ready ms_ready "
                 "sd_ready h_ready tp_ready tp_ev mm_ready act_ev dve_ev sq_ready ss_mm rt_ready "
                 "sqrt_ready latn sc_ready nm_ready p_ready pt_ready pt_ev o_ready o_ev at_ready "
                 "at_ev d_ready d_ev kpe_ready pads lnf rows_a rows_s rows_e ae_ready ae_ev "
                 "conv_ready nmb_ready nmb_ev nmd_ready dw_ready s_ready pm_ready n_ready n_ev "
                 "var_ready dev_ready hn_ready hnT_ready y_ev e_ready e_act e_dve wo_ready x_ready "
                 "q_ready q_ev s2_ready s2_act s2_dve passed stage_ready best_ready exp_ready "
                 "idx_ready dots_ready gelu_ready diag_ready slot_free h_now_ready y_done y_free").split()
        w_loaded = [sem(f"w_loaded{i}") for i in range(W_SLOTS)]
        ada_loaded = [sem(f"ada_loaded{i}") for i in range(ADA_SLOTS)]
        S = {n: sem(n) for n in names}
        layer_sems = w_loaded + ada_loaded + list(S.values())

        def w_here(eng, item):
            eng.wait_ge(w_loaded[item % W_SLOTS], 16 * (item // W_SLOTS + 1))
            return w_ring[:, item % W_SLOTS, :]

        def item_used(sp, i):
            if i < IT_KUP:
                sp.wait_ge(S["mm_ready"], i + 1)
            elif i == IT_KUP:
                sp.wait_ge(S["mm_ready"], B_V)
            elif i < IT_IF:
                sp.wait_ge(S["mm_ready"], B_Q + i - IT_VUP)
            elif i < IT_MV:
                sp.wait_ge(S["d_ready"], i - IT_IF + 1)
            elif i < IT_GA:
                sp.wait_ge(S["d_ready"], D_HEAD)
            elif i < IT_MERGE:
                h, j = divmod(i - IT_GA, D_GA)
                sp.wait_ge(S["d_ready"], D_HEAD + h * D_PER + 2 + j + 1)
            elif i < IT_OUT:
                sp.wait_ge(S["e_ready"], i - IT_MERGE + 1)
            elif i < IT_PQ - 1:
                sp.wait_ge(S["out_used"], i - IT_OUT + 1)
            elif i == IT_PQ - 1:
                sp.wait_ge(S["wo_ready"], 2 * TILES)
            else:
                sp.wait_ge(S["q_ready"], i - IT_PQ + 1)

        def load_weights(sp, l, first, last):
            for i in range(first, min(last, N_ITEMS)):
                if i >= W_SLOTS:
                    item_used(sp, i - W_SLOTS)
                sp.dma_start(w_ring[:, i % W_SLOTS, :],
                             w_in[bass.ds(l, 1), i].rearrange("a p n -> (a p) n")
                             ).then_inc(w_loaded[i % W_SLOTS], 16)

        def split_high(ac, n):
            i = SPLIT[n]
            if n < SPLIT_OUT:
                w_here(ac, i)
            else:
                ac.wait_ge(S["scaled"], n - SPLIT_OUT + 1)
            if n >= HI_SLOTS:
                item_used(ac, SPLIT[n - HI_SLOTS])
            nc.scalar.copy(w_high[:, n % HI_SLOTS, :], w_ring[:, i % W_SLOTS, :]
                           ).then_inc(S["high_ready"], 1)

        def split_low(po, n):
            slot = SPLIT[n] % W_SLOTS
            po.wait_ge(S["high_ready"], n + 1)
            nc.gpsimd.tensor_tensor(w_low[:, slot, :], w_ring[:, slot, :], w_high[:, n % HI_SLOTS, :], ALU.subtract
                                    ).then_inc(S["low_ready"], 1)

        def split_product(pe, o, n, k, m=P):
            if k == 0:
                pe.wait_ge(S["low_ready"], n + 1)
            c = slice(k * P, k * P + m)
            high = w_high[:, n % HI_SLOTS, c]
            low = w_low[:, SPLIT[n] % W_SLOTS, c]
            nc.tensor.matmul(o, high, h_high[:, k, :], start=k == 0, stop=False)
            nc.tensor.matmul(o, high, h_low[:, k], start=False, stop=False)
            return nc.tensor.matmul(o, low, h_high[:, k, :], start=False, stop=k == KT - 1)

        def load_ada(sp, area, l, i):
            k = ADA_ORDER[i]
            if i >= ADA_SLOTS:
                sp.wait_ge(S["ada_acc"], i - ADA_SLOTS + 1)
            sp.dma_start(area[0][i % ADA_SLOTS].rearrange("p k n -> p (k n)"),
                         wada_in[bass.ds(l, 1), k].rearrange("a p n -> (a p) n")
                         ).then_inc(ada_loaded[i % ADA_SLOTS], 16)

        def load_ada_bias(sp, l, first, last, loaded=S["bias_loaded"]):
            sp.dma_start(ada[:, first * D:last * D],
                         bada_in[bass.ds(l, 1), first * D:last * D].to_broadcast([P, (last - first) * D])
                         ).then_inc(loaded, 16)

        def load_gain(sp, to, l, n, loaded=S["bias_loaded"]):
            sp.dma_start(to, ng_in[bass.ds(l, 1), n:n + 1, :].rearrange("a b n -> (a b) n")
                         .to_broadcast([P, D])).then_inc(loaded, 16)

        def ada_sum_dve(ve, area, i):
            ve.wait_ge(ada_loaded[i % ADA_SLOTS], 16 * (i // ADA_SLOTS + 1))
            if i >= 2:
                ve.wait_ge(S["ada_sum"], i - 1)
            sum_tiles(ve, area[1][:, i % 2, :], area[0][i % ADA_SLOTS]).then_inc(S["ada_acc"], 1)

        def sum_tiles(ve, a, w):
            ins = nc.vector.tensor_scalar(a, w[:, 0, :], cact[:, 0:1], None, ALU.mult)
            for j in range(1, KT):
                ve.drain()
                ins = nc.vector.scalar_tensor_tensor(out=a, in0=w[:, j, :], scalar=cact[:, j:j + 1], in1=a,
                                                     op0=ALU.mult, op1=ALU.add)
            return ins

        def ada_bias_dve(ve, area, i):
            ve.wait_ge(S["ada_sum"], i + 1)
            if i in (0, ADA_LATE):
                ve.wait_ge(S["bias_loaded"], 32 if i == 0 else 64)
            add_bias(ve, bank[6 + i % 2], ADA_ORDER[i], area[2], S["ada_ev"])

        def add_bias(ve, o, k, gain, read=None):
            a = ada[:, k * ADA_W:(k + 1) * ADA_W]
            ins = nc.vector.tensor_tensor(a, a, o[:, 0:ADA_W], ALU.add)
            if read is not None:
                ins.then_inc(read, 1)
            if k // SEC in (1, 4):
                g = gain[:, (k % SEC) * ADA_W:(k % SEC + 1) * ADA_W]
                ve.drain()
                nc.vector.scalar_tensor_tensor(out=a, in0=a, scalar=1.0, in1=g, op0=ALU.add, op1=ALU.mult)

        def ada_step_dve(ve, area, i, first, last):
            if i < last:
                ada_sum_dve(ve, area, i)
            if i > first:
                ada_bias_dve(ve, area, i - 1)

        def ada_pe(pe, area, i):
            pe.wait_ge(S["ada_acc"], i + 1)
            if i >= 2:
                pe.wait_ge(S["ada_ev"], i - 1)
            nc.tensor.matmul(bank[6 + i % 2][:, 0:ADA_W], ones[:, :], area[1][:, i % 2, :], start=True,
                             stop=True).then_inc(S["ada_sum"], 1)

        def clear_semaphores():
            nc.all_engine_barrier()
            for i, s in enumerate(layer_sems):
                (nc.gpsimd, nc.vector, nc.scalar, nc.tensor, nc.sync)[i % 5].sem_clear(s)
            nc.all_engine_barrier()

        def norm_act_sums(ac, n, scratch):
            for t in range(0 if n else TILES // 2, TILES):
                ac.drain()
                if n == 1:
                    ac.wait_ge(S["x_ready"], t + 1)
                ins = nc.scalar.activation(scratch, x[:, t, :], ACT.Square, accum_out=small[:, t:t + 1])
            ac.drain().then_inc(S["ss_ready"], 1)
            ac.wait_ge(S["ms_ready"], n + 1)
            nc.scalar.activation(small[:, 8:12], small[:, 4:8], ACT.Sqrt).then_inc(S["sd_ready"], 1)

        def norm_dve_sums(ve):
            for t in range(TILES // 2):
                nc.vector.tensor_tensor_reduce(h_tok[:, t, :], x[:, t, :], x[:, t, :], 1.0, 0.0, ALU.mult, ALU.add,
                                               small[:, t:t + 1])
            ve.drain()

        def norm_dve(ve, n, shift, gain):
            if n == 0:
                norm_dve_sums(ve)
            ve.wait_ge(S["ss_ready"], n + 1)
            nc.vector.tensor_scalar(small[:, 4:8], small[:, 0:4], 1.0 / D, EPS, ALU.mult,
                                    ALU.add).then_inc(S["ms_ready"], 1)
            ve.wait_ge(S["sd_ready"], n + 1)
            nc.vector.reciprocal(small[:, 12:16], small[:, 8:12])
            ve.drain()
            for t in range(TILES + 1):
                if t < TILES:
                    nc.vector.scalar_tensor_tensor(out=h_tok[:, t, :], in0=x[:, t, :], scalar=small[:, 12 + t:13 + t],
                                                   in1=gain, op0=ALU.mult, op1=ALU.mult)
                    ve.drain()
                    nc.vector.tensor_tensor(h_tok[:, t, :], h_tok[:, t, :], shift, ALU.add).then_inc(S["h_ready"], 1)
                if n == 0 and t >= 1:
                    for g in range(2):
                        i = 2 * (t - 1) + g
                        k, c = slice(4 * g, 4 * g + 4), slice((t - 1) * P, t * P)
                        ve.wait_ge(S["tp_ev"], i + 1)
                        nc.vector.tensor_tensor(h_low[:, k, t - 1, :],
                                                bank[i % 4][:, :].rearrange("p (j t) -> p j t", j=4), h_high[:, k, c],
                                                ALU.subtract).then_inc(S["tp_low"], 1)

        def norm_pe(pe, n):
            for t in range(TILES):
                pe.wait_ge(S["h_ready"], n * TILES + t + 1)
                for g in range(2):
                    i = 2 * t + g
                    if i >= 4 and n == 0:
                        pe.wait_ge(S["tp_low"], i - 3)
                    elif i >= 4:
                        pe.wait_ge(S["tp_ev"], 2 * TILES + i - 3)
                    for j in range(4):
                        ins = nc.tensor.transpose(bank[i % 4][:, j * P:(j + 1) * P],
                                                  h_tok[:, t, (4 * g + j) * P:(4 * g + j + 1) * P], ident)
                    ins.then_inc(S["tp_ready"], 1)

        def norm_act_copies(ac, n):
            for t in range(TILES):
                for g in range(2):
                    i = 2 * t + g
                    ac.wait_ge(S["tp_ready"], n * 2 * TILES + i + 1)
                    nc.scalar.copy((h_high if n == 0 else hT)[:, 4 * g:4 * g + 4, t * P:(t + 1) * P],
                                   bank[i % 4][:, :].rearrange("p (j t) -> p j t", j=4)).then_inc(S["tp_ev"], 1)

        FIRST_ORDER = [i ^ 1 for i in range(ADA_FIRST)]
        with nc.Block() as block:
            @block.sync
            def _(sp):
                sp.dma_start(cact[:, :], ct_in).then_inc(c_loaded, 16)
                for i in range(ADA_FIRST):
                    sp.dma_start(first_w[:, i], wada_in[0, i]).then_inc(first_loaded[i], 16)
                    if i == 1:
                        sp.dma_start(const[:, :], const_in).then_inc(once_dma, 16)
                        sp.dma_start(pos_i, pos_in.to_broadcast([P, SEQ])).then_inc(once_dma, 16)
                        load_ada_bias(sp, 0, 0, 2, first_bias)
                        load_gain(sp, first_gain, 0, 0, first_bias)
                sp.dma_start(x[:, :, :], x_in.rearrange("(t p) d -> p t d", p=P)).then_inc(x_loaded, 16)
                sp.wait_ge(x_loaded, 16)

            @block.tensor
            def _(pe):
                pe.wait_ge(c_spread, 1)
                for i in FIRST_ORDER:
                    if i % 2:
                        pe.wait_ge(first_loaded[i], 16)
                        for k in range(KT):
                            ins = nc.tensor.matmul(bank[i][:, 0:ADA_W], c_rows[:, k, :],
                                                   first_w[:, i, k * ADA_W:(k + 1) * ADA_W], start=k == 0,
                                                   stop=k == KT - 1)
                    else:
                        pe.wait_ge(first_sum, i // 2 + 1)
                        ins = nc.tensor.matmul(bank[i][:, 0:ADA_W], ones[:, :], first_acc[:, i // 2, :], start=True,
                                               stop=True)
                    ins.then_inc(first_done, 1)

            @block.vector
            def _(ve):
                def sum_step(i):
                    ve.wait_ge(first_loaded[i], 16)
                    sum_tiles(ve, first_acc[:, i // 2, :], first_w[:, i, :].rearrange("p (k n) -> p k n", k=KT)
                              ).then_inc(first_sum, 1)

                def finish_step(n):
                    i = FIRST_ORDER[n]
                    ve.wait_ge(first_done, n + 1)
                    add_bias(ve, bank[i], i, first_gain)

                nc.vector.memset(ones[:, :], 1.0)
                nc.vector.memset(zeros[:, :], 0.0)
                nc.vector.memset(layer_row[:, :], 0.0)
                ve.wait_ge(once_act, 1)
                nc.vector.tensor_copy(c_rows[:, :, :], cact[:, :].unsqueeze(2).to_broadcast([P, KT, P]))
                ve.drain().then_inc(c_spread, 1)
                sum_step(0)
                ve.wait_ge(once_dma, 32)
                nc.vector.tensor_copy(ang, pos_i)
                ve.drain()
                nc.vector.tensor_scalar(ang, ang, const[:, K_FREQ:K_FREQ + 1], None, ALU.mult)
                ve.drain()
                nc.vector.tensor_scalar(turns, ang, 1.0 / TWO_PI, ROUND, ALU.mult, ALU.add)
                ve.drain()
                nc.vector.tensor_scalar(turns, turns, ROUND, None, ALU.subtract)
                ve.drain()
                for part in (TP_HI, TP_LO):
                    nc.vector.scalar_tensor_tensor(out=ang, in0=turns, scalar=-part, in1=ang, op0=ALU.mult,
                                                   op1=ALU.add)
                    ve.drain()
                nc.vector.tensor_scalar(ang, ang, PI_LO, -PI_LO, ALU.min, ALU.max).then_inc(once_dve, 1)
                ve.wait_ge(first_bias, 32)
                for n in range(0, ADA_FIRST, 2):
                    if n + 2 < ADA_FIRST:
                        sum_step(n + 2)
                    finish_step(n)
                    finish_step(n + 1)

            @block.scalar
            def _(ac):
                ac.wait_ge(c_loaded, 16)
                nc.scalar.activation(cact[:, :], cact[:, :], ACT.Silu).then_inc(once_act, 1)
                ac.wait_ge(once_dve, 1)
                nc.scalar.activation(turns[64:96, :], ang[64:96, :], ACT.Abs)
                ac.drain()
                nc.scalar.activation(rope[64:96, :], turns[64:96, :], ACT.Sin, scale=-1.0,
                                     bias=const[64:96, K_HPI:K_HPI + 1])
                nc.scalar.activation(rope[96:128, :], ang[96:128, :], ACT.Sin,
                                     scale=const[96:128, K_SIGN:K_SIGN + 1]).then_inc(once_act, 1)

        with nc.Fori(0, DEPTH) as l:
            with nc.Block() as block:
                @block.sync
                def _(sp):
                    sp.dma_start(cols[:, :], cols_in[bass.ds(l, 1)].rearrange("a p n -> (a p) n")
                                 ).then_inc(S["cols_loaded"], 16)
                    load_weights(sp, l, 0, W_SLOTS)
                    for i in range(ADA_SLOTS):
                        load_ada(sp, ada_early, l, i)
                    load_ada_bias(sp, l, 2, 6)
                    load_gain(sp, ada_early[2], l, 1)

                @block.vector
                def _(ve):
                    norm_dve(ve, 0, ada[:, 0:D], ada[:, D:2 * D])

                @block.tensor
                def _(pe):
                    norm_pe(pe, 0)

                @block.scalar
                def _(ac):
                    norm_act_sums(ac, 0, junk)
                    for n in range(HI_SLOTS):
                        split_high(ac, n)
                    norm_act_copies(ac, 0)

                @block.gpsimd
                def _(po):
                    for n in range(HI_SLOTS):
                        split_low(po, n)

            act_tiles = [b for b in range(B_N) if b != B_KPE]
            dve_tiles = [b for b in range(B_N) if b == B_KPE or b >= B_Q]

            ADA_AFTER = [1, 2, *range(4, B_KPE + 1), B_K + 7, B_V + 3, B_Q, B_Q + 2, B_Q + 3, B_Q + 5, B_Q + 6, B_Q + 7]
            ADA_HEADS = [0, 1, 3, 4, 5]
            assert len(ADA_AFTER) == ADA_LATE

            def bank_free(pe, b):
                if b in act_tiles:
                    pe.wait_ge(S["act_ev"], act_tiles.index(b) + 1)
                if b in dve_tiles:
                    pe.wait_ge(S["dve_ev"], dve_tiles.index(b) + 1)

            with nc.Block() as block:
                @block.sync
                def _(sp):
                    for i in range(W_SLOTS, IT_IF + W_SLOTS):
                        load_weights(sp, l, i, i + 1)
                        if ADA_SLOTS + i - W_SLOTS < ADA_LATE:
                            load_ada(sp, ada_early, l, ADA_SLOTS + i - W_SLOTS)
                    sp.dma_start(w_mqk[:, :], w_in[bass.ds(l, 1), IT_MQK].rearrange("a p n -> (a p) n")
                                 ).then_inc(S["mqk_loaded"], 16)

                @block.tensor
                def _(pe):
                    def square_sum(b):
                        pe.wait_ge(S["sq_ready"], b + 1)
                        nc.tensor.matmul(bank[3 if b < KVT else 4][:, :], ones[:, :], sq[:, b % 2, :],
                                         start=b in (0, KVT), stop=b in (KVT - 1, B_KPE - 1)
                                         ).then_inc(S["ss_mm"], 1)

                    for b in range(B_N):
                        if b >= 3:
                            bank_free(pe, b - 3)
                        o = bank[b % 3]
                        if b <= B_KPE:
                            for k in range(KT):
                                ins = split_product(pe, o[:, :], b, k)
                            ins.then_inc(S["mm_ready"], 1)
                        elif b < B_V:
                            if b == B_K:
                                w = w_here(pe, IT_KUP)
                                pe.wait_ge(S["latn"], 1)
                            h = b - B_K
                            for j in range(KVT):
                                ins = nc.tensor.matmul(o[0:NOPE, :], w[:, j * 512 + h * NOPE:j * 512 + (h + 1) * NOPE],
                                                       lat[:, j, :], start=j == 0, stop=j == KVT - 1)
                            ins.then_inc(S["mm_ready"], 1)
                        elif b < B_Q:
                            if b == B_V:
                                w = w_here(pe, IT_VUP)
                            t = b - B_V
                            for j in range(KVT):
                                ins = nc.tensor.matmul(o[:, :], lat[:, j, t * P:(t + 1) * P],
                                                       w[:, j * 512:(j + 1) * 512], start=j == 0, stop=j == KVT - 1)
                            ins.then_inc(S["mm_ready"], 1)
                        else:
                            w = w_here(pe, IT_QUP + b - B_Q)
                            if b == B_Q:
                                pe.wait_ge(S["latn"], 2)
                            for j in range(QT):
                                ins = nc.tensor.matmul(o[:, :], w[:, j * P:(j + 1) * P], lat[:, KVT + j, :],
                                                       start=j == 0, stop=j == QT - 1)
                            ins.then_inc(S["mm_ready"], 1)
                        if 1 <= b <= B_KPE:
                            square_sum(b - 1)
                        for i in range(ADA_LATE):
                            if ADA_AFTER[i] == b:
                                ada_pe(pe, ada_early, i)

                @block.scalar
                def _(ac):
                    def sqrt(n):
                        ac.wait_ge(S["rt_ready"], n)
                        nc.scalar.activation(rms, rms, ACT.Sqrt).then_inc(S["sqrt_ready"], 1)

                    for b in act_tiles:
                        ac.wait_ge(S["mm_ready"], b + 1)
                        o = bank[b % 3]
                        if b < B_KPE:
                            if b + HI_SLOTS < SPLIT_IF:
                                split_high(ac, b + HI_SLOTS)
                            nc.scalar.copy(lat[:, b, :], o[:, :]).then_inc(S["act_ev"], 1)
                            ac.drain()
                            if b >= 2:
                                ac.wait_ge(S["ss_mm"], b - 1)
                            nc.scalar.activation(sq[:, b % 2, :], lat[:, b, :], ACT.Square).then_inc(S["sq_ready"], 1)
                            if b == KVT:
                                sqrt(1)
                            if b == B_KPE - 1:
                                sqrt(2)
                        elif b < B_V:
                            nc.scalar.copy(kh[0:NOPE, b - B_K, :], o[0:NOPE, :]).then_inc(S["act_ev"], 1)
                        elif b < B_Q:
                            nc.scalar.copy(v[:, b - B_V, :], o[:, :]).then_inc(S["act_ev"], 1)
                        else:
                            nc.scalar.copy(qh[0:NOPE, b - B_Q, :], o[0:NOPE, :]).then_inc(S["act_ev"], 1)
                    for n in range(HI_SLOTS):
                        split_high(ac, SPLIT_IF + n)

                @block.vector
                def _(ve):
                    def mean_square(n, width):
                        ve.wait_ge(S["ss_mm"], KVT if n == 0 else B_KPE)
                        nc.vector.tensor_scalar(rms, bank[3 + n][:, :], 1.0 / width, EPS, ALU.mult,
                                                ALU.add).then_inc(S["rt_ready"], 1)

                    def scale_latents(n, first, count, gain):
                        ve.wait_ge(S["sqrt_ready"], n + 1)
                        nc.vector.reciprocal(rms, rms)
                        ve.drain()
                        for j in range(count):
                            nc.vector.scalar_tensor_tensor(out=lat[:, first + j, :], in0=lat[:, first + j, :],
                                                           scalar=cols[:, gain + j:gain + j + 1], in1=rms,
                                                           op0=ALU.mult, op1=ALU.mult)
                        ve.drain().then_inc(S["latn"], 1)

                    def rotate(o, dst):
                        nc.vector.tensor_tensor(rtmp[64:96, :], o[96:128, :], rope[96:128, :], ALU.mult)
                        nc.vector.tensor_tensor(dst, o[64:96, :], rope[64:96, :], ALU.mult)
                        ve.drain().then_inc(S["dve_ev"], 1)
                        nc.vector.tensor_tensor(dst, dst, rtmp[64:96, :], ALU.add)
                        ve.drain()

                    def ada_steps(first, last):
                        for i in range(first, last):
                            ada_step_dve(ve, ada_early, i, 0, ADA_LATE)

                    ada_steps(0, 2)
                    ve.wait_ge(S["cols_loaded"], 16)
                    mean_square(0, KV_LORA)
                    scale_latents(0, 0, KVT, C_KVG)
                    ada_steps(2, 7)
                    ve.wait_ge(S["mm_ready"], B_KPE + 1)
                    rotate(bank[B_KPE % 3], kpe[64:96, :])
                    ve.sem_inc(S["kpe_ready"], 1)
                    mean_square(1, Q_LORA)
                    scale_latents(1, KVT, QT, C_QG)
                    ada_steps(7, 10)
                    for h in range(HEADS):
                        ve.wait_ge(S["mm_ready"], B_Q + h + 1)
                        rotate(bank[(B_Q + h) % 3], qh[64:96, h, :])
                        if h in ADA_HEADS:
                            i = 10 + ADA_HEADS.index(h)
                            ada_steps(i, i + 1)
                    ada_steps(ADA_LATE, ADA_LATE + 1)

                @block.gpsimd
                def _(po):
                    for n in range(HI_SLOTS, SPLIT_IF):
                        split_low(po, n)
                    po.drain()
                    po.wait_ge(S["kpe_ready"], 1)
                    for h in range(HEADS):
                        nc.gpsimd.tensor_copy(kh[64:96, h, :], kpe[64:96, :])
                    po.drain()
                    for n in range(SPLIT_IF, SPLIT_IF + HI_SLOTS):
                        split_low(po, n)

            ITEMS = HEADS * TILES
            V_ITEM = D_V * KT // 3
            AE_ITEM = V_ITEM + TILES + 1
            with nc.Block() as block:
                @block.sync
                def _(sp):
                    load_weights(sp, l, IT_IF + W_SLOTS, IT_MV + W_SLOTS)

                @block.gpsimd
                def _(po):
                    nc.gpsimd.memset(up[:, :, 0:PAD], 0.0)
                    nc.gpsimd.memset(v1[:, :, :, MD:VW], 1.0)
                    po.drain().then_inc(S["pads"], 1)
                    for n in range(SPLIT_IF + HI_SLOTS, SPLIT_GA + HI_SLOTS):
                        split_low(po, n)

                @block.tensor
                def _(pe):
                    def score(i):
                        h, t = divmod(i, TILES)
                        n = (t + 1) * P
                        if i >= 2:
                            pe.wait_ge(S["p_ready"], i - 1)
                        nc.tensor.matmul(bank[i % 2][:, 0:n], qh[0:QK, h, t * P:(t + 1) * P], kh[0:QK, h, 0:n],
                                         start=True, stop=True).then_inc(S["sc_ready"], 1)

                    def turn(i):
                        t = i % TILES
                        pe.wait_ge(S["p_ready"], i + 1)
                        if i >= 2:
                            pe.wait_ge(S["pt_ev"], i - 1)
                        for j in range(t + 1):
                            ins = nc.tensor.transpose(bank[2 + i % 2][:, j * P:(j + 1) * P],
                                                      prob[:, i % 3, j * P:(j + 1) * P], ident)
                        ins.then_inc(S["pt_ready"], 1)

                    def values(i):
                        h, t = divmod(i, TILES)
                        pe.wait_ge(S["pt_ev"], i + 1)
                        if i >= 2:
                            pe.wait_ge(S["o_ev"], i - 1)
                        for j in range(t + 1):
                            ins = nc.tensor.matmul(bank[4 + i % 2][:, 0:VDIM], probT[:, i % 2, j * P:(j + 1) * P],
                                                   v[:, j, h * VDIM:(h + 1) * VDIM], start=j == 0, stop=j == t)
                        ins.then_inc(S["o_ready"], 1)

                    def project(n):
                        e, k = divmod(n, KT)
                        m = 64 if e == 0 else P
                        if k == 0 and e >= 2:
                            pe.wait_ge(S["d_ev"], e - 1)
                        ins = split_product(pe, bank[6 + e % 2][0:m, :], SPLIT_IF + e, k, m)
                        if k == KT - 1:
                            ins.then_inc(S["d_ready"], 1)

                    def project_v(t):
                        e = D_V + t
                        if t == 0:
                            w_here(pe, IT_MV)
                        pe.wait_ge(S["d_ev"], e - 1)
                        w = w_ring[:, IT_MV % W_SLOTS, :]
                        for h in range(MH):
                            ins = nc.tensor.matmul(bank[6 + e % 2][:, h * MD:(h + 1) * MD],
                                                   up[:, h, PAD + t * P:PAD + (t + 1) * P],
                                                   w[:, h * MD:(h + 1) * MD], start=True, stop=True)
                        ins.then_inc(S["d_ready"], 1)

                    def gate_columns():
                        pe.wait_ge(S["d_ev"], D_HEAD - 1)
                        for r, (row, ready) in enumerate(((row_a, "rows_a"), (row_e, "rows_e"))):
                            pe.wait_ge(S[ready], 1)
                            for t in range(TILES):
                                c = (r * TILES + t) * MH
                                ins = nc.tensor.transpose(bank[7][:, c:c + MH], row[:, t * P:(t + 1) * P],
                                                          ident[0:MH, 0:MH])
                        ins.then_inc(S["ae_ready"], 1)

                    def turn_heads(f):
                        pe.wait_ge(S["o_ev"], 2 * TILES * (f + 1))
                        if f == 0:
                            pe.wait_ge(S["d_ev"], D_HEAD)
                        elif f == 1:
                            pe.wait_ge(S["ae_ev"], 1)
                        else:
                            pe.wait_ge(S["at_ev"], f - 1)
                        for t in range(TILES):
                            ins = nc.tensor.transpose(bank[6 + f % 2][:, t * P:(t + 1) * P],
                                                      att[:, t, f * P:(f + 1) * P], ident)
                        ins.then_inc(S["at_ready"], 1)

                    for i in range(ITEMS + 2):
                        if i < ITEMS:
                            score(i)
                        for n in range(3 * i, min(3 * i + 3, D_V * KT)):
                            project(n)
                        if V_ITEM <= i < V_ITEM + TILES:
                            project_v(i - V_ITEM)
                        if i == AE_ITEM:
                            gate_columns()
                        if 1 <= i <= ITEMS:
                            turn(i - 1)
                        if i >= 2:
                            values(i - 2)
                        if AE_ITEM < i <= AE_ITEM + 3:
                            turn_heads(i - AE_ITEM - 1)
                    turn_heads(3)

                @block.vector
                def _(ve):
                    def maximum(i):
                        t = i % TILES
                        n = (t + 1) * P
                        s = bank[i % 2]
                        ve.wait_ge(S["sc_ready"], i + 1)
                        nc.vector.tensor_tensor(s[:, t * P:n], s[:, t * P:n], mask_q, ALU.add)
                        ve.drain()
                        nc.vector.tensor_reduce(scol[:, 0, i:i + 1], s[:, 0:n], AX.X, ALU.max)
                        ve.drain()
                        nc.vector.tensor_scalar(scol[:, 1, i:i + 1], scol[:, 0, i:i + 1], -SM_SCALE, None,
                                                ALU.mult).then_inc(S["nm_ready"], 1)

                    def normalise(i):
                        h, t = divmod(i, TILES)
                        ve.wait_ge(S["o_ready"], i + 1)
                        nc.vector.reciprocal(scol[:, 3, i:i + 1], scol[:, 2, i:i + 1])
                        ve.drain()
                        nc.vector.tensor_scalar(att[:, t, h * VDIM:(h + 1) * VDIM], bank[4 + i % 2][:, 0:VDIM],
                                                scol[:, 3, i:i + 1], None, ALU.mult).then_inc(S["o_ev"], 1)

                    def gate_rows():
                        ve.wait_ge(S["lnf"], 1)
                        nc.vector.memset(row_m, 1.0)
                        nc.vector.scalar_tensor_tensor(out=row_f, in0=row_f, scalar=0.0, in1=row_ln,
                                                       op0=ALU.min, op1=ALU.subtract)
                        ve.drain()
                        nc.vector.tensor_tensor_scan(row_cum, row_m, row_f, 0.0, ALU.mult, ALU.add)
                        ve.drain()
                        nc.vector.tensor_tensor(row_a, row_i, row_cum, ALU.subtract).then_inc(S["rows_a"], 1)
                        ve.drain()
                        nc.vector.tensor_tensor_scan(row_m, row_a, row_a, 0.0, ALU.max, ALU.max)
                        ve.drain()
                        nc.vector.tensor_scalar(row_nm, row_m, -1.0, None, ALU.mult)
                        nc.vector.tensor_tensor(row_s, row_cum, row_m, ALU.add)
                        ve.drain().then_inc(S["rows_s"], 1)

                    def conv(h):
                        ve.wait_ge(S["d_ev"], h + 2)
                        ve.wait_ge(S["pads"], 1)
                        c = C_CW + h * CONV
                        nc.vector.tensor_scalar(ca[:, h, :], up[:, h, PAD:UP], cols[:, c + PAD:c + PAD + 1],
                                                cols[:, C_CB + h:C_CB + h + 1], ALU.mult, ALU.add)
                        for j in range(PAD):
                            ve.drain()
                            nc.vector.scalar_tensor_tensor(out=ca[:, h, :], in0=up[:, h, j:j + SEQ],
                                                           scalar=cols[:, c + j:c + j + 1], in1=ca[:, h, :],
                                                           op0=ALU.mult, op1=ALU.add)
                        ve.drain().then_inc(S["conv_ready"], 1)

                    for i in range(ITEMS + 3):
                        if i < ITEMS:
                            maximum(i)
                        if i >= 3:
                            normalise(i - 3)
                        if i == 6:
                            gate_rows()
                        if i in (9, 12, 15, 18):
                            conv(i // 3 - 3)
                        if i == AE_ITEM + 1:
                            ve.wait_ge(S["ae_ready"], 1)
                            nc.vector.tensor_copy(ae[:, :, :, :].rearrange("p r t h -> p (r t h)"),
                                                  bank[7][:, 0:32]).then_inc(S["ae_ev"], 1)

                @block.scalar
                def _(ac):
                    def keep_heads(f):
                        ac.wait_ge(S["at_ready"], f + 1)
                        nc.scalar.copy(attT[:, f, :], bank[6 + f % 2][:, :]).then_inc(S["at_ev"], 1)

                    for i in range(ITEMS + 1):
                        if i < ITEMS:
                            n = (i % TILES + 1) * P
                            ac.wait_ge(S["nm_ready"], i + 1)
                            if i >= 3:
                                ac.wait_ge(S["pt_ready"], i - 2)
                            nc.scalar.activation(prob[:, i % 3, 0:n], bank[i % 2][:, 0:n], ACT.Exp,
                                                 bias=scol[:, 1, i:i + 1], scale=SM_SCALE,
                                                 accum_out=scol[:, 2, i:i + 1])
                            ac.drain().then_inc(S["p_ready"], 1)
                        if i >= 1:
                            n = ((i - 1) % TILES + 1) * P
                            ac.wait_ge(S["pt_ready"], i)
                            if i >= 3:
                                ac.wait_ge(S["o_ready"], i - 2)
                            nc.scalar.copy(probT[:, (i - 1) % 2, 0:n], bank[2 + (i - 1) % 2][:, 0:n]
                                           ).then_inc(S["pt_ev"], 1)
                        for e in [e for e in range(D_V) if (KT * e + KT - 1) // 3 + 1 == i]:
                            ac.wait_ge(S["d_ready"], e + 1)
                            split_high(ac, SPLIT_IF + e + HI_SLOTS)
                            o = bank[6 + e % 2]
                            if e == 0:
                                nc.scalar.activation(row_i, o[0:MH, :], ACT.Identity, bias=cols[0:MH, C_BI:C_BI + 1])
                                nc.scalar.activation(row_f, o[32:32 + MH, :], ACT.Identity,
                                                     bias=cols[0:MH, C_BF:C_BF + 1])
                                ac.drain().then_inc(S["d_ev"], 1)
                            elif e <= MH:
                                nc.scalar.copy(up[:, e - 1, PAD:UP], o[:, :]).then_inc(S["d_ev"], 1)
                            else:
                                nc.scalar.copy(so[:, e - 1 - MH, :], o[:, :]).then_inc(S["d_ev"], 1)
                        if i == 4:
                            nc.scalar.activation(row_t, row_f, ACT.Abs)
                            ac.drain()
                            nc.scalar.activation(row_t, row_t, ACT.Exp, scale=-1.0)
                            ac.drain()
                            nc.scalar.activation(row_ln, row_t, ACT.Ln, bias=1.0).then_inc(S["lnf"], 1)
                        if i == 9:
                            ac.wait_ge(S["rows_s"], 1)
                            nc.scalar.activation(row_e, row_s, ACT.Exp, scale=-1.0).then_inc(S["rows_e"], 1)
                        if i == 21:
                            for h in range(MH):
                                ac.wait_ge(S["conv_ready"], h + 1)
                                nc.scalar.activation(ca[:, h, :], ca[:, h, :], ACT.Silu)
                        if V_ITEM < i <= V_ITEM + TILES:
                            t = i - V_ITEM - 1
                            ac.wait_ge(S["d_ready"], D_V + t + 1)
                            nc.scalar.copy(v1[:, t, :, 0:MD], bank[6 + (D_V + t) % 2][:, :]
                                           .rearrange("p (h e) -> p h e", h=MH)).then_inc(S["d_ev"], 1)
                        if i > AE_ITEM + 1:
                            keep_heads(i - AE_ITEM - 2)
                    for f in range(ITEMS - AE_ITEM - 1, 4):
                        keep_heads(f)

            with nc.Block() as block:
                @block.sync
                def _(sp):
                    load_weights(sp, l, IT_MV + W_SLOTS, IT_MERGE + W_SLOTS)

                @block.gpsimd
                def _(po):
                    for n in range(SPLIT_GA + HI_SLOTS, SPLIT_GM + HI_SLOTS):
                        split_low(po, n)

                def turn_back(pe, h):
                    pe.wait_ge(S["hn_ready"], h + 1)
                    if h >= 1:
                        pe.wait_ge(S["y_ev"], h)
                    for t in range(TILES):
                        ins = nc.tensor.transpose(bank[2][:, t * P:(t + 1) * P], hn[:, h % 2, t * P:(t + 1) * P],
                                                  ident)
                    ins.then_inc(S["hnT_ready"], 1)

                def second_gate(pe, j):
                    if j >= 2:
                        pe.wait_ge(S["e_act"], 2 * (j - 1))
                    else:
                        pe.wait_ge(S["d_ev"], D_N - 1 + j)
                    for k in range(KT):
                        ins = split_product(pe, bank[(D_N + j) % 2][:, :], SPLIT_GM + j, k)
                    ins.then_inc(S["e_ready"], 1)

                @block.tensor
                def _(pe):
                    def free(e):
                        pe.wait_ge(S["d_ev"], e - 1)
                        return bank[e % 2]

                    def queries_keys(h):
                        w = w_mqk
                        for q in range(2):
                            o = free(D_HEAD + h * D_PER + q)
                            nc.tensor.matmul(o[:, :], w[:, (q * MH + h) * MD:(q * MH + h + 1) * MD], ca[:, h, :],
                                             start=True, stop=True).then_inc(S["d_ready"], 1)

                    def merge_gate(h, quarter):
                        for n in range(quarter * D_GA * KT // 4, (quarter + 1) * D_GA * KT // 4):
                            j, k = divmod(n, KT)
                            if k == 0:
                                free(D_HEAD + h * D_PER + 2 + j)
                            o = bank[(D_HEAD + h * D_PER + 2 + j) % 2]
                            ins = split_product(pe, o[:, :], SPLIT_GA + h * D_GA + j, k)
                            if k == KT - 1:
                                ins.then_inc(S["d_ready"], 1)

                    pe.wait_ge(S["mqk_loaded"], 16)
                    queries_keys(0)
                    for h in range(MH):
                        if h >= 1:
                            pe.wait_ge(S["nmb_ev"], h)
                        nc.tensor.matmul(bank[3][:, :], sel[0:MH, h, :], row_nm, start=True,
                                         stop=True).then_inc(S["nmb_ready"], 1)
                        merge_gate(h, 0)
                        pe.wait_ge(S["d_ev"], D_HEAD + h * D_PER + 2)
                        for s in range(TILES):
                            g = h * TILES + s
                            if g >= 2:
                                pe.wait_ge(S["pm_ready"], g - 1)
                            nc.tensor.matmul(bank[4 + g % 2][:, 0:SEQ - s * P], mk[:, h % 2, s * P:(s + 1) * P],
                                             mq[:, h % 2, s * P:SEQ], start=True, stop=True
                                             ).then_inc(S["s_ready"], 1)
                            if s + 1 < TILES:
                                merge_gate(h, s + 1)
                        if h + 1 < MH:
                            queries_keys(h + 1)
                        else:
                            second_gate(pe, 0)
                        for half in range(2):
                            pe.wait_ge(S["pm_ready"], h * TILES + 2 * half + 2)
                            if h >= 1:
                                pe.wait_ge(S["n_ev"], 2 * (h - 1) + half + 1)
                            for t in (2 * half, 2 * half + 1):
                                for s in range(t + 1):
                                    o = P_OFF[s] + (t - s) * P
                                    ins = nc.tensor.matmul(bank[6 + half][:, (t % 2) * 256:(t % 2) * 256 + VW],
                                                           pm[:, h % 2, o:o + P], v1[:, s, h, :], start=s == 0,
                                                           stop=s == t)
                            ins.then_inc(S["n_ready"], 1)
                        if h >= 1:
                            turn_back(pe, h - 1)
                        if h == MH - 1:
                            second_gate(pe, 1)
                    turn_back(pe, MH - 1)

                @block.scalar
                def _(ac):
                    def taken(e):
                        ac.wait_ge(S["d_ready"], e + 1)
                        return bank[e % 2]

                    def queries_keys(h):
                        for q, (dst, scale) in enumerate(((mq, 1.0), (mk, K_SCALE))):
                            o = taken(D_HEAD + h * D_PER + q)
                            nc.scalar.mul(dst[:, h % 2, :], o[:, :], scale).then_inc(S["d_ev"], 1)

                    queries_keys(0)
                    for h in range(MH):
                        ac.wait_ge(S["nmb_ready"], h + 1)
                        nc.scalar.copy(nmb[:, h % 2, :], bank[3][:, :])
                        ac.drain().then_inc(S["nmb_ev"], 1)
                        ac.wait_ge(S["nmd_ready"], h + 1)
                        for s in range(TILES):
                            g = h * TILES + s
                            if g >= 2:
                                ac.wait_ge(S["pm_ready"], g - 1)
                            a_s = ae[:, 0, s, h:h + 1]
                            ins = nc.scalar.activation(dw[:, g % 2, 0:P], nmd[:, h % 2, s * P:(s + 1) * P], ACT.Exp,
                                                       bias=a_s)
                            if s + 1 < TILES:
                                ins = nc.scalar.activation(dw[:, g % 2, P:SEQ - s * P], nmb[:, h % 2, (s + 1) * P:SEQ],
                                                           ACT.Exp, bias=a_s)
                            ac.drain().then_inc(S["dw_ready"], 1)
                        for j in range(D_GA):
                            o = taken(D_HEAD + h * D_PER + 2 + j)
                            split_high(ac, SPLIT_GA + h * D_GA + j + HI_SLOTS)
                            nc.scalar.copy(ga_raw[h * D_GA + j], o[:, :]).then_inc(S["d_ev"], 1)
                        if h + 1 < MH:
                            queries_keys(h + 1)
                        if h == 0:
                            for g in range(MH):
                                nc.scalar.activation(so[:, g, :], so[:, g, :], ACT.Sigmoid)
                            ac.drain().then_inc(S["so_ready"], 1)
                        ac.wait_ge(S["var_ready"], h + 1)
                        nc.scalar.activation(mcol[:, 52:56], mcol[:, 48:52], ACT.Sqrt).then_inc(S["dev_ready"], 1)

                @block.vector
                def _(ve):
                    def weigh(h):
                        ve.wait_ge(S["nmb_ev"], h + 1)
                        nc.vector.tensor_tensor(nmd[:, h % 2, :].rearrange("p (s t) -> p s t", s=TILES),
                                                nmb[:, h % 2, :].rearrange("p (s t) -> p s t", s=TILES),
                                                mask_t.unsqueeze(1).to_broadcast([P, TILES, P]),
                                                ALU.add).then_inc(S["nmd_ready"], 1)
                        for s in range(TILES):
                            g, n = h * TILES + s, SEQ - s * P
                            ve.wait_ge(S["s_ready"], g + 1)
                            ve.wait_ge(S["dw_ready"], g + 1)
                            nc.vector.tensor_tensor(pm[:, h % 2, P_OFF[s]:P_OFF[s] + n], bank[4 + g % 2][:, 0:n],
                                                    dw[:, g % 2, 0:n], ALU.mult).then_inc(S["pm_ready"], 1)

                    def head_norm(h):
                        den, peak, inv = mcol[:, 0:4], mcol[:, 4:8], mcol[:, 8:12]
                        st6 = mcol[:, 12:36].rearrange("p (t c) -> p t c", t=TILES)
                        mv = mcol[:, 36:44].rearrange("p (t c) -> p t c", t=TILES)
                        for half in range(2):
                            ve.wait_ge(S["n_ready"], 2 * h + half + 1)
                            num = bank[6 + half][:, :].rearrange("p (t e) -> p t e", t=2)
                            nc.vector.tensor_copy(den[:, 2 * half:2 * half + 2], num[:, :, MD])
                        ve.drain()
                        nc.vector.scalar_tensor_tensor(out=peak, in0=den, scalar=-1.0, in1=den, op0=ALU.mult,
                                                       op1=ALU.max)
                        ve.drain()
                        nc.vector.tensor_tensor(peak, peak, ae[:, 1, :, h], ALU.max)
                        ve.drain()
                        nc.vector.reciprocal(inv, peak)
                        ve.drain()
                        hd = hn[:, h % 2, :].rearrange("p (t e) -> p t e", t=TILES)
                        for t in range(TILES):
                            ins = nc.vector.tensor_scalar(hd[:, t, :], bank[6 + t // 2][:, (t % 2) * 256:(t % 2) * 256 + MD],
                                                          inv[:, t:t + 1], None, ALU.mult)
                            if t % 2:
                                ins.then_inc(S["n_ev"], 1)
                        ve.drain()
                        for t in range(TILES):
                            nc.vector.bn_stats(st6[:, t, :], hd[:, t, :])
                        ve.drain()
                        for t in range(TILES):
                            nc.vector.bn_aggr(mv[:, t, :], st6[:, t, :])
                        ve.drain()
                        nc.vector.tensor_scalar(mcol[:, 48:52], mv[:, :, 1], EPS, None,
                                                ALU.add).then_inc(S["var_ready"], 1)
                        ve.wait_ge(S["dev_ready"], h + 1)
                        nc.vector.reciprocal(mcol[:, 56:60], mcol[:, 52:56])
                        ve.drain()
                        for t in range(TILES):
                            nc.vector.tensor_scalar(hd[:, t, :], hd[:, t, :], mv[:, t, 0:1], mcol[:, 56 + t:57 + t],
                                                    ALU.subtract, ALU.mult)
                        ve.drain().then_inc(S["hn_ready"], 1)

                    def gated(h):
                        nc.vector.tensor_scalar(ctmp, ca[:, h, :], cols[:, C_SK + h:C_SK + h + 1], None, ALU.mult)
                        ve.drain()
                        ve.wait_ge(S["hnT_ready"], h + 1)
                        nc.vector.scalar_tensor_tensor(out=ctmp, in0=bank[2][:, :], scalar=cols[:, C_MG + h:C_MG + h + 1],
                                                       in1=ctmp, op0=ALU.mult, op1=ALU.add).then_inc(S["y_ev"], 1)
                        ve.drain()
                        if h == 0:
                            ve.wait_ge(S["so_ready"], 1)
                        nc.vector.tensor_tensor(ymT[:, h, :], ctmp, so[:, h, :], ALU.mult)
                        ve.drain()

                    for h in range(MH):
                        weigh(h)
                        head_norm(h)
                        if h >= 1:
                            gated(h - 1)
                    gated(MH - 1)

            def wait_alone(eng, s, value):
                eng.wait_ge(s, value)
                eng.sem_inc(S["passed"], 1)

            HEAD_PAIRS = PH // 2
            QP_SLOTS = 2
            SB = TILES * PH // 2
            SCORE_ORDER = [t * HEAD_PAIRS + hp for half in range(2) for t in range(TILES)
                           for hp in (2 * half, 2 * half + 1)]
            with nc.Block() as block:
                @block.sync
                def _(sp):
                    after = (l + 1) % DEPTH
                    load_ada(sp, ada_late, l, ADA_LATE)
                    load_ada(sp, ada_late, after, ADA_LATE + 1)
                    load_ada_bias(sp, after, 0, 2)
                    load_gain(sp, ada_late[2], after, 0)
                    for n in range(2 * KT):
                        load_weights(sp, l, IT_MERGE + W_SLOTS + n, IT_MERGE + W_SLOTS + n + 1)
                        if n in LOAD_AFTER:
                            load_ada(sp, ada_late, after, ADA_LATE + ADA_SLOTS + LOAD_AFTER.index(n))
                    load_weights(sp, l, IT_MERGE + W_SLOTS + 2 * KT, IT_PQ + W_SLOTS)
                    load_weights(sp, l, IT_PQ + W_SLOTS, N_ITEMS)

                @block.gpsimd
                def _(po):
                    for n in range(SPLIT_GM + HI_SLOTS, len(SPLIT)):
                        split_low(po, n)
                    with po.Fori(0, TILES) as t:
                        with po.Fori(0, HEAD_PAIRS) as i:
                            for par in range(2):
                                n = t * PH + i * 2 + par
                                for s in range(TOPK):
                                    if s == 0:
                                        wait_alone(po, S["idx_ready"], n + 1)
                                    wait_alone(po, S["slot_free"], n * TOPK + (s + 1))
                                    po.indirect_dma_start(ring[:, s % RING, :], None, experts_in,
                                                          bass.IndirectOffsetOnAxis(ap=idx[:, par, s:s + 1], axis=0)
                                                          ).then_inc(gathered[s % RING], 16)

                @block.scalar
                def _(ac):
                    def keep_scores(half):
                        for m in range(half * SB // 2, (half + 1) * SB // 2, 2):
                            i = SCORE_ORDER[m]
                            ac.wait_ge(S["s2_ready"], m + 1)
                            nc.scalar.copy(scores[:, i * 512:(i + 1) * 512], bank[m % 4][:, :]).then_inc(S["s2_act"], 1)

                    def stage_scores(n, par):
                        nc.scalar.copy(stage[:, par, :, :].rearrange("p q n -> p (q n)"),
                                       scores[:, bass.ds(n * (2 * NKEYS), 2 * NKEYS)]).then_inc(S["stage_ready"], 1)

                    def exponentials(n):
                        ac.wait_ge(S["best_ready"], n + 1)
                        nc.scalar.activation(gexp, best, ACT.Exp, bias=gs[:, 0:1], accum_out=gs[:, 1:2])
                        ac.drain().then_inc(S["exp_ready"], 1)

                    def round_merged(j):
                        ac.wait_ge(S["e_dve"], j + 1)
                        nc.scalar.copy(mg_high[:, j, :], mt[:, j % 2, 0, :]).then_inc(S["mg_high_ready"], 1)

                    for j in range(KT):
                        if j >= 2:
                            ac.wait_ge(S["e_dve"], j - 1)
                        nc.scalar.activation(sg[:, j % 2, 0, :], ga_raw[j], ACT.Sigmoid).then_inc(S["e_act"], 1)
                        ac.wait_ge(S["e_ready"], GATE_AT[j] + 1)
                        if j + HI_SLOTS < KT:
                            split_high(ac, SPLIT_GM + j + HI_SLOTS)
                        nc.scalar.activation(sg[:, j % 2, 1, :], bank[(D_N + j) % 2][:, :], ACT.Sigmoid
                                             ).then_inc(S["e_act"], 1)
                        if j >= 1:
                            round_merged(j - 1)
                    split_high(ac, SPLIT_OUT)
                    round_merged(KT - 1)
                    for k in range(1, KT):
                        split_high(ac, SPLIT_OUT + k)
                    norm_act_sums(ac, 1, at(16, D))
                    norm_act_copies(ac, 1)
                    for h in range(PH):
                        if h == PH // 2:
                            keep_scores(0)
                            ac.drain()
                            stage_scores(0, 0)
                            stage_scores(1, 1)
                        if h == PH - 2:
                            exponentials(0)
                        ac.wait_ge(S["q_ready"], h + 1)
                        nc.scalar.copy(qp[:, h, :], bank[4 + h % 2][:, :]).then_inc(S["q_ev"], 1)
                    keep_scores(1)
                    ac.drain()
                    ac.wait_ge(S["s2_dve"], SB // 2)
                    with ac.Fori(0, TILES) as t:
                        nc.scalar.copy(h_now, h_tok[:, bass.ds(t, 1), :].rearrange("p a d -> p (a d)")
                                       ).then_inc(S["h_now_ready"], 1)
                        with ac.Fori(0, HEAD_PAIRS) as i:
                            for par in range(2):
                                n = t * PH + i * 2 + par
                                stage_scores((n + 2) % UNITS, par)
                                for g in range(TOPK // GROUP):
                                    if g == 2:
                                        exponentials(n + 1)
                                    ac.wait_ge(S["dots_ready"], n * (TOPK // GROUP) + (g + 1))
                                    c = slice(g * GROUP, (g + 1) * GROUP)
                                    nc.scalar.activation(gel[:, par, c], dots[:, par, c],
                                                         ACT.Gelu).then_inc(S["gelu_ready"], 1)

                @block.vector
                def _(ve):
                    def top8(vals, poss, src, scratch):
                        nc.vector.max(vals, src)
                        ve.drain()
                        nc.vector.max_index(poss, vals, src)
                        if scratch is not None:
                            nc.vector.match_replace(scratch, vals, src, FLOOR)
                        ve.drain()

                    def route(part, n, par):
                        if part < 4:
                            q, half = divmod(part, 2)
                            if part == 0:
                                wait_alone(ve, S["stage_ready"], n + 1)
                            c = slice(8 * half, 8 * half + 8)
                            top8(top[:, q, c], top_i[:, q, c], rest if half else stage[:, par, q, :],
                                 None if half else rest)
                        elif part == 4:
                            a = top[:, 0, :].unsqueeze(2).to_broadcast([P, TOPK, TOPK])
                            b = top[:, 1, :].unsqueeze(1).to_broadcast([P, TOPK, TOPK])
                            nc.vector.tensor_tensor(cand[:, 0, :].rearrange("p (a b) -> p a b", a=TOPK), a, b, ALU.add)
                            nc.vector.tensor_copy(top_f[:, :, :], top_i[:, :, :])
                            ve.drain()
                            top8(best[:, 0:8], pos[:, 0:8], cand[:, 0, :], cand[:, 1, :])
                        elif part == 5:
                            top8(best[:, 8:16], pos[:, 8:16], cand[:, 1, :], None)
                            nc.vector.tensor_scalar(gs[:, 0:1], best[:, 0:1], -1.0, None, ALU.mult)
                            ve.drain().then_inc(S["best_ready"], 1)
                        elif part == 6:
                            nc.vector.tensor_scalar(posab[:, 0, :], pos, 4, None, ALU.logical_shift_right)
                            nc.vector.tensor_scalar(posab[:, 1, :], pos, 15, None, ALU.bitwise_and)
                            ve.drain()
                            nc.vector.tensor_copy(posab_f[:, :, :], posab[:, :, :])
                            ve.drain()
                            hot3 = hot.rearrange("p (k j) -> p k j", j=TOPK)
                            nc.vector.tensor_tensor(hot3, posab_f[:, :, :].rearrange("p q k -> p (q k)").unsqueeze(2)
                                                    .to_broadcast([P, 2 * TOPK, TOPK]),
                                                    iota.unsqueeze(1).to_broadcast([P, 2 * TOPK, TOPK]), ALU.is_equal)
                            ve.drain()
                            hot4 = hot.rearrange("p (q k j) -> p q k j", q=2, k=TOPK)
                            nc.vector.tensor_tensor(hot4, hot4, top_f[:, :, :].unsqueeze(2)
                                                    .to_broadcast([P, 2, TOPK, TOPK]), ALU.mult)
                            ve.drain()
                        else:
                            nc.vector.tensor_reduce(pick, hot.rearrange("p (k j) -> p k j", j=TOPK), AX.X, ALU.add)
                            ve.drain()
                            nc.vector.scalar_tensor_tensor(out=flat_i, in0=pick[:, 0:TOPK], scalar=float(NKEYS),
                                                           in1=pick[:, TOPK:2 * TOPK], op0=ALU.mult, op1=ALU.add)
                            ve.drain()
                            nc.vector.tensor_scalar(idx[:, par, :], flat_i, layer_row[:, 0:1], None, ALU.add)
                            ve.drain().then_inc(S["idx_ready"], 1)
                            ve.wait_ge(S["exp_ready"], n + 1)
                            nc.vector.reciprocal(gs[:, 2:3], gs[:, 1:2])
                            ve.drain()
                            nc.vector.tensor_scalar(gate[:, par, :], gexp, gs[:, 2:3], None, ALU.mult)
                            ve.drain()

                    def keep_scores(half):
                        for m in range(half * SB // 2 + 1, (half + 1) * SB // 2, 2):
                            i = SCORE_ORDER[m]
                            ve.wait_ge(S["s2_ready"], m + 1)
                            nc.vector.tensor_copy(scores[:, i * 512:(i + 1) * 512], bank[m % 4][:, :]
                                                  ).then_inc(S["s2_dve"], 1)

                    def merged_rest(j):
                        ve.wait_ge(S["mg_high_ready"], j + 1)
                        nc.vector.tensor_tensor(mg_low[j], mt[:, j % 2, 0, :], mg_high[:, j, :],
                                                ALU.subtract).then_inc(S["mg_low_ready"], 1)

                    def scale_out(k):
                        w = w_here(ve, IT_OUT + k)
                        nc.vector.tensor_tensor(w, w, ada[:, 2 * D:3 * D], ALU.mult).then_inc(S["scaled"], 1)

                    for j in range(KT):
                        for i in ADA_IN_MERGE[j] or [ADA_STEPS - ADA_LATE] * (j == KT - 2):
                            ada_step_dve(ve, ada_late, ADA_LATE + i, ADA_LATE, ADA_STEPS)
                        ve.wait_ge(S["e_ready"], BRANCH_AT[j] + 1)
                        ve.wait_ge(S["e_act"], 2 * j + 2)
                        ve.drain()
                        for g in range(2):
                            nc.vector.tensor_tensor(mt[:, j % 2, g, :], bank[2 + 2 * (j % 2) + g][:, :], sg[:, j % 2, g, :],
                                                    ALU.mult)
                        ve.drain()
                        m = mt[:, j % 2, 0, :]
                        nc.vector.tensor_tensor(m, m, mt[:, j % 2, 1, :], ALU.add).then_inc(S["e_dve"], 1)
                        if j >= 1:
                            merged_rest(j - 1)
                        if j >= KT - 2:
                            scale_out(j - (KT - 2))
                    merged_rest(KT - 1)
                    for k in range(2, KT):
                        scale_out(k)
                    for t in range(TILES):
                        for c in range(2):
                            b = 2 * t + c
                            ve.wait_ge(S["wo_ready"], b + 1)
                            xs = x[:, t, c * 512:(c + 1) * 512]
                            nc.vector.tensor_tensor(xs, xs, bank[b][:, :], ALU.add)
                        ve.drain().then_inc(S["x_ready"], 1)
                    norm_dve(ve, 1, ada[:, 3 * D:4 * D], ada[:, 4 * D:5 * D])
                    keep_scores(0)
                    for part in range(ROUTE_PARTS):
                        route(part, 0, 0)
                    for part in range(ROUTE_PARTS // 2):
                        route(part, 1, 1)
                    keep_scores(1)
                    ve.sem_inc(S["y_free"], 1)
                    with ve.Fori(0, TILES) as t:
                        wait_alone(ve, S["h_now_ready"], t + 1)
                        with ve.Fori(0, HEAD_PAIRS) as i:
                            for par in range(2):
                                n = t * PH + i * 2 + par
                                for g in range(TOPK // GROUP):
                                    for s in range(g * GROUP, (g + 1) * GROUP):
                                        ve.wait_ge(gathered[s % RING],
                                                l * (UNITS * 32) + n * 32 + 16 * (s // RING + 1))
                                        u = ring[:, s % RING, 0:D]
                                        nc.vector.tensor_tensor_reduce(u, u, h_now, 1.0, 0.0, ALU.mult, ALU.add,
                                                                       dots[:, par, s:s + 1])
                                    ve.drain().then_inc(S["dots_ready"], 1)
                                    if g < ROUTE_PARTS // 2:
                                        route(g + ROUTE_PARTS // 2, n + 1, 1 - par)
                                    else:
                                        route(g - ROUTE_PARTS // 2, n + 2, par)
                                    ve.wait_ge(S["gelu_ready"], n * (TOPK // GROUP) + (g + 1))
                                    for s in range(g * GROUP, (g + 1) * GROUP):
                                        ve.wait_ge(S["slot_free"], n * TOPK + (s + 1))
                                        nc.vector.tensor_scalar(diag[:, s % 8, :], ident, gel[:, par, s:s + 1],
                                                                gate[:, par, s:s + 1], ALU.mult,
                                                                ALU.mult).then_inc(S["diag_ready"], 1)
                        ve.wait_ge(S["y_done"], t + 1)
                        for c in range(2):
                            nc.vector.tensor_tensor(ytmp[:, c * 512:(c + 1) * 512], bank[c][:, :],
                                                    ada[:, 5 * D + c * 512:5 * D + (c + 1) * 512], ALU.mult)
                        ve.drain().then_inc(S["y_free"], 1)
                        xt = x[:, bass.ds(t, 1), :].rearrange("p a d -> p (a d)")
                        nc.vector.tensor_tensor(xt, xt, ytmp, ALU.add)
                        ve.drain()
                    nc.vector.tensor_scalar(layer_row[:, :], layer_row[:, :], float(EXPERTS), None, ALU.add)

                @block.tensor
                def _(pe):
                    for j in range(KT):
                        w = w_here(pe, IT_MERGE + BRANCH_AT[j])
                        if j >= 2:
                            pe.wait_ge(S["e_dve"], j - 1)
                        for g, branch in enumerate((attT, ymT)):
                            for k in range(4):
                                ins = nc.tensor.matmul(bank[2 + 2 * (j % 2) + g][:, :],
                                                       w[:, (4 * g + k) * P:(4 * g + k + 1) * P],
                                                       branch[:, k, :], start=k == 0, stop=k == 3)
                        ins.then_inc(S["e_ready"], 1)
                        steps = ADA_IN_MERGE[j]
                        for i in steps[:-1]:
                            ada_pe(pe, ada_late, ADA_LATE + i)
                        if j + 2 < KT:
                            second_gate(pe, j + 2)
                        for i in steps[-1:]:
                            ada_pe(pe, ada_late, ADA_LATE + i)
                    pe.wait_ge(S["e_act"], 2 * KT)
                    pe.wait_ge(S["e_dve"], KT)
                    pe.wait_ge(S["ada_ev"], ADA_STEPS)
                    for k in range(KT):
                        pe.wait_ge(S["low_ready"], SPLIT_OUT + k + 1)
                        pe.wait_ge(S["mg_low_ready"], k + 1)
                        high, low = w_high[:, (SPLIT_OUT + k) % HI_SLOTS, :], w_low[:, (IT_OUT + k) % W_SLOTS, :]
                        for t in range(TILES):
                            m_high, m_low = (m[:, t * P:(t + 1) * P] for m in (mg_high[:, k, :], mg_low[k]))
                            for c in range(2):
                                o, cc = bank[2 * t + c][:, :], slice(c * 512, (c + 1) * 512)
                                nc.tensor.matmul(o, m_high, high[:, cc], start=k == 0, stop=False)
                                nc.tensor.matmul(o, m_high, low[:, cc], start=False, stop=False)
                                ins = nc.tensor.matmul(o, m_low, high[:, cc], start=False, stop=k == KT - 1)
                                if k == KT - 1:
                                    ins.then_inc(S["wo_ready"], 1)
                        if k < KT - 1:
                            ins.then_inc(S["out_used"], 1)
                    norm_pe(pe, 1)
                    pe.wait_ge(S["tp_ev"], 4 * TILES)
                    for half in range(2):
                        for h in range(half * PH // 2, (half + 1) * PH // 2):
                            w = w_here(pe, IT_PQ + h + half)
                            if h >= 2:
                                pe.wait_ge(S["q_ev"], h - 1)
                            for k in range(KT):
                                ins = nc.tensor.matmul(bank[4 + h % 2][:, :], w[:, k * P:(k + 1) * P], hT[:, k, :],
                                                       start=k == 0, stop=k == KT - 1)
                            ins.then_inc(S["q_ready"], 1)
                        pe.wait_ge(S["q_ev"], (half + 1) * PH // 2)
                        w = w_here(pe, IT_PQ + (half + 1) * PH // 2 + half)
                        for m in range(half * SB // 2, (half + 1) * SB // 2):
                            t, hp = divmod(SCORE_ORDER[m], HEAD_PAIRS)
                            if m >= 4:
                                pe.wait_ge(S["s2_act" if m % 2 == 0 else "s2_dve"], (m - 4) // 2 + 1)
                            for q in range(2):
                                h = 2 * hp + q
                                ins = nc.tensor.matmul(bank[m % 4][:, q * 256:(q + 1) * 256],
                                                       qp[:, h, t * P:(t + 1) * P],
                                                       w[:, (h % 4) * 256:(h % 4 + 1) * 256], start=True, stop=True)
                            ins.then_inc(S["s2_ready"], 1)
                        if half == 0:
                            pe.sem_inc(S["slot_free"], RING - QP_SLOTS)
                    pe.drain().then_inc(S["slot_free"], QP_SLOTS)
                    pe.wait_ge(S["s2_act"], SB // 2)
                    pe.wait_ge(S["s2_dve"], SB // 2)
                    with pe.Fori(0, TILES) as t:
                        pe.wait_ge(S["y_free"], t + 1)
                        for c in range(2):
                            nc.tensor.matmul(bank[c][:, :], zeros[:, :], const[:, 0:512], start=True, stop=False)
                        with pe.Fori(0, HEAD_PAIRS) as i:
                            for par in range(2):
                                n = t * PH + i * 2 + par
                                for s in range(TOPK):
                                    pe.wait_ge(S["diag_ready"], n * TOPK + (s + 1))
                                    for c in range(2):
                                        ins = nc.tensor.matmul(bank[c][:, :], diag[:, s % 8, :],
                                                               ring[:, s % RING, D + c * 512:D + (c + 1) * 512],
                                                               start=False, stop=False)
                                    ins.then_inc(S["slot_free"], 1)
                        for c in range(2):
                            ins = nc.tensor.matmul(bank[c][:, :], zeros[:, :], const[:, 0:512], start=False, stop=True)
                        ins.then_inc(S["y_done"], 1)

            clear_semaphores()

        fg = at(0, D)
        with nc.Block() as block:
            @block.sync
            def _(sp):
                sp.dma_start(fg, fg_in.to_broadcast([P, D])).then_inc(once_dma, 16)
                for t in range(TILES):
                    sp.wait_ge(S["h_ready"], t + 1)
                    sp.dma_start(out[t * P:(t + 1) * P, :], h_tok[:, t, :]).then_inc(stored, 16)
                sp.wait_ge(stored, 16 * TILES)

            @block.scalar
            def _(ac):
                norm_act_sums(ac, 0, at(8, D))

            @block.vector
            def _(ve):
                norm_dve_sums(ve)
                ve.wait_ge(S["ss_ready"], 1)
                nc.vector.tensor_scalar(small[:, 4:8], small[:, 0:4], 1.0 / D, EPS, ALU.mult,
                                        ALU.add).then_inc(S["ms_ready"], 1)
                ve.wait_ge(S["sd_ready"], 1)
                nc.vector.reciprocal(small[:, 12:16], small[:, 8:12])
                ve.wait_ge(once_dma, 48)
                ve.drain()
                for t in range(TILES):
                    nc.vector.scalar_tensor_tensor(out=h_tok[:, t, :], in0=x[:, t, :], scalar=small[:, 12 + t:13 + t],
                                                   in1=fg, op0=ALU.mult, op1=ALU.mult
                                                   ).then_inc(S["h_ready"], 1)


def _feature_tiles(w):
    return w.reshape(w.shape[0] // P, P, w.shape[1]).transpose(1, 0, 2)


def _item(parts):
    flat = parts.reshape(P, -1)
    out = np.zeros((P, D), np.float32)
    out[:, :flat.shape[1]] = flat
    return out


def _weights(a, l):
    w = a["w_in"][l]
    edge = np.cumsum([0, Q_LORA, KV_LORA, ROPE, MI, MI, MH, MH, D, D])
    q, kv, kr, u, o, i, f, ga, gm = (w[:, edge[n]:edge[n + 1]] for n in range(9))
    swap = np.r_[ROPE // 2:ROPE, 0:ROPE // 2]
    items = [_item(_feature_tiles(kv[:, j * P:(j + 1) * P])) for j in range(KVT)]
    items += [_item(_feature_tiles(q[:, j * P:(j + 1) * P])) for j in range(QT)]
    none = np.zeros((D, NOPE), np.float32)
    items.append(_item(_feature_tiles(np.concatenate([none, kr, kr[:, swap]], 1))))
    up = a["w_kv_up"][l].reshape(KV_LORA, HEADS, NOPE + VDIM)
    items.append(_item(_feature_tiles(up[:, :, :NOPE].reshape(KV_LORA, -1))))
    items.append(_item(_feature_tiles(up[:, :, NOPE:].reshape(KV_LORA, -1))))
    qu = a["w_q_up"][l].reshape(Q_LORA, HEADS, QK)
    for h in range(HEADS):
        r = qu[:, h, NOPE:]
        items.append(_item(_feature_tiles(np.concatenate([qu[:, h, :NOPE], r, r[:, swap]], 1))))
    gates = np.zeros((D, P), np.float32)
    gates[:, 0:MH] = i
    gates[:, 32:32 + MH] = f
    items.append(_item(_feature_tiles(gates)))
    for m in (u, o):
        items += [_item(_feature_tiles(m[:, j * P:(j + 1) * P])) for j in range(MH)]
    items.append(_item(a["wv_m"][l].transpose(1, 0, 2)))
    items += [_item(_feature_tiles(ga[:, j * P:(j + 1) * P])) for j in range(KT)]
    merge = [None] * (2 * KT)
    for j in range(KT):
        c = slice(j * P, (j + 1) * P)
        merge[GATE_AT[j]] = _item(_feature_tiles(gm[:, c]))
        merge[BRANCH_AT[j]] = _item(np.concatenate([_feature_tiles(a["w_branch_a"][l][:, c]),
                                                    _feature_tiles(a["w_branch_m"][l][:, c])], 1))
    items += merge
    items += [_item(a["w_out"][l][k * P:(k + 1) * P]) for k in range(KT)]
    queries = [_item(_feature_tiles(a["peer_wq"][l][:, h * P:(h + 1) * P])) for h in range(PH)]
    keys = np.zeros((P, PH, 2, NKEYS), np.float32)
    for q2 in range(2):
        keys[q2 * HALF:(q2 + 1) * HALF, :, q2, :] = a["peer_keys"][l][:, q2].transpose(2, 0, 1)
    keys = keys.reshape(P, PH, 2 * NKEYS)
    for half in (slice(0, PH // 2), slice(PH // 2, PH)):
        items += [*queries[half], _item(keys[:, half])]
    items.append(_item(np.concatenate([a["wq_m"][l].transpose(1, 0, 2).reshape(P, -1),
                                       a["wk_m"][l].transpose(1, 0, 2).reshape(P, -1)], 1)))
    return np.stack(items)


def _columns(a, l):
    c = np.zeros((P, N_COLS), np.float32)
    c[:, C_QG:C_QG + QT] = a["q_norm_g"][l].reshape(QT, P).T
    c[:, C_KVG:C_KVG + KVT] = a["kv_norm_g"][l].reshape(KVT, P).T
    c[:, C_CW:C_CW + MH * CONV] = a["conv_w"][l].reshape(CONV, MH, P).transpose(2, 1, 0).reshape(P, -1)
    c[:, C_CB:C_CB + MH] = a["conv_b"][l].reshape(MH, P).T
    c[:, C_MG:C_MG + MH] = a["mh_norm_g"][l].reshape(MH, P).T
    c[:, C_SK:C_SK + MH] = a["m_skip"][l].reshape(MH, P).T
    c[0:MH, C_BI] = a["b_i"][l]
    c[0:MH, C_BF] = a["b_f"][l]
    return c


def _constants():
    c = np.zeros((P, N_CONST), np.float32)
    c[:, K_ID:K_ID + P] = np.eye(P)
    above = np.triu(np.full((P, P), NEG, np.float32), 1)
    c[:, K_MQ:K_MQ + P] = above
    c[:, K_MT:K_MT + P] = above.T
    for h in range(MH):
        c[h, K_SEL + h * P:K_SEL + (h + 1) * P] = 1.0
    c[:, K_IOTA:K_IOTA + TOPK] = np.arange(TOPK)
    freq = np.float32(THETA) ** (-np.arange(0, ROPE, 2, dtype=np.float32) / np.float32(ROPE))
    c[64:128, K_FREQ] = np.tile(freq, 4)
    c[96:112, K_SIGN] = -1.0
    c[112:128, K_SIGN] = 1.0
    c[:, K_HPI] = np.pi / 2
    return c


def kernel(**inputs):
    import concourse.bacc as bacc
    from concourse.bass_utils import run_bass_kernel_spmd

    a = {k: np.asarray(v) for k, v in inputs.items()}
    wada = a["w_ada"].reshape(DEPTH, KT, P, ADA_STEPS, ADA_W).transpose(0, 3, 2, 1, 4)
    arrays = {
        "x": a["x"][0],
        "c_cols": a["c"][0].reshape(KT, P).T,
        "positions": a["positions"],
        "w_ada": wada.reshape(DEPTH, ADA_STEPS, P, KT * ADA_W),
        "b_ada": a["b_ada"],
        "norm_g": np.stack([a["norm1_g"], a["norm2_g"]], 1),
        "weights": np.stack([_weights(a, l) for l in range(DEPTH)]),
        "columns": np.stack([_columns(a, l) for l in range(DEPTH)]),
        "constants": _constants(),
        "final_g": a["final_g"][None, :],
        "experts": np.concatenate([a["peer_u"], a["peer_v"]], -1).reshape(DEPTH * EXPERTS, ROW),
    }
    arrays = {k: np.ascontiguousarray(v) for k, v in arrays.items()}
    nc = bacc.Bacc("TRN2", target_bir_lowering=False, num_devices=1)
    args = [nc.dram_tensor("in_" + k, v.shape, mybir.dt.from_np(v.dtype), kind="ExternalInput").ap()
            for k, v in arrays.items()]
    out = nc.dram_tensor("out_0", (SEQ, D), F32, kind="ExternalOutput").ap()
    build_trunk(nc, *args, out)
    r = run_bass_kernel_spmd(nc, [{"in_" + k: v for k, v in arrays.items()}], core_ids=[0])
    return r.results[0]["out_0"].reshape(1, SEQ, D)
```
